# Optimizing a Trainium2 kernel written in Bass

```python
import math
import jax, jax.numpy as jnp
from jax import lax
import numpy as np
import jax
import jax.numpy as jnp

D_MODEL = 1024
BATCH = 1
SEQ = 256
DEPTH = 4

N_MIXERS = 3
EPS = 1e-6
D_FF = 2816
CONV_WIDTH = 3
MLA_HEADS = 16
Q_LORA = 256
KV_LORA = 128
QK_NOPE = 64
QK_ROPE = 32
QK_HEAD = QK_NOPE + QK_ROPE
V_HEAD = 64
ROPE_THETA = 10000.0
Q_BLOCK = 128
SG_WIDTH = D_MODEL
SG_GROUPS = 8
SG_CHUNK = 128
N_A = (DEPTH + 2) // 3
N_B = (DEPTH + 1) // 3
N_C = DEPTH // 3


def rms_norm(x, g):
    xf = x.astype(jnp.float32)
    y = xf * lax.rsqrt(jnp.mean(xf * xf, axis=-1, keepdims=True) + EPS)
    return y.astype(x.dtype) * g

def swiglu(x, w_gate, w_up, w_down):
    return (jax.nn.silu(x @ w_gate) * (x @ w_up)) @ w_down

def rope(t, cos, sin):
    t1, t2 = jnp.split(t, 2, axis=-1)
    return jnp.concatenate([t1 * cos - t2 * sin, t2 * cos + t1 * sin], axis=-1)

def short_conv_mixer(x, w_in, conv_k, w_out):
    d = x.shape[-1]
    proj = x @ w_in
    b_gate, c_gate, h = proj[..., :d], proj[..., d:2 * d], proj[..., 2 * d:]
    z = c_gate * h
    conv = lax.conv_general_dilated(
        z, conv_k[:, None, :].astype(z.dtype), window_strides=(1,),
        padding=[(CONV_WIDTH - 1, 0)], dimension_numbers=("NWC", "WIO", "NWC"),
        feature_group_count=d)
    return (b_gate * conv) @ w_out

def mla_mixer(x, cos, sin, w_a, q_norm, w_uq, kv_norm, w_ukv, q_gain, k_gain, w_o):
    bsz, s, _ = x.shape
    a = x @ w_a
    c_q = a[..., :Q_LORA]
    c_kv = a[..., Q_LORA:Q_LORA + KV_LORA]
    k_pe = a[..., Q_LORA + KV_LORA:]
    q = (rms_norm(c_q, q_norm) @ w_uq).reshape(bsz, s, MLA_HEADS, QK_HEAD)
    kv = (rms_norm(c_kv, kv_norm) @ w_ukv).reshape(bsz, s, MLA_HEADS, QK_NOPE + V_HEAD)
    k_nope, v = kv[..., :QK_NOPE], kv[..., QK_NOPE:]
    k = jnp.concatenate(
        [k_nope, jnp.broadcast_to(k_pe[:, :, None, :], (bsz, s, MLA_HEADS, QK_ROPE))], axis=-1)
    q = rms_norm(q, q_gain)
    k = rms_norm(k, k_gain)
    cos_h, sin_h = cos[:, :, None, :], sin[:, :, None, :]
    q = jnp.concatenate([q[..., :QK_NOPE], rope(q[..., QK_NOPE:], cos_h, sin_h)], axis=-1)
    k = jnp.concatenate([k[..., :QK_NOPE], rope(k[..., QK_NOPE:], cos_h, sin_h)], axis=-1)
    q = q.transpose(0, 2, 1, 3)
    k = k.transpose(0, 2, 1, 3)
    v = v.transpose(0, 2, 1, 3)
    scale = QK_HEAD ** -0.5
    outs = []
    for blk in range(s // Q_BLOCK):
        q0, end = blk * Q_BLOCK, (blk + 1) * Q_BLOCK
        qb = q[:, :, q0:end]
        kb, vb = k[:, :, :end], v[:, :, :end]
        sc = jnp.einsum("bhqd,bhkd->bhqk", qb, kb).astype(jnp.float32) * scale
        mask = jnp.arange(end)[None, :] <= jnp.arange(q0, end)[:, None]
        sc = jnp.where(mask[None, None], sc, -jnp.inf)
        p = jax.nn.softmax(sc, axis=-1).astype(vb.dtype)
        outs.append(jnp.einsum("bhqk,bhkd->bhqd", p, vb))
    o = jnp.concatenate(outs, axis=2)
    o = o.transpose(0, 2, 1, 3).reshape(bsz, s, MLA_HEADS * V_HEAD)
    return o @ w_o

def spatial_gating_mixer(x, w_in, v_norm, w_s, b_s, w_out):
    bsz, s, _ = x.shape
    z = jax.nn.gelu(x @ w_in)
    u, v = z[..., :SG_WIDTH], z[..., SG_WIDTH:]
    v = rms_norm(v, v_norm)
    cg = SG_WIDTH // SG_GROUPS
    v = v.reshape(bsz, s // SG_CHUNK, SG_CHUNK, SG_GROUPS, cg)
    causal = jnp.tril(jnp.ones((SG_CHUNK, SG_CHUNK), dtype=bool))
    w_masked = jnp.where(causal[None], w_s, jnp.zeros((), w_s.dtype))
    mixed = jnp.einsum("gts,bcsgk->bctgk", w_masked, v) + b_s.T[None, None, :, :, None]
    return (u * mixed.reshape(bsz, s, SG_WIDTH)) @ w_out

def first_inputs(seed: int = 0) -> dict:
    key = jax.random.key(seed)
    ks = jax.random.split(key, 24)

    def nrm(k, shape, fan_in):
        return jax.random.normal(k, shape, jnp.float32) * fan_in ** -0.5

    def gain(k, shape):
        return 1.0 + 0.05 * jax.random.normal(k, shape, jnp.float32)

    x = jax.random.normal(ks[0], (BATCH, SEQ, D_MODEL), jnp.float32)
    start = jax.random.randint(ks[1], (BATCH,), 0, 4096, dtype=jnp.int32)
    positions = (start[:, None] + jnp.arange(SEQ, dtype=jnp.int32)[None, :]).astype(jnp.int32)
    return {
        "x": x,
        "positions": positions,
        "norm_g": gain(ks[2], (DEPTH, 3, D_MODEL)),
        "ffn_gate": nrm(ks[3], (DEPTH, 2, D_MODEL, D_FF), D_MODEL),
        "ffn_up": nrm(ks[4], (DEPTH, 2, D_MODEL, D_FF), D_MODEL),
        "ffn_down": nrm(ks[5], (DEPTH, 2, D_FF, D_MODEL), D_FF),
        "conv_w_in": nrm(ks[6], (N_A, D_MODEL, 3 * D_MODEL), D_MODEL),
        "conv_k": nrm(ks[7], (N_A, CONV_WIDTH, D_MODEL), CONV_WIDTH),
        "conv_w_out": nrm(ks[8], (N_A, D_MODEL, D_MODEL), D_MODEL),
        "mla_w_a": nrm(ks[9], (N_B, D_MODEL, Q_LORA + KV_LORA + QK_ROPE), D_MODEL),
        "mla_q_norm": gain(ks[10], (N_B, Q_LORA)),
        "mla_w_uq": nrm(ks[11], (N_B, Q_LORA, MLA_HEADS * QK_HEAD), Q_LORA),
        "mla_kv_norm": gain(ks[12], (N_B, KV_LORA)),
        "mla_w_ukv": nrm(ks[13], (N_B, KV_LORA, MLA_HEADS * (QK_NOPE + V_HEAD)), KV_LORA),
        "mla_q_gain": gain(ks[14], (N_B, QK_HEAD)),
        "mla_k_gain": gain(ks[15], (N_B, QK_HEAD)),
        "mla_w_o": nrm(ks[16], (N_B, MLA_HEADS * V_HEAD, D_MODEL), MLA_HEADS * V_HEAD),
        "sg_w_in": nrm(ks[17], (N_C, D_MODEL, 2 * SG_WIDTH), D_MODEL),
        "sg_v_norm": gain(ks[18], (N_C, SG_WIDTH)),
        "sg_w_s": nrm(ks[19], (N_C, SG_GROUPS, SG_CHUNK, SG_CHUNK), SG_CHUNK),
        "sg_b": 1.0 + 0.1 * jax.random.normal(ks[20], (N_C, SG_GROUPS, SG_CHUNK), jnp.float32),
        "sg_w_out": nrm(ks[21], (N_C, SG_WIDTH, D_MODEL), SG_WIDTH),
    }

def first_block(x, positions, norm_g, ffn_gate, ffn_up, ffn_down,
              conv_w_in, conv_k, conv_w_out,
              mla_w_a, mla_q_norm, mla_w_uq, mla_kv_norm, mla_w_ukv, mla_q_gain, mla_k_gain, mla_w_o,
              sg_w_in, sg_v_norm, sg_w_s, sg_b, sg_w_out):
    inv_freq = 1.0 / (ROPE_THETA ** (jnp.arange(0, QK_ROPE, 2, dtype=jnp.float32) / QK_ROPE))
    ang = positions.astype(jnp.float32)[..., None] * inv_freq
    cos = jnp.cos(ang).astype(x.dtype)
    sin = jnp.sin(ang).astype(x.dtype)

    ia = ib = ic = 0
    for i in range(DEPTH):
        x = x + 0.5 * swiglu(rms_norm(x, norm_g[i, 0]), ffn_gate[i, 0], ffn_up[i, 0], ffn_down[i, 0])
        hn = rms_norm(x, norm_g[i, 1])
        kind = i % N_MIXERS
        if kind == 0:
            mix = short_conv_mixer(hn, conv_w_in[ia], conv_k[ia], conv_w_out[ia])
            ia += 1
        elif kind == 1:
            mix = mla_mixer(hn, cos, sin, mla_w_a[ib], mla_q_norm[ib], mla_w_uq[ib], mla_kv_norm[ib],
                            mla_w_ukv[ib], mla_q_gain[ib], mla_k_gain[ib], mla_w_o[ib])
            ib += 1
        else:
            mix = spatial_gating_mixer(hn, sg_w_in[ic], sg_v_norm[ic], sg_w_s[ic], sg_b[ic], sg_w_out[ic])
            ic += 1
        x = x + mix
        x = x + 0.5 * swiglu(rms_norm(x, norm_g[i, 2]), ffn_gate[i, 1], ffn_up[i, 1], ffn_down[i, 1])
    return x


DEPTH_2 = 2

PLE_DIM = 256
NORM_EPS = 1e-6
NEG_INF = -1e30
NUM_BUCKETS = 32
MAX_DISTANCE = 128
A_HEADS = 4
A_HEAD_DIM = 64
A_QBLOCK = 128
B_HEADS = 8
B_GROUPS = 2
B_REP = B_HEADS // B_GROUPS
B_HEAD_DIM = 64
B_CMP_LEN = 32
B_CMP_STRIDE = 16
B_CMP_HIDDEN = 256
B_SEL_BLOCK = 64
B_SEL_TOPK = 16
B_WINDOW = 512
B_QBLOCK = 64
B_SEL_FORCE = 1e6
C_HEADS = 8
C_GROUPS = 2
C_REP = C_HEADS // C_GROUPS
C_HEAD_DIM = 64
C_WINDOW = 128
C_QBLOCK = 128

A_WIDTH = A_HEADS * 2 * A_HEAD_DIM
B_WIDTH = B_HEADS * B_HEAD_DIM
B_KV = B_GROUPS * B_HEAD_DIM
C_WIDTH = C_HEADS * C_HEAD_DIM
C_KV = C_GROUPS * C_HEAD_DIM
N_BIAS_HEADS = A_HEADS + B_HEADS + C_HEADS
IN_SPLITS = (A_WIDTH, A_WIDTH, A_WIDTH,
             B_WIDTH, B_KV, B_KV, B_KV, B_KV, B_KV, B_KV, 3 * B_HEADS,
             C_WIDTH, C_KV, C_KV,
             D_MODEL, D_MODEL, D_MODEL)
D_IN = 3 * A_WIDTH + B_WIDTH + 6 * B_KV + 3 * B_HEADS + C_WIDTH + 2 * C_KV + 3 * D_MODEL


def rms_norm_2(x, g):
    xf = x.astype(jnp.float32)
    y = xf * lax.rsqrt(jnp.mean(xf * xf, axis=-1, keepdims=True) + NORM_EPS)
    return (y * g.astype(jnp.float32)).astype(x.dtype)

def swiglu_2(x, wi, wo):
    gate, up = jnp.split(x @ wi, 2, axis=-1)
    return (jax.nn.silu(gate) * up) @ wo

def split_cols(z, sizes):
    outs, start = [], 0
    for s in sizes:
        outs.append(z[..., start:start + s])
        start += s
    return outs

def rel_bucket(dist):
    n = jnp.maximum(dist, 0)
    max_exact = NUM_BUCKETS // 2
    nf = jnp.maximum(n, 1).astype(jnp.float32)
    large = max_exact + (jnp.log(nf / max_exact) / math.log(MAX_DISTANCE / max_exact)
                         * (NUM_BUCKETS - max_exact)).astype(jnp.int32)
    large = jnp.minimum(large, NUM_BUCKETS - 1)
    return jnp.where(n < max_exact, n, large)

def head_bias(table, dist):
    return jnp.moveaxis(table[rel_bucket(dist)].astype(jnp.float32), -1, 0)

def grouped_head_bias(table, dist, groups, rep):
    b = head_bias(table, dist)
    return b.reshape((groups, rep) + dist.shape)

def masked_softmax(s, mask):
    return jax.nn.softmax(jnp.where(mask, s, NEG_INF), axis=-1) * mask

def diff_attention(q, k, v, bias_table, lam, lam_init, subln_g):
    bsz, seq = q.shape[:2]
    nblk = seq // A_QBLOCK
    scale = A_HEAD_DIM ** -0.5
    qb = q.reshape(bsz, nblk, A_QBLOCK, A_HEADS, 2, A_HEAD_DIM).swapaxes(0, 1)
    kpos = jnp.arange(seq)

    def block(args):
        i, qi = args
        qpos = i * A_QBLOCK + jnp.arange(A_QBLOCK)
        dist = qpos[:, None] - kpos[None, :]
        s = jnp.einsum('bqhcd,bkhcd->bchqk', qi, k, preferred_element_type=jnp.float32) * scale
        s = s + head_bias(bias_table, dist)[None, None]
        pr = masked_softmax(s, dist >= 0)
        attn = pr[:, 0] - lam * pr[:, 1]
        return jnp.einsum('bhqk,bkhe->bqhe', attn.astype(v.dtype), v)

    o = lax.map(block, (jnp.arange(nblk), qb))
    o = o.swapaxes(0, 1).reshape(bsz, seq, A_HEADS, 2 * A_HEAD_DIM)
    o = rms_norm_2(o, subln_g) * (1.0 - lam_init)
    return o.reshape(bsz, seq, A_WIDTH)

def nsa_attention(q, kc, vc, ks, vs, kw, vw, gates, bias_table, cmp_pos, cmp_w1, cmp_w2):
    bsz, seq = q.shape[:2]
    scale = B_HEAD_DIM ** -0.5
    n_chunk = seq // B_CMP_STRIDE
    n_cmp = n_chunk - 1
    n_sel = seq // B_SEL_BLOCK
    top_k = min(B_SEL_TOPK, n_sel)
    nblk = seq // B_QBLOCK

    def compress(t, pos, w1, w2):
        c = t.reshape(bsz, n_chunk, B_CMP_STRIDE, B_GROUPS, B_HEAD_DIM)
        blk = jnp.concatenate([c[:, :-1], c[:, 1:]], axis=2) + pos[None, None, :, None, :]
        blk = blk.transpose(0, 1, 3, 2, 4).reshape(bsz, n_cmp, B_GROUPS, B_CMP_LEN * B_HEAD_DIM)
        return jax.nn.gelu(blk @ w1) @ w2

    k_cmp = compress(kc, cmp_pos[0], cmp_w1[0], cmp_w2[0])
    v_cmp = compress(vc, cmp_pos[1], cmp_w1[1], cmp_w2[1])
    cmp_start = jnp.arange(n_cmp) * B_CMP_STRIDE
    cmp_end = cmp_start + B_CMP_LEN - 1
    sel_start = jnp.arange(n_sel) * B_SEL_BLOCK
    overlap = ((cmp_start[:, None] < sel_start[None, :] + B_SEL_BLOCK)
               & (cmp_start[:, None] + B_CMP_LEN > sel_start[None, :])).astype(jnp.float32)
    ks_blk = ks.reshape(bsz, n_sel, B_SEL_BLOCK, B_GROUPS, B_HEAD_DIM).transpose(0, 3, 1, 2, 4)
    vs_blk = vs.reshape(bsz, n_sel, B_SEL_BLOCK, B_GROUPS, B_HEAD_DIM).transpose(0, 3, 1, 2, 4)
    kw_pad = jnp.pad(kw, ((0, 0), (B_WINDOW, 0), (0, 0), (0, 0)))
    vw_pad = jnp.pad(vw, ((0, 0), (B_WINDOW, 0), (0, 0), (0, 0)))
    tbg = bias_table.reshape(NUM_BUCKETS, B_GROUPS, B_REP).transpose(1, 0, 2)
    b_idx = jnp.arange(bsz)[:, None, None, None]
    g_idx = jnp.arange(B_GROUPS)[None, :, None, None]
    blk_id = jnp.arange(n_sel)
    qb = q.reshape(bsz, nblk, B_QBLOCK, B_GROUPS, B_REP, B_HEAD_DIM).swapaxes(0, 1)
    gb = gates.reshape(bsz, nblk, B_QBLOCK, B_GROUPS, B_REP, 3).swapaxes(0, 1)

    def block(args):
        i, qi, gi = args
        qpos = i * B_QBLOCK + jnp.arange(B_QBLOCK)
        dist_c = qpos[:, None] - cmp_end[None, :]
        s_c = jnp.einsum('bqgrd,bngd->bgrqn', qi, k_cmp, preferred_element_type=jnp.float32) * scale
        s_c = s_c + grouped_head_bias(bias_table, dist_c, B_GROUPS, B_REP)
        p_c = masked_softmax(s_c, dist_c >= 0)
        o_c = jnp.einsum('bgrqn,bngd->bqgrd', p_c.astype(v_cmp.dtype), v_cmp)
        imp = jnp.einsum('bgrqn,nm->bgqm', p_c, overlap)
        cur = qpos // B_SEL_BLOCK
        forced = (blk_id[None, :] == 0) | (blk_id[None, :] == cur[:, None]) | (blk_id[None, :] == cur[:, None] - 1)
        future = blk_id[None, :] > cur[:, None]
        imp = jnp.where(forced, B_SEL_FORCE, jnp.where(future, -B_SEL_FORCE, imp))
        _, idx = lax.top_k(imp, top_k)
        n_keys = top_k * B_SEL_BLOCK
        k_sel = ks_blk[b_idx, g_idx, idx].reshape(bsz, B_GROUPS, B_QBLOCK, n_keys, B_HEAD_DIM)
        v_sel = vs_blk[b_idx, g_idx, idx].reshape(bsz, B_GROUPS, B_QBLOCK, n_keys, B_HEAD_DIM)
        kpos_s = (idx[..., None] * B_SEL_BLOCK + jnp.arange(B_SEL_BLOCK)).reshape(bsz, B_GROUPS, B_QBLOCK, n_keys)
        dist_s = qpos[None, None, :, None] - kpos_s
        bias_s = tbg[g_idx, rel_bucket(dist_s)].astype(jnp.float32).transpose(0, 1, 4, 2, 3)
        s_s = jnp.einsum('bqgrd,bgqld->bgrql', qi, k_sel, preferred_element_type=jnp.float32) * scale + bias_s
        p_s = masked_softmax(s_s, (dist_s >= 0)[:, :, None])
        o_s = jnp.einsum('bgrql,bgqld->bqgrd', p_s.astype(v_sel.dtype), v_sel)
        start = i * B_QBLOCK
        k_win = lax.dynamic_slice_in_dim(kw_pad, start, B_WINDOW + B_QBLOCK, axis=1)
        v_win = lax.dynamic_slice_in_dim(vw_pad, start, B_WINDOW + B_QBLOCK, axis=1)
        kpos_w = start - B_WINDOW + jnp.arange(B_WINDOW + B_QBLOCK)
        dist_w = qpos[:, None] - kpos_w[None, :]
        mask_w = (dist_w >= 0) & (dist_w < B_WINDOW) & (kpos_w >= 0)[None, :]
        s_w = jnp.einsum('bqgrd,bkgd->bgrqk', qi, k_win, preferred_element_type=jnp.float32) * scale
        s_w = s_w + grouped_head_bias(bias_table, dist_w, B_GROUPS, B_REP)
        p_w = masked_softmax(s_w, mask_w)
        o_w = jnp.einsum('bgrqk,bkgd->bqgrd', p_w.astype(v_win.dtype), v_win)
        return gi[..., 0:1] * o_c + gi[..., 1:2] * o_s + gi[..., 2:3] * o_w

    o = lax.map(block, (jnp.arange(nblk), qb, gb))
    return o.swapaxes(0, 1).reshape(bsz, seq, B_WIDTH)

def swa_sink_attention(q, k, v, bias_table, sinks):
    bsz, seq = q.shape[:2]
    scale = C_HEAD_DIM ** -0.5
    nblk = seq // C_QBLOCK
    k_pad = jnp.pad(k, ((0, 0), (C_WINDOW, 0), (0, 0), (0, 0)))
    v_pad = jnp.pad(v, ((0, 0), (C_WINDOW, 0), (0, 0), (0, 0)))
    qb = q.reshape(bsz, nblk, C_QBLOCK, C_GROUPS, C_REP, C_HEAD_DIM).swapaxes(0, 1)
    sink = jnp.broadcast_to(sinks.astype(jnp.float32).reshape(C_GROUPS, C_REP, 1, 1),
                            (bsz, C_GROUPS, C_REP, C_QBLOCK, 1))

    def block(args):
        i, qi = args
        start = i * C_QBLOCK
        qpos = start + jnp.arange(C_QBLOCK)
        kb = lax.dynamic_slice_in_dim(k_pad, start, C_WINDOW + C_QBLOCK, axis=1)
        vb = lax.dynamic_slice_in_dim(v_pad, start, C_WINDOW + C_QBLOCK, axis=1)
        kpos = start - C_WINDOW + jnp.arange(C_WINDOW + C_QBLOCK)
        dist = qpos[:, None] - kpos[None, :]
        mask = (dist >= 0) & (dist < C_WINDOW) & (kpos >= 0)[None, :]
        s = jnp.einsum('bqgrd,bkgd->bgrqk', qi, kb, preferred_element_type=jnp.float32) * scale
        s = jnp.where(mask, s + grouped_head_bias(bias_table, dist, C_GROUPS, C_REP), NEG_INF)
        pr = jax.nn.softmax(jnp.concatenate([s, sink], axis=-1), axis=-1)[..., :-1]
        return jnp.einsum('bgrqk,bkgd->bqgrd', pr.astype(vb.dtype), vb)

    o = lax.map(block, (jnp.arange(nblk), qb))
    return o.swapaxes(0, 1).reshape(bsz, seq, C_WIDTH)

def second_inputs(seed: int = 0) -> dict:
    key = jax.random.key(seed)
    ks = jax.random.split(key, 20)

    def nrm(k, shape, scale):
        return jax.random.normal(k, shape, jnp.float32) * scale

    return {
        'x': nrm(ks[0], (BATCH, SEQ, D_MODEL), 1.0),
        'p': nrm(ks[1], (DEPTH_2, BATCH, SEQ, PLE_DIM), 1.0),
        'norm_g': 1.0 + nrm(ks[2], (DEPTH_2, 4, D_MODEL), 0.05),
        'ffn1_wi': nrm(ks[3], (DEPTH_2, D_MODEL, 2 * D_FF), D_MODEL ** -0.5),
        'ffn1_wo': nrm(ks[4], (DEPTH_2, D_FF, D_MODEL), D_FF ** -0.5),
        'w_in': nrm(ks[5], (DEPTH_2, D_MODEL, D_IN), D_MODEL ** -0.5),
        'diff_lambda': nrm(ks[6], (DEPTH_2, 4, A_HEAD_DIM), 0.1),
        'diff_subln': 1.0 + nrm(ks[7], (DEPTH_2, 2 * A_HEAD_DIM), 0.05),
        'nsa_cmp_pos': nrm(ks[8], (DEPTH_2, 2, B_CMP_LEN, B_HEAD_DIM), 0.1),
        'nsa_cmp_w1': nrm(ks[9], (DEPTH_2, 2, B_CMP_LEN * B_HEAD_DIM, B_CMP_HIDDEN), (B_CMP_LEN * B_HEAD_DIM) ** -0.5),
        'nsa_cmp_w2': nrm(ks[10], (DEPTH_2, 2, B_CMP_HIDDEN, B_HEAD_DIM), B_CMP_HIDDEN ** -0.5),
        'swa_sinks': nrm(ks[11], (DEPTH_2, C_HEADS), 0.5),
        'w_branch': nrm(ks[12], (DEPTH_2, 3, A_WIDTH, D_MODEL), A_WIDTH ** -0.5),
        'w_out': nrm(ks[13], (DEPTH_2, D_MODEL, D_MODEL), D_MODEL ** -0.5),
        'ffn2_wi': nrm(ks[14], (DEPTH_2, D_MODEL, 2 * D_FF), D_MODEL ** -0.5),
        'ffn2_wo': nrm(ks[15], (DEPTH_2, D_FF, D_MODEL), D_FF ** -0.5),
        'w_ple': nrm(ks[16], (DEPTH_2, PLE_DIM, D_MODEL), PLE_DIM ** -0.5),
        'w_ple_gate': nrm(ks[17], (DEPTH_2, D_MODEL, D_MODEL), D_MODEL ** -0.5),
        'rel_bias': nrm(ks[18], (NUM_BUCKETS, N_BIAS_HEADS), 0.5),
        'final_norm': 1.0 + nrm(ks[19], (D_MODEL,), 0.05),
    }

def second_block(x, p, norm_g, ffn1_wi, ffn1_wo, w_in, diff_lambda, diff_subln, nsa_cmp_pos,
              nsa_cmp_w1, nsa_cmp_w2, swa_sinks, w_branch, w_out, ffn2_wi, ffn2_wo,
              w_ple, w_ple_gate, rel_bias, final_norm):
    bsz, seq, _ = x.shape
    bias_a = rel_bias[:, :A_HEADS]
    bias_b = rel_bias[:, A_HEADS:A_HEADS + B_HEADS]
    bias_c = rel_bias[:, A_HEADS + B_HEADS:]
    h = x
    for i in range(DEPTH_2):
        h = h + 0.5 * swiglu_2(rms_norm_2(h, norm_g[i, 0]), ffn1_wi[i], ffn1_wo[i])
        n = rms_norm_2(h, norm_g[i, 1])
        (aq, ak, av, bq, bkc, bvc, bks, bvs, bkw, bvw, bgate,
         cq, ck, cv, ga, gb, gc) = split_cols(n @ w_in[i], IN_SPLITS)
        lam_init = 0.8 - 0.6 * math.exp(-0.3 * i)
        lp = diff_lambda[i].astype(jnp.float32)
        lam = jnp.exp(jnp.sum(lp[0] * lp[1])) - jnp.exp(jnp.sum(lp[2] * lp[3])) + lam_init
        ya = diff_attention(aq.reshape(bsz, seq, A_HEADS, 2, A_HEAD_DIM),
                            ak.reshape(bsz, seq, A_HEADS, 2, A_HEAD_DIM),
                            av.reshape(bsz, seq, A_HEADS, 2 * A_HEAD_DIM),
                            bias_a, lam, lam_init, diff_subln[i])
        kvb = lambda t: t.reshape(bsz, seq, B_GROUPS, B_HEAD_DIM)
        yb = nsa_attention(bq.reshape(bsz, seq, B_GROUPS, B_REP, B_HEAD_DIM),
                           kvb(bkc), kvb(bvc), kvb(bks), kvb(bvs), kvb(bkw), kvb(bvw),
                           jax.nn.sigmoid(bgate.reshape(bsz, seq, B_GROUPS, B_REP, 3)),
                           bias_b, nsa_cmp_pos[i], nsa_cmp_w1[i], nsa_cmp_w2[i])
        yc = swa_sink_attention(cq.reshape(bsz, seq, C_GROUPS, C_REP, C_HEAD_DIM),
                                ck.reshape(bsz, seq, C_GROUPS, C_HEAD_DIM),
                                cv.reshape(bsz, seq, C_GROUPS, C_HEAD_DIM),
                                bias_c, swa_sinks[i])
        merged = (jax.nn.sigmoid(ga) * (ya @ w_branch[i, 0])
                  + jax.nn.sigmoid(gb) * (yb @ w_branch[i, 1])
                  + jax.nn.sigmoid(gc) * (yc @ w_branch[i, 2]))
        h = h + merged @ w_out[i]
        h = h + 0.5 * swiglu_2(rms_norm_2(h, norm_g[i, 2]), ffn2_wi[i], ffn2_wo[i])
        h = h + jax.nn.sigmoid(rms_norm_2(h, norm_g[i, 3]) @ w_ple_gate[i]) * (p[i] @ w_ple[i])
    return rms_norm_2(h, final_norm)


def setup_inputs(seed=0):
    out = dict(first_inputs(seed))
    for name, value in second_inputs(seed + 1).items():
        if name != "x":
            out[name + "_2"] = value
    return out


def reference(
    x, positions, norm_g, ffn_gate, ffn_up, ffn_down, conv_w_in, conv_k, conv_w_out, mla_w_a,
    mla_q_norm, mla_w_uq, mla_kv_norm, mla_w_ukv, mla_q_gain, mla_k_gain, mla_w_o, sg_w_in,
    sg_v_norm, sg_w_s, sg_b, sg_w_out, p_2, norm_g_2, ffn1_wi_2, ffn1_wo_2, w_in_2,
    diff_lambda_2, diff_subln_2, nsa_cmp_pos_2, nsa_cmp_w1_2, nsa_cmp_w2_2, swa_sinks_2,
    w_branch_2, w_out_2, ffn2_wi_2, ffn2_wo_2, w_ple_2, w_ple_gate_2, rel_bias_2, final_norm_2,
):
    x = first_block(
        x, positions, norm_g, ffn_gate, ffn_up, ffn_down, conv_w_in, conv_k, conv_w_out,
        mla_w_a, mla_q_norm, mla_w_uq, mla_kv_norm, mla_w_ukv, mla_q_gain, mla_k_gain, mla_w_o,
        sg_w_in, sg_v_norm, sg_w_s, sg_b, sg_w_out,
    )
    return second_block(
        x, p_2, norm_g_2, ffn1_wi_2, ffn1_wo_2, w_in_2, diff_lambda_2, diff_subln_2,
        nsa_cmp_pos_2, nsa_cmp_w1_2, nsa_cmp_w2_2, swa_sinks_2, w_branch_2, w_out_2, ffn2_wi_2,
        ffn2_wo_2, w_ple_2, w_ple_gate_2, rel_bias_2, final_norm_2,
    )


_drawn_inputs = setup_inputs


def setup_inputs(seed=0):
    import zlib

    import numpy as np

    out = dict(_drawn_inputs(seed))
    spreads = {}
    factors = {'mla_q_norm': 6.178,
     'mla_kv_norm': 4.372,
     'mla_q_gain': 6.528,
     'mla_k_gain': 6.615,
     'sg_v_norm': 11.225,
     'diff_subln_2': 15.92,
     'nsa_cmp_pos_2': 17.116,
     'swa_sinks_2': 70.241,
     'sg_b': 3.834}
    for name, (base, spread) in spreads.items():
        noise = np.random.default_rng([zlib.crc32(name.encode()), seed]).standard_normal(out[name].shape)
        drawn = base * np.exp(spread * noise) if base else spread * noise
        out[name] = jnp.asarray(drawn.astype(out[name].dtype))
    for name, factor in factors.items():
        out[name] = (out[name] * factor).astype(out[name].dtype)
    return out
```

```python
from contextlib import ExitStack

import numpy as np

import concourse.bass as bass
from concourse import mybir

ALU = mybir.AluOpType
ACT = mybir.ActivationFunctionType
AX = mybir.AxisListType
F32 = mybir.dt.float32
F32R = mybir.dt.float32r
I32 = mybir.dt.int32

P = 128
TOK = 256
NT = TOK // P
D = 1024
KD = D // P
FF = 2816
EPS = 1e-6
TILE = 2048
RING = 3
CW = 256
NCH = FF // CW
NEG = -1e30
QL, KVL, ROPE, NOPE, VH, QKH, MH = 256, 128, 32, 64, 64, 96, 16
RSQRT_MAGIC = float(0x5F3759DF)
TWO_PI = (6.28125, 0.0019340515136718750, 1.255665914356996e-06)
PI_IN = 3.1415925

C_ID = 0
C_FLIP = 128
C_CAUSAL = 256
C_LOWT = 512
C_CMPOK = 640
C_FREQ = 672
C_OHREV = 688
C_OHF = C_OHREV + 768
C_END = C_OHF + 512
ARENA = 15880

G_SGV = 20
G_CONV = 21
G_MISC = 27
G_ROWS = 28


W_AQ, W_AK, W_AV, W_BQ, W_BC, W_BS, W_BW, W_BG = 0, 512, 1024, 1536, 2048, 2304, 2560, 2816
W_CQ, W_CKV, W_G = 2840, 3352, 3608
NCMP = 15
LAM_INIT = [0.8 - 0.6 * float(np.exp(-0.3 * i)) for i in range(2)]


class Seen:

    def __init__(self):
        self.n, self.turn, self.rate, self.before = {}, None, {}, {}

    def next(self, sem, k=1):
        self.n[sem.name] = self.n.get(sem.name, 0) + k
        v = self.n[sem.name]
        if self.turn is not None:
            v = self.turn * self.rate[sem.name] + v
        return v

    def enter(self, turn, rate):
        self.turn, self.rate, self.before = turn, {s.name: r for s, r in rate}, dict(self.n)

    def leave(self, turns):
        for name, r in self.rate.items():
            assert self.n.get(name, 0) - self.before.get(name, 0) == r, (name, r)
            self.n[name] += (turns - 1) * r
        self.turn = None


def full_plan():
    plan = []
    for i in range(4):
        plan += [("norm", 3 * i), ("ffn", 1, i, 0), ("norm", 3 * i + 1)]
        plan += [("conv", i // 3)] if i % 3 == 0 else [("mla",)] if i == 1 else [("sg",)]
        plan += [("norm", 3 * i + 2), ("ffn", 1, i, 1)]
    plan += [("tables",)]
    for i in range(2):
        plan += [("norm", 12 + 4 * i), ("ffn", 2, i, 0), ("norm", 13 + 4 * i), ("mix", i)]
        plan += [("norm", 14 + 4 * i), ("ffn", 2, i, 1), ("norm", 15 + 4 * i), ("ple", i)]
    return plan + [("final",)]


def build(nc, A, out, plan=None):
    plan = plan or full_plan()
    with ExitStack() as ctx:
        def sb(name, shape, dt=F32):
            return ctx.enter_context(nc.sbuf_tensor(name, shape, dt))

        def sem(name):
            return ctx.enter_context(nc.semaphore(name))

        MIX_BANKS = 21 + 24
        raw = [sb(f"raw{i}", [P, TILE]) for i in range(RING)]
        w_hi = [sb(f"w_hi{i}", [P, TILE], F32R) for i in range(RING)]
        w_lo = [sb(f"w_lo{i}", [P, TILE], F32R) for i in range(RING)]
        xT_hi = sb("xT_hi", [P, KD, TOK], F32R)
        xT_lo = sb("xT_lo", [P, KD, TOK], F32R)
        hT_hi = sb("hT_hi", [P, 2, 2, TOK], F32R)
        hT_lo = sb("hT_lo", [P, 2, 2, TOK], F32R)
        yT_hi = sb("yT_hi", [P, 4, TOK], F32R)
        yT_lo = sb("yT_lo", [P, 4, TOK], F32R)
        x = sb("x", [P, NT, D])
        xn = sb("xn", [P, NT, D])
        gate = sb("gate", [P, 512])
        prod = sb("prod", [P, 512])
        consts = sb("consts", [P, C_END])
        gains = sb("gains", [P, KD, 32])
        ss = sb("ss", [P, 8])
        nwt = sb("nwt", [P, 64])
        nwv = sb("nwv", [P, 64])
        rstd = sb("rstd", [P, 8])
        arena = sb("arena", [P, ARENA])
        pos = sb("pos", [P, NT], I32)
        cos = sb("cos", [P, NT, 16])
        sin = sb("sin", [P, NT, 16])
        g96 = sb("g96", [P, 2, QKH])

        def carve(at, *shape):
            n = int(np.prod(shape))
            v = arena[:, at:at + n]
            names = " ".join("abcd"[:len(shape)])
            dims = {"abcd"[i]: shape[i] for i in range(len(shape) - 1)}
            return v.rearrange(f"p ({names}) -> p {names}", **dims) if len(shape) > 1 else v

        g_rows = arena[0:G_ROWS, 0:D]
        zconv = carve(0, 2, TOK + 2)
        yconv = carve(520, 2, TOK)
        Q = carve(0, NT, MH, QKH)
        KV = carve(3072, NT, MH, NOPE + VH)
        KF = carve(7168, NT, MH, QKH)
        squares = carve(7168, NT, MH, QKH)
        latent = carve(10240, NT, QL + KVL + ROPE)
        cn = carve(11072, NT, QL + KVL)
        kpe = carve(11840, NT, ROPE)
        rtmp = carve(11904, 4, NT * MH, 16)
        headT = [carve(13952 + 512 * i, 512) for i in range(2)]
        S = [sb(f"S{i}", [P, 384]) for i in range(2)]
        PT = [sb(f"PT{i}", [P, 384]) for i in range(2)]
        nmax = [sb(f"nmax{i}", [P, 2]) for i in range(2)]
        esum = [sb(f"esum{i}", [P, 2]) for i in range(2)]
        rsum = [sb(f"rsum{i}", [P, 2]) for i in range(2)]
        ssh = sb("ssh", [P, 64])
        rsh = sb("rsh", [P, 64])
        esink = [sb(f"esink{i}", [P, 2]) for i in range(2)]
        T = carve(0, 20, 256)
        TC = carve(5120, 8, 2 * NCMP)
        U = carve(5376, 20, 256)
        rv = carve(10496, 2, 384)
        lp = carve(11264, 2, 4, 64)
        prows = arena[0:64, 11776:11904]
        relb = arena[0:33, 11904:11924]
        AQ, AK, AV = carve(5376, 4, TOK), carve(6400, 4, TOK), carve(7424, NT, 512)
        BQ, CQ = carve(8448, 4, TOK), carve(11008, 4, TOK)
        KC = carve(9472, 2, TOK)
        BS, BW, CKV = carve(9984, 512), carve(10496, 512), carve(12032, 512)
        gB = carve(12544, NT, 24)
        KC2 = carve(12592, 2, 2, TOK)
        blk = carve(13616, 2, 16, 2 * NCMP)
        hidT = carve(14576, 2, 2, 2 * NCMP)
        kcT = carve(14696, 2 * NCMP)
        vc = arena[0:NCMP, 14726:14854]
        YA = carve(14854, NT, 512)
        merged = xn[:].rearrange("p t (m n) -> p (t m) n", n=TOK)
        blk_hi = yT_hi[:].rearrange("p k n -> p (k n)")[:, 0:960].rearrange("p (v j n) -> p v j n", v=2, j=16)
        blk_lo = yT_lo[:].rearrange("p k n -> p (k n)")[:, 0:960].rearrange("p (v j n) -> p v j n", v=2, j=16)
        pos2 = sb("pos2", [P, 2, 2, 16])
        w2 = sb("w2", [P, 2, 2, 2, 64])
        neglam = sb("neglam", [P, 2])
        sinks = sb("sinks", [P, 16])
        negsinks = sb("negsinks", [P, 16])
        subln = sb("subln", [P, 2])
        ple_in = sb("ple_in", [P, NT, 256])
        gfin = carve(0, D)
        wsT = carve(0, 8, P)
        wsr = carve(1024, 8, P)
        mixed = carve(2048, 2, TOK)
        sgb = carve(2560, D)

        ident = consts[:, C_ID:C_ID + P]

        acc = [ctx.enter_context(nc.psum_tensor(f"acc{i}", [P, 512], F32)) for i in range(4)]
        up = [ctx.enter_context(nc.psum_tensor(f"up{i}", [P, 512], F32)) for i in range(4)]

        landed = [sem(f"landed{i}") for i in range(RING)]
        const_in = sem("const_in")
        gain_in = sem("gain_in")
        rows_clear = sem("rows_clear")
        hi_ready = sem("hi_ready")
        lo_ready = sem("lo_ready")
        tile_used = sem("tile_used")
        bank_free = sem("bank_free")
        setup_pe = sem("setup_pe")
        setup_dve = sem("setup_dve")
        x_ready = sem("x_ready")
        ss_ready = sem("ss_ready")
        xn_ready = sem("xn_ready")
        xT_ready = sem("xT_ready")
        xhi_ready = sem("xhi_ready")
        xlo_ready = sem("xlo_ready")
        gate_ready = sem("gate_ready")
        prod_ready = sem("prod_ready")
        hhi_ready = sem("hhi_ready")
        hlo_ready = sem("hlo_ready")
        acc_done = sem("acc_done")
        dve_step = sem("dve_step")
        act_step = sem("act_step")
        misc_in = sem("misc_in")
        trig_arg = sem("trig_arg")
        trig_done = sem("trig_done")
        cn_ready = sem("cn_ready")
        group_done = sem("group_done")
        kv_copied = sem("kv_copied")
        qk_ready = sem("qk_ready")
        headT_done = sem("headT_done")
        headT_ready = sem("headT_ready")
        scores_done = sem("scores_done")
        s_ready = sem("s_ready")
        nmax_ready = sem("nmax_ready")
        exp_ready = sem("exp_ready")
        p_ready = sem("p_ready")
        turned = sem("turned")
        pt_ready = sem("pt_ready")
        o_done, oa_done = sem("o_done"), sem("oa_done")
        ohi_ready = sem("ohi_ready")
        olo_ready = sem("olo_ready")
        ws_in = sem("ws_in")
        ws_turned = sem("ws_turned")
        ws_ready = sem("ws_ready")
        v_ready = sem("v_ready")
        mix_done = sem("mix_done")
        tables_in = sem("tables_in")
        arena_free = sem("arena_free")
        tab_pe = sem("tab_pe")
        tab_dve = sem("tab_dve")
        tab_act = sem("tab_act")
        rv_stored = sem("rv_stored")
        rv_ready = sem("rv_ready")
        u_in = sem("u_in")
        gates_ready = sem("gates_ready")
        kc_ready = sem("kc_ready")
        kc2_in = sem("kc2_in")
        blk_ready = sem("blk_ready")
        blkhi_ready = sem("blkhi_ready")
        blklo_ready = sem("blklo_ready")
        hid_ready = sem("hid_ready")
        cmp_done = sem("cmp_done")
        cmp_ready = sem("cmp_ready")
        proj_ready = sem("proj_ready")
        ya_copied = sem("ya_copied")
        ya_ready = sem("ya_ready")
        merge_step = sem("merge_step")
        mhi_ready = sem("mhi_ready")
        mlo_ready = sem("mlo_ready")
        ple_arrived = sem("ple_arrived")
        fin_in = sem("fin_in")
        w2_in = sem("w2_in")
        fin_ready = sem("fin_ready")
        scratch = nc.dram_tensor("bias_rows", (20, 384), F32, kind="Internal").ap()
        vn_ready = sem("vn_ready")
        stored = sem("stored")

        def kpn(w):
            return w.rearrange("(k p) n -> p k n", p=P)

        def tview(buf, nk, n):
            return buf[:, 0:nk * n].rearrange("p (k n) -> p k n", k=nk)

        def ffn_weights(s):
            _, blk, i, j = s
            if blk == 1:
                return A["ffn_gate"][i, j], A["ffn_up"][i, j], A["ffn_down"][i, j]
            wi = A["ffn1_wi_2" if j == 0 else "ffn2_wi_2"][i]
            wo = A["ffn1_wo_2" if j == 0 else "ffn2_wo_2"][i]
            return wi[:, 0:FF], wi[:, FF:2 * FF], wo

        def up_tile(w, col):
            return (KD, CW, [(slice(None), kpn(w)[:, :, col:col + CW])])

        def query_tile(w, col, j):
            return (KD, CW, [(slice(P * r + 64 * g, P * r + 64 * g + 64),
                              kpn(w)[:, :, col + 256 * g + 64 * (2 * j + r):col + 256 * g + 64 * (2 * j + r) + 64])
                             for r in range(2) for g in range(2)])

        def cols_tile(w, nk, col, n):
            return (nk, n, [(slice(None), kpn(w)[:, :, col:col + n])])

        def down_tile(w, row):
            return (2, D, [(slice(None), kpn(w[row:row + 2 * P, :]))])

        def tiles_of(s):
            if s[0] == "conv":
                w, wo = A["conv_w_in"][s[1]], A["conv_w_out"][s[1]]
                t = []
                for c in range(4):
                    t += [up_tile(w, D * m + CW * c) for m in (1, 2, 0)]
                    if c:
                        t.append(down_tile(wo, CW * (c - 1)))
                return t + [down_tile(wo, CW * 3)]
            if s[0] == "mla":
                wa, wq, wkv, wo = A["mla_w_a"][0], A["mla_w_uq"][0], A["mla_w_ukv"][0], A["mla_w_o"][0]
                t = [cols_tile(wa[512 * h:512 * h + 512, :], 4, 0, QL + KVL + ROPE) for h in range(2)]
                t += [cols_tile(wq, 2, 0, 1024), cols_tile(wq, 2, 1024, 512), cols_tile(wkv, 1, 0, 2048)]
                return t + [down_tile(wo, CW * i) for i in range(4)]
            if s[0] == "sg":
                w, wo = A["sg_w_in"][0], A["sg_w_out"][0]
                t = [cols_tile(w[512 * h:512 * h + 512, :], 4, D + 512 * g, 512) for g in range(2) for h in range(2)]
                for c in range(4):
                    t.append(up_tile(w, CW * c))
                    if c:
                        t.append(down_tile(wo, CW * (c - 1)))
                return t + [down_tile(wo, CW * 3)]
            if s[0] == "mix":
                w, w1 = A["w_in_2"][s[1]], A["nsa_cmp_w1_2"][s[1]]
                wb, wo = A["w_branch_2"][s[1]], A["w_out_2"][s[1]]
                t = [up_tile(w, W_BC)] + [up_tile(w, W_AQ + CW * j) for j in range(4)]
                t += [cols_tile(w[512 * h:512 * h + 512, :], 4, W_AV, 512) for h in range(2)]
                t += [query_tile(w, W_BQ, j) for j in range(2)] + [up_tile(w, W_BS), up_tile(w, W_BW)]
                t += [cols_tile(w, KD, W_BG, 24)]
                t += [up_tile(w1[v, 1024 * h:1024 * h + 1024, :], 0) for v in range(2) for h in range(2)]
                t += [query_tile(w, W_CQ, j) for j in range(2)] + [up_tile(w, W_CKV)]
                for br in range(3):
                    for c in range(2):
                        t += [up_tile(w, W_G + D * br + 512 * c + CW * j) for j in range(2)]
                        t += [cols_tile(wb[br], 4, 512 * c, 512)]
                return t + [down_tile(wo, CW * j) for j in range(4)]
            if s[0] == "ple":
                wg, wp = A["w_ple_gate_2"][s[1]], A["w_ple_2"][s[1]]
                t = []
                for c in range(2):
                    t += [cols_tile(wg[512 * h:512 * h + 512, :], 4, 512 * c, 512) for h in range(2)]
                    t += [cols_tile(wp, 2, 512 * c, 512)]
                return t
            return []

        def branch_units(br):
            if br == 0:
                return [(c, h, c == 1) for h in range(4) for c in range(2)]
            if br == 1:
                return [(k, h, h % 2 == 1 and k == "cmp") for h in range(8) for k in ("sel", "win", "cmp")]
            return [("win", h, h % 2 == 1) for h in range(8)]

        first = []
        count = 0
        for s in plan:
            first.append(count)
            count += 3 * NCH if s[0] == "ffn" else len(tiles_of(s))
        n_tiles = count

        block = ctx.enter_context(nc.Block())

        @block.sync
        def _(sp):
            seen = Seen()

            def slot_free(n):
                if n >= RING:
                    sp.wait_ge(lo_ready, seen.next(lo_ready))

            def load(n, t):
                slot_free(n)
                nk, ncol, parts = t
                dst = tview(raw[n % RING], nk, ncol)
                for cols, src in parts:
                    sp.dma_start(dst[:, :, cols], src).then_inc(landed[n % RING], 16)

            def ffn(s, n0):
                wg, wu, wd = ffn_weights(s)
                G = [up_tile(wg, CW * c) for c in range(NCH)]
                U = [up_tile(wu, CW * c) for c in range(NCH)]
                Dn = [down_tile(wd, CW * c) for c in range(NCH)]
                for j, t in enumerate([G[0], U[0], G[1], U[1], Dn[0]]):
                    load(n0 + j, t)
                base = n0 + 5
                with sp.Fori(0, 4) as i:
                    seen.enter(i, [(lo_ready, 6)])
                    for c in range(2):
                        for j, w in enumerate((wg, wu)):
                            n = base + 3 * c + j
                            slot_free(n)
                            sp.dma_start(tview(raw[n % RING], KD, CW),
                                         kpn(w)[:, :, bass.ds(i * (2 * CW) + (2 + c) * CW, CW)]
                                         ).then_inc(landed[n % RING], 16)
                        n = base + 3 * c + 2
                        slot_free(n)
                        sp.dma_start(tview(raw[n % RING], 2, D),
                                     wd[bass.ds(i * (2 * CW) + (1 + c) * CW, CW), :].rearrange("(k p) n -> p k n", p=P)
                                     ).then_inc(landed[n % RING], 16)
                    seen.leave(4)
                for j, t in enumerate([G[10], U[10], Dn[9], Dn[10]]):
                    load(n0 + 29 + j, t)

            for s, n0 in zip(plan, first):
                if s[0] == "ffn":
                    ffn(s, n0)
                else:
                    for j, t in enumerate(tiles_of(s)):
                        load(n0 + j, t)
            if plan[-1][0] == "final":
                sp.wait_ge(fin_ready, seen.next(fin_ready))
                res = xn
            else:
                sp.wait_ge(x_ready, NT * (1 + sum(s[0] not in ("norm", "tables", "final") for s in plan)))
                res = x
            sp.dma_start(out[0].rearrange("(t p) d -> p t d", p=P), res[:]).then_inc(stored, 16)
            sp.wait_ge(stored, 16)

        @block.scalar
        def _(act):
            seen = Seen()
            act.dma_start(consts[:], A["consts"]).then_inc(const_in, 16)
            act.dma_start(x[:], A["x"][0].rearrange("(t p) d -> p t d", p=P)).then_inc(const_in, 16)

            parts_of = {}
            for s, n0 in zip(plan, first):
                for j, t in enumerate(tiles_of(s)):
                    parts_of[n0 + j] = len(t[2])

            def split_hi(n):
                if n >= n_tiles:
                    return
                act.wait_ge(landed[n % RING], seen.next(landed[n % RING], 16 * parts_of.get(n, 1)))
                nc.scalar.activation(w_hi[n % RING][:], raw[n % RING][:], ACT.Copy).then_inc(hi_ready, 1)

            def consumed(n):
                act.wait_ge(tile_used, seen.next(tile_used))
                split_hi(n + RING)

            def parts_hi(nk, row, dst=xT_hi, same=None):
                for k in range(nk):
                    if k % 2 == 0:
                        act.wait_ge(xT_ready, seen.next(xT_ready))
                    g = gains[:, k, row:row + 1] if same is None else same
                    last = nc.scalar.activation(dst[:, k, :], acc[k // 2][:, (k % 2) * TOK:(k % 2 + 1) * TOK],
                                                ACT.Copy, scale=g)
                    if k % 2 or k == nk - 1:
                        last.then_inc(xhi_ready, 1)

            def norm(row):
                for t in range(NT):
                    act.wait_ge(x_ready, seen.next(x_ready))
                    nc.scalar.activation(xn[:, t, :], x[:, t, :], ACT.Square,
                                         accum_out=ss[:, t:t + 1]).then_inc(ss_ready, 1)
                parts_hi(KD, row)

            def product_hi(par):
                act.wait_ge(prod_ready, seen.next(prod_ready))
                nc.scalar.activation(hT_hi[:, par], prod[:].rearrange("p (k n) -> p k n", k=2),
                                     ACT.Copy).then_inc(hhi_ready, 1)

            def ffn(s, n0, bank0):
                def chunk(n, c, down):
                    consumed(n)
                    b = (bank0 + 2 * c) % 4
                    nc.scalar.activation(gate[:], up[b][:], ACT.Silu).then_inc(gate_ready, 1)
                    consumed(n + 1)
                    product_hi(c % 2)
                    if down:
                        consumed(n + 2)

                chunk(n0, 0, False)
                chunk(n0 + 2, 1, True)
                with act.Fori(0, 4) as i:
                    seen.enter(i, [(landed[r], 32) for r in range(RING)] + [(tile_used, 6), (prod_ready, 2)])
                    chunk(n0 + 5, 2, True)
                    chunk(n0 + 8, 3, True)
                    seen.leave(4)
                chunk(n0 + 29, 10, True)
                consumed(n0 + 32)

            def conv(s, n0, bank0):
                for c in range(4):
                    n = n0 + 4 * c - (c > 0)
                    b = (bank0 + 3 * c) % 4
                    consumed(n)
                    nc.scalar.activation(gate[:], up[b][:], ACT.Copy).then_inc(gate_ready, 1)
                    consumed(n + 1)
                    consumed(n + 2)
                    product_hi(c % 2)
                    if c:
                        consumed(n + 3)
                consumed(n0 + 15)

            def exp_unit(u, widths=((1, 0, 256), (0, 256, 384)), sink=None):
                b = u % 2
                act.wait_ge(nmax_ready, seen.next(nmax_ready))
                for i, lo, hi in widths:
                    last = nc.scalar.activation(S[b][:, lo:hi], S[b][:, lo:hi], ACT.Exp, bias=nmax[b][:, i:i + 1],
                                                accum_out=esum[b][:, i:i + 1])
                if sink is not None:
                    last = nc.scalar.activation(esink[b][:], nmax[b][:], ACT.Exp, bias=sink)
                last.then_inc(exp_ready, 1)

            def copy_turned(u, rows=P, width=384):
                act.wait_ge(turned, seen.next(turned))
                nc.scalar.activation(PT[u % 2][0:rows, 0:width], acc[2 + u % 2][0:rows, 0:width],
                                     ACT.Copy).then_inc(pt_ready, 1)

            def mla(s, n0, bank0):
                consumed(n0)
                consumed(n0 + 1)
                parts_hi(3, G_MISC)
                consumed(n0 + 2)
                consumed(n0 + 3)
                b = (bank0 + 8) % 4
                for g in range(4):
                    if g < 3:
                        act.wait_ge(group_done, seen.next(group_done))
                    else:
                        consumed(n0 + 4)
                    for t in range(NT):
                        last = nc.scalar.activation(
                            arena[:, 3072 + 2048 * t + 512 * g:3072 + 2048 * t + 512 * g + 512],
                            up[(b + 2 * g + t) % 4][:], ACT.Copy)
                    last.then_inc(kv_copied, 1)

                def o_hi(j):
                    act.wait_ge(o_done, seen.next(o_done))
                    nc.scalar.activation(xT_hi[:, j, :], up[2 + j % 2][:, 0:TOK],
                                         ACT.Copy).then_inc(ohi_ready, 1)

                for i in range(MH + 3):
                    if i < MH:
                        act.wait_ge(headT_done, seen.next(headT_done))
                        nc.scalar.activation(headT[i % 2][0:QKH, :], up[i % 2][0:QKH, :],
                                             ACT.Copy).then_inc(headT_ready, 1)
                    if 0 <= i - 1 < MH:
                        exp_unit(i - 1)
                    if 0 <= i - 2 < MH:
                        copy_turned(i - 2)
                    if 0 <= i - 3 < MH and (i - 3) % 2:
                        o_hi((i - 3) // 2)
                for j in range(4):
                    consumed(n0 + 5 + j)

            def sg(s, n0, bank0):
                for g in range(2):
                    consumed(n0 + 2 * g)
                    consumed(n0 + 2 * g + 1)
                    for t in range(NT):
                        last = nc.scalar.activation(xn[:, t, 512 * g:512 * g + 512],
                                                    up[(bank0 + 2 * g + t) % 4][:], ACT.Gelu_apprx_tanh)
                    last.then_inc(v_ready, 1)
                for c in range(4):
                    n = n0 + 4 + 2 * c - (c > 0)
                    consumed(n)
                    nc.scalar.activation(gate[:], up[(bank0 + 4 + 2 * c) % 4][:],
                                         ACT.Gelu_apprx_tanh).then_inc(gate_ready, 1)
                    product_hi(c % 2)
                    if c:
                        consumed(n + 1)
                consumed(n0 + 11)

            def tables():
                act.wait_ge(tab_dve, seen.next(tab_dve))
                nc.scalar.activation(ssh[:, 4:8], ssh[:, 0:4], ACT.Exp).then_inc(tab_act, 1)

            def mix(s, n0, bank0):
                n = n0
                for i in range(11):
                    consumed(n)
                    n += 1
                    if i == 6:
                        for v in range(2):
                            act.wait_ge(blk_ready, seen.next(blk_ready))
                            nc.scalar.activation(blk_hi[:, v], blk[:, v], ACT.Copy).then_inc(blkhi_ready, 1)
                consumed(n)
                nc.scalar.activation(gB.rearrange("p t h -> p (t h)"), up[(bank0 + 11) % 4][:, 0:48],
                                     ACT.Sigmoid).then_inc(gates_ready, 1)
                n += 1
                for v in range(2):
                    consumed(n)
                    consumed(n + 1)
                    n += 2
                    for m in range(2):
                        last = nc.scalar.activation(hidT[:, v, m, :], up[(bank0 + 12 + 2 * v + m) % 4][:, 0:2 * NCMP],
                                                    ACT.Gelu_apprx_tanh)
                    last.then_inc(hid_ready, 1)
                for _ in range(3):
                    consumed(n)
                    n += 1
                for br in range(3):
                    units = branch_units(br)
                    for i in range(len(units) + 2):
                        if i < len(units):
                            kind, h = units[i][:2]
                            if kind == "cmp":
                                exp_unit(i, ((0, 0, NCMP), (1, NCMP, 2 * NCMP)))
                            else:
                                exp_unit(i, sink=sinks[:, 8 * s[1] + h:8 * s[1] + h + 1] if br == 2 else None)
                        if 0 <= i - 1 < len(units):
                            if units[i - 1][0] == "cmp":
                                copy_turned(i - 1, NCMP, 256)
                            else:
                                copy_turned(i - 1)
                        if br and 0 <= i - 2 < len(units) and units[i - 2][2]:
                            j = units[i - 2][1] // 2
                            act.wait_ge(o_done, seen.next(o_done))
                            nc.scalar.activation(yT_hi[:, j, :], up[2 + j % 2][:, 0:TOK],
                                                 ACT.Copy).then_inc(ohi_ready, 1)
                    if br == 0:
                        parts_hi(4, 0, yT_hi, subln[:, s[1]:s[1] + 1])
                    for c in range(2):
                        if br or c:
                            act.wait_ge(merge_step, seen.next(merge_step))
                        for j, dst in enumerate((gate, prod)):
                            consumed(n)
                            n += 1
                            nc.scalar.activation(dst[:], up[(bank0 + 21 + 8 * br + 4 * c + j) % 4][:],
                                                 ACT.Sigmoid).then_inc(gate_ready, 1)
                        consumed(n)
                        n += 1
                act.wait_ge(merge_step, seen.next(merge_step))
                for j in range(4):
                    if j >= 2:
                        consumed(n)
                        n += 1
                    nc.scalar.activation(hT_hi[:, j % 2], merged[:, 2 * j:2 * j + 2, :], ACT.Copy).then_inc(mhi_ready, 1)
                consumed(n)
                consumed(n + 1)

            def ple(s, n0, bank0):
                act.wait_ge(xT_ready, seen.next(xT_ready))
                nc.scalar.activation(hT_hi[:, 0], acc[0][:].rearrange("p (k n) -> p k n", k=2),
                                     ACT.Copy).then_inc(xhi_ready, 1)
                for c in range(2):
                    consumed(n0 + 3 * c)
                    consumed(n0 + 3 * c + 1)
                    if c:
                        act.wait_ge(merge_step, seen.next(merge_step))
                    for t, dst in enumerate((gate, prod)):
                        last = nc.scalar.activation(dst[:], up[(bank0 + 4 * c + t) % 4][:], ACT.Sigmoid)
                    last.then_inc(gate_ready, 1)
                    consumed(n0 + 3 * c + 2)
                act.wait_ge(merge_step, seen.next(merge_step))

            def final():
                for t in range(NT):
                    act.wait_ge(x_ready, seen.next(x_ready))
                    nc.scalar.activation(xn[:, t, :], x[:, t, :], ACT.Square,
                                         accum_out=ss[:, t:t + 1]).then_inc(ss_ready, 1)

            act.wait_ge(trig_arg, seen.next(trig_arg))
            nc.scalar.activation(sin[:], sin[:], ACT.Sin)
            nc.scalar.activation(cos[:], cos[:], ACT.Sin).then_inc(trig_done, 1)
            act.wait_ge(const_in, seen.next(const_in, 32))
            for n in range(RING):
                split_hi(n)
            bank = 0
            for s, n0 in zip(plan, first):
                if s[0] == "norm":
                    norm(s[1])
                elif s[0] == "ffn":
                    ffn(s, n0, bank)
                    bank = (bank + 2 * NCH) % 4
                elif s[0] == "conv":
                    conv(s, n0, bank)
                    bank = (bank + 12) % 4
                elif s[0] == "mla":
                    mla(s, n0, bank)
                    bank = (bank + 16) % 4
                elif s[0] == "sg":
                    sg(s, n0, bank)
                    bank = (bank + 12) % 4
                elif s[0] == "tables":
                    tables()
                elif s[0] == "mix":
                    mix(s, n0, bank)
                    bank = (bank + MIX_BANKS) % 4
                elif s[0] == "ple":
                    ple(s, n0, bank)
                    bank = (bank + 8) % 4
                elif s[0] == "final":
                    final()

        @block.vector
        def _(dve):
            seen = Seen()

            def step(ins):
                ins.then_inc(dve_step, 1)
                dve.wait_ge(dve_step, seen.next(dve_step))

            def split_lo(n):
                if n >= n_tiles:
                    return
                dve.wait_ge(hi_ready, seen.next(hi_ready))
                nc.vector.tensor_tensor(w_lo[n % RING][:], raw[n % RING][:], w_hi[n % RING][:].bitcast(F32),
                                        ALU.subtract).then_inc(lo_ready, 1)

            def consumed(n):
                dve.wait_ge(tile_used, seen.next(tile_used))
                split_lo(n + RING)

            def rsqrt(dst, src, scale, width):
                v, t, y = nwv[:, 0:width], nwt[:, 0:width], dst
                step(nc.vector.tensor_scalar(v, src, scale, EPS, ALU.mult, ALU.add))
                step(nc.vector.tensor_single_scalar(t.bitcast(I32), v.bitcast(I32), 1, ALU.logical_shift_right))
                step(nc.vector.tensor_scalar(y.bitcast(I32), t.bitcast(I32), -1.0, RSQRT_MAGIC, ALU.mult, ALU.add))
                for _ in range(3):
                    step(nc.vector.tensor_tensor(t, y, y, ALU.mult))
                    step(nc.vector.tensor_tensor(t, t, v, ALU.mult))
                    step(nc.vector.tensor_scalar(t, t, -0.5, 1.5, ALU.mult, ALU.add))
                    step(nc.vector.tensor_tensor(y, y, t, ALU.mult))

            def parts_lo(nk, row, dst=xT_lo, hi=xT_hi, same=None):
                for k in range(nk):
                    if k % 2 == 0:
                        dve.wait_ge(xhi_ready, seen.next(xhi_ready))
                    g = gains[:, k, row:row + 1] if same is None else same
                    last = nc.vector.scalar_tensor_tensor(
                        dst[:, k, :], acc[k // 2][:, (k % 2) * TOK:(k % 2 + 1) * TOK], g,
                        hi[:, k, :].bitcast(F32), ALU.mult, ALU.subtract)
                    if k % 2 or k == nk - 1:
                        last.then_inc(xlo_ready, 1)

            def norm(row):
                dve.wait_ge(ss_ready, seen.next(ss_ready, NT))
                rsqrt(rstd[:, 0:NT], ss[:, 0:NT], 1.0 / D, NT)
                for t in range(NT):
                    nc.vector.tensor_scalar(xn[:, t, :], x[:, t, :], rstd[:, t:t + 1], None,
                                            ALU.mult).then_inc(xn_ready, 1)
                parts_lo(KD, row)

            def residual(scale):
                dve.wait_ge(acc_done, seen.next(acc_done))
                for t in range(NT):
                    for h in range(2):
                        cols = slice(512 * h, 512 * h + 512)
                        last = nc.vector.scalar_tensor_tensor(x[:, t, cols], acc[2 * t + h][:], scale, x[:, t, cols],
                                                              ALU.mult, ALU.add)
                    last.then_inc(x_ready, 1)
                dve.wait_ge(x_ready, seen.next(x_ready, NT))

            def product_parts(c):
                dve.wait_ge(hhi_ready, seen.next(hhi_ready))
                nc.vector.tensor_tensor(hT_lo[:, c % 2], prod[:].rearrange("p (k n) -> p k n", k=2),
                                        hT_hi[:, c % 2].bitcast(F32), ALU.subtract).then_inc(hlo_ready, 1)
                dve.wait_ge(hlo_ready, seen.next(hlo_ready))

            def ffn(s, n0, bank0):
                def chunk(n, c, down):
                    consumed(n)
                    consumed(n + 1)
                    dve.wait_ge(gate_ready, seen.next(gate_ready))
                    nc.vector.tensor_tensor(prod[:], gate[:], up[(bank0 + 2 * c + 1) % 4][:],
                                            ALU.mult).then_inc(prod_ready, 1)
                    dve.wait_ge(prod_ready, seen.next(prod_ready))
                    dve.sem_inc(bank_free, 2)
                    product_parts(c)
                    if down:
                        consumed(n + 2)

                chunk(n0, 0, False)
                chunk(n0 + 2, 1, True)
                with dve.Fori(0, 4) as i:
                    seen.enter(i, [(hi_ready, 6), (tile_used, 6), (gate_ready, 2), (prod_ready, 2), (hhi_ready, 2),
                                   (hlo_ready, 2)])
                    chunk(n0 + 5, 2, True)
                    chunk(n0 + 8, 3, True)
                    seen.leave(4)
                chunk(n0 + 29, 10, True)
                consumed(n0 + 32)
                residual(0.5)

            def conv(s, n0, bank0):
                step(nc.vector.memset(zconv[:, :, 0:2], 0.0))
                for c in range(4):
                    n = n0 + 4 * c - (c > 0)
                    b = bank0 + 3 * c
                    consumed(n)
                    consumed(n + 1)
                    dve.wait_ge(gate_ready, seen.next(gate_ready))
                    step(nc.vector.tensor_tensor(zconv[:, :, 2:], gate[:].rearrange("p (k n) -> p k n", k=2),
                                                 up[(b + 1) % 4][:].rearrange("p (k n) -> p k n", k=2), ALU.mult))
                    dve.sem_inc(bank_free, 2)
                    for j in (2, 1, 0):
                        for m in range(2):
                            tap = gains[:, 2 * c + m, G_CONV + 3 * s[1] + j:G_CONV + 3 * s[1] + j + 1]
                            z = zconv[:, m, j:j + TOK]
                            if j == 2:
                                last = nc.vector.tensor_scalar(yconv[:, m, :], z, tap, None, ALU.mult)
                            else:
                                last = nc.vector.scalar_tensor_tensor(yconv[:, m, :], z, tap, yconv[:, m, :],
                                                                      ALU.mult, ALU.add)
                        step(last)
                    consumed(n + 2)
                    nc.vector.tensor_tensor(prod[:], yconv[:].rearrange("p k n -> p (k n)"), up[(b + 2) % 4][:],
                                            ALU.mult).then_inc(prod_ready, 1)
                    dve.wait_ge(prod_ready, seen.next(prod_ready))
                    dve.sem_inc(bank_free, 1)
                    product_parts(c)
                    if c:
                        consumed(n + 3)
                consumed(n0 + 15)
                residual(1.0)

            def trig_arguments():
                posf, k = rsh[:, 0:NT], nwt[:, 0:32]
                step(nc.vector.tensor_copy(posf, pos[:]))
                for t in range(NT):
                    last = nc.vector.tensor_scalar(sin[:, t, :], consts[:, C_FREQ:C_FREQ + 16], posf[:, t:t + 1], None,
                                                   ALU.mult)
                step(last)
                ang = sin[:].rearrange("p t f -> p (t f)")
                shifted = cos[:].rearrange("p t f -> p (t f)")
                big = 1.5 * 2.0 ** 23
                step(nc.vector.tensor_scalar(k, ang, 1.0 / (2 * np.pi), big, ALU.mult, ALU.add))
                step(nc.vector.tensor_scalar(k, k, big, None, ALU.subtract))
                for part in TWO_PI:
                    step(nc.vector.scalar_tensor_tensor(ang, k, -part, ang, ALU.mult, ALU.add))
                step(nc.vector.tensor_scalar(shifted, ang, np.pi / 2, None, ALU.add))
                step(nc.vector.tensor_scalar(k, shifted, np.pi, -2 * np.pi, ALU.is_gt, ALU.mult))
                step(nc.vector.tensor_tensor(shifted, shifted, k, ALU.add))
                step(nc.vector.tensor_scalar(shifted, shifted, PI_IN, -PI_IN, ALU.min, ALU.max))
                nc.vector.tensor_scalar(ang, ang, PI_IN, -PI_IN, ALU.min, ALU.max).then_inc(trig_arg, 1)

            def score_unit(u, scale, near, far, negsink=None):
                b = u % 2
                if u >= 2:
                    dve.wait_ge(turned, seen.next(turned))
                dve.wait_ge(scores_done, seen.next(scores_done))
                nc.vector.scalar_tensor_tensor(S[b][:, 0:256], acc[b][:, 0:256], scale, far, ALU.mult, ALU.add)
                nc.vector.scalar_tensor_tensor(S[b][:, 256:384], acc[b][:, 256:384], scale, near, ALU.mult,
                                               ALU.add).then_inc(s_ready, 1)
                dve.wait_ge(s_ready, seen.next(s_ready))
                nc.vector.tensor_reduce(nmax[b][:, 1:2], S[b][:, 0:256], AX.X, ALU.max, negate=True)
                last = nc.vector.tensor_reduce(nmax[b][:, 0:1], S[b][:, 256:384], AX.X, ALU.max, negate=True)
                if negsink is not None:
                    step(last)
                    last = nc.vector.tensor_scalar(nmax[b][:], nmax[b][:], negsink, None, ALU.min)
                last.then_inc(nmax_ready, 1)

            def row_factors(u, sink=False, gates=None, factor=None):
                b = u % 2
                dve.wait_ge(exp_ready, seen.next(exp_ready))
                if sink:
                    step(nc.vector.tensor_tensor(esum[b][:], esum[b][:], esink[b][:], ALU.add))
                step(nc.vector.reciprocal(rsum[b][:], esum[b][:]))
                if gates is not None:
                    step(nc.vector.tensor_tensor(rsum[b][:], rsum[b][:], gates, ALU.mult))
                if factor is not None:
                    step(nc.vector.tensor_scalar(rsum[b][:], rsum[b][:], factor, None, ALU.mult))

            def norm_unit(u, **how):
                b = u % 2
                row_factors(u, **how)
                nc.vector.tensor_scalar(S[b][:, 0:256], S[b][:, 0:256], rsum[b][:, 1:2], None, ALU.mult)
                nc.vector.tensor_scalar(S[b][:, 256:384], S[b][:, 256:384], rsum[b][:, 0:1], None,
                                        ALU.mult).then_inc(p_ready, 1)

            def rope(dst, src, w):
                def table(v):
                    if w is None:
                        return v
                    return v.rearrange("p t (o f) -> p t o f", o=1).broadcast_to([P, NT, w, 16])
                c, sn = table(cos[:]), table(sin[:])
                n = NT * (w or 1)
                tmp = [rtmp[:, i, 0:n, :] for i in range(4)]
                if w is not None:
                    tmp = [v.rearrange("p (t h) f -> p t h f", t=NT) for v in tmp]
                a1, a2 = src[..., 0:16], src[..., 16:32]
                nc.vector.tensor_tensor(tmp[0], a1, c, ALU.mult)
                nc.vector.tensor_tensor(tmp[1], a2, sn, ALU.mult)
                nc.vector.tensor_tensor(tmp[2], a2, c, ALU.mult)
                step(nc.vector.tensor_tensor(tmp[3], a1, sn, ALU.mult))
                nc.vector.tensor_tensor(dst[..., 0:16], tmp[0], tmp[1], ALU.subtract)
                step(nc.vector.tensor_tensor(dst[..., 16:32], tmp[2], tmp[3], ALU.add))

            def mla(s, n0, bank0):
                consumed(n0)
                consumed(n0 + 1)
                for t in range(NT):
                    last = nc.vector.tensor_copy(latent[:, t, :], up[(bank0 + t) % 4][:, 0:QL + KVL + ROPE])
                step(last)
                dve.sem_inc(bank_free, NT)
                for t in range(NT):
                    nc.vector.tensor_tensor_reduce(cn[:, t, 0:QL], latent[:, t, 0:QL], latent[:, t, 0:QL], 1.0, 0.0,
                                                   ALU.mult, ALU.add, ssh[:, t:t + 1])
                    last = nc.vector.tensor_tensor_reduce(cn[:, t, QL:QL + KVL], latent[:, t, QL:QL + KVL],
                                                          latent[:, t, QL:QL + KVL], QL / KVL, 0.0,
                                                          ALU.mult, ALU.add, ssh[:, 2 + t:3 + t])
                step(last)
                rsqrt(rsh[:, 0:4], ssh[:, 0:4], 1.0 / QL, 4)
                for t in range(NT):
                    nc.vector.tensor_scalar(cn[:, t, 0:QL], latent[:, t, 0:QL], rsh[:, t:t + 1], None, ALU.mult)
                    nc.vector.tensor_scalar(cn[:, t, QL:], latent[:, t, QL:QL + KVL], rsh[:, 2 + t:3 + t], None,
                                            ALU.mult).then_inc(cn_ready, 1)
                parts_lo(3, G_MISC)
                pe_in = latent[:, :, QL + KVL:]
                nc.vector.tensor_tensor(rtmp[:, 0, 0:2, :].rearrange("p a b -> p (a b)"), pe_in[:, 0, :],
                                        pe_in[:, 0, :], ALU.mult)
                step(nc.vector.tensor_tensor(rtmp[:, 0, 2:4, :].rearrange("p a b -> p (a b)"), pe_in[:, 1, :],
                                             pe_in[:, 1, :], ALU.mult))
                step(nc.vector.tensor_reduce(ss[:, 4:6], rtmp[:, 0, 0:4, :].rearrange("p (t a) b -> p t (a b)", t=NT),
                                             AX.X, ALU.add))
                for t in range(NT):
                    last = nc.vector.tensor_tensor(kpe[:, t, :], pe_in[:, t, :], g96[:, 1, NOPE:], ALU.mult)
                step(last)
                rope(kpe, kpe, None)
                for i, (tile, groups) in enumerate(((n0 + 2, (0, 1)), (n0 + 3, (2,)))):
                    consumed(tile)
                    for g in groups:
                        for t in range(NT):
                            last = nc.vector.tensor_copy(arena[:, 1536 * t + 512 * g:1536 * t + 512 * g + 512],
                                                         up[(bank0 + 2 + 2 * g + t) % 4][:])
                    step(last)
                    dve.sem_inc(bank_free, NT * len(groups))
                dve.wait_ge(kv_copied, seen.next(kv_copied, 2))
                dve.sem_inc(bank_free, 4)
                consumed(n0 + 4)

                def flat(v):
                    return v.rearrange("p t h d -> p (t h) d")

                def over(v, n):
                    return v.rearrange("p (a o) -> p a o", o=1).broadcast_to([P, NT * MH, n])

                def gain(v, n):
                    return v.rearrange("p (o d) -> p o d", o=1).broadcast_to([P, NT * MH, n])

                step(nc.vector.tensor_tensor(squares, Q, Q, ALU.mult))
                step(nc.vector.tensor_reduce(ssh[:, 0:32], flat(squares), AX.X, ALU.add))
                dve.wait_ge(kv_copied, seen.next(kv_copied, 2))
                dve.sem_inc(bank_free, 4)
                kn = KV[:, :, :, 0:NOPE]
                step(nc.vector.tensor_tensor(squares[:, :, :, 0:NOPE], kn, kn, ALU.mult))
                step(nc.vector.tensor_reduce(ssh[:, 32:64], flat(squares)[:, :, 0:NOPE], AX.X, ALU.add))
                for t in range(NT):
                    last = nc.vector.tensor_scalar(ssh[:, 32 + MH * t:48 + MH * t], ssh[:, 32 + MH * t:48 + MH * t],
                                                   ss[:, 4 + t:5 + t], None, ALU.add)
                step(last)
                rsqrt(rsh[:], ssh[:], 1.0 / QKH, 64)
                nc.vector.tensor_tensor(flat(Q), flat(Q), over(rsh[:, 0:32], QKH), ALU.mult)
                nc.vector.tensor_tensor(flat(KF)[:, :, 0:NOPE], flat(KV)[:, :, 0:NOPE], over(rsh[:, 32:64], NOPE), ALU.mult)
                for t in range(NT):
                    last = nc.vector.tensor_tensor(
                        KF[:, t, :, NOPE:], kpe[:, t, :].rearrange("p (o d) -> p o d", o=1).broadcast_to([P, MH, ROPE]),
                        rsh[:, 32 + MH * t:48 + MH * t].rearrange("p (h o) -> p h o", o=1).broadcast_to([P, MH, ROPE]),
                        ALU.mult)
                step(last)
                nc.vector.tensor_tensor(flat(KF)[:, :, 0:NOPE], flat(KF)[:, :, 0:NOPE], gain(g96[:, 1, 0:NOPE], NOPE),
                                        ALU.mult)
                step(nc.vector.tensor_tensor(flat(Q), flat(Q), gain(g96[:, 0, :], QKH), ALU.mult))
                rope(Q[:, :, :, NOPE:], Q[:, :, :, NOPE:], MH)
                dve.sem_inc(qk_ready, 1)
                scale = float(QKH) ** -0.5
                far, near = consts[:, C_CAUSAL:C_CAUSAL + 256], consts[:, C_CAUSAL + 128:C_CAUSAL + 256]

                def o_lo(j):
                    dve.wait_ge(ohi_ready, seen.next(ohi_ready))
                    nc.vector.tensor_tensor(xT_lo[:, j, :], up[2 + j % 2][:, 0:TOK],
                                            xT_hi[:, j, :].bitcast(F32), ALU.subtract).then_inc(olo_ready, 1)
                    dve.wait_ge(olo_ready, seen.next(olo_ready))

                for i in range(MH + 3):
                    if i < MH:
                        score_unit(i, scale, near, far)
                    if 0 <= i - 1 < MH:
                        norm_unit(i - 1)
                    if 0 <= i - 3 < MH and (i - 3) % 2:
                        o_lo((i - 3) // 2)
                dve.wait_ge(turned, seen.next(turned, 2))
                for j in range(4):
                    consumed(n0 + 5 + j)
                residual(1.0)

            def sg(s, n0, bank0):
                for h in range(2):
                    dve.wait_ge(ws_turned, seen.next(ws_turned))
                    last = nc.vector.tensor_tensor(
                        wsT[:, 4 * h:4 * h + 4, :], acc[h][:].rearrange("p (g t) -> p g t", g=4),
                        consts[:, C_LOWT:C_LOWT + P].rearrange("p (o t) -> p o t", o=1).broadcast_to([P, 4, P]),
                        ALU.mult)
                last.then_inc(ws_ready, 1)
                for g in range(2):
                    consumed(n0 + 2 * g)
                    consumed(n0 + 2 * g + 1)
                    dve.wait_ge(v_ready, seen.next(v_ready))
                    dve.sem_inc(bank_free, NT)
                    for t in range(NT):
                        last = nc.vector.tensor_tensor_reduce(prod[:], xn[:, t, 512 * g:512 * g + 512],
                                                              xn[:, t, 512 * g:512 * g + 512], 1.0, 0.0, ALU.mult,
                                                              ALU.add, ssh[:, 2 * g + t:2 * g + t + 1])
                        step(last)
                step(nc.vector.tensor_tensor(ssh[:, 0:2], ssh[:, 0:2], ssh[:, 2:4], ALU.add))
                rsqrt(rsh[:, 0:2], ssh[:, 0:2], 1.0 / D, 2)
                for t in range(NT):
                    last = nc.vector.tensor_scalar(xn[:, t, :], xn[:, t, :], rsh[:, t:t + 1], None, ALU.mult)
                last.then_inc(vn_ready, 1)
                for c in range(4):
                    n = n0 + 4 + 2 * c - (c > 0)
                    consumed(n)
                    dve.wait_ge(mix_done, seen.next(mix_done))
                    dve.wait_ge(gate_ready, seen.next(gate_ready))
                    ps = up[(bank0 + 5 + 2 * c) % 4]
                    for m in range(2):
                        g = 2 * c + m
                        for t in range(NT):
                            last = nc.vector.scalar_tensor_tensor(
                                mixed[:, m, t * P:(t + 1) * P], ps[:, m * TOK + t * P:m * TOK + (t + 1) * P],
                                gains[:, g, G_SGV:G_SGV + 1], sgb[:, g * P:(g + 1) * P], ALU.mult, ALU.add)
                    step(last)
                    dve.sem_inc(bank_free, 2)
                    nc.vector.tensor_tensor(prod[:], gate[:], mixed.rearrange("p m t -> p (m t)"),
                                            ALU.mult).then_inc(prod_ready, 1)
                    dve.wait_ge(prod_ready, seen.next(prod_ready))
                    product_parts(c)
                    if c:
                        consumed(n + 1)
                consumed(n0 + 11)
                residual(1.0)

            def tables():
                nc.vector.memset(relb, NEG).then_inc(arena_free, 1)
                dve.wait_ge(tables_in, seen.next(tables_in, 16 * 7))
                for i in range(2):
                    for j in range(2):
                        last = nc.vector.tensor_tensor_reduce(nwt[:], lp[:, i, 2 * j, :], lp[:, i, 2 * j + 1, :], 1.0, 0.0,
                                                              ALU.mult, ALU.add, ssh[:, 2 * i + j:2 * i + j + 1])
                        step(last)
                    step(nc.vector.tensor_scalar(subln[:, i:i + 1], gains[:, 3 + i, G_MISC:G_MISC + 1],
                                                 1.0 - LAM_INIT[i], None, ALU.mult))
                nc.vector.tensor_scalar(negsinks[:], sinks[:], -1.0, None, ALU.mult).then_inc(tab_dve, 1)
                dve.wait_ge(tab_dve, seen.next(tab_dve))
                dve.wait_ge(tab_pe, seen.next(tab_pe))
                nc.vector.tensor_copy(rv[0:12, 0, :], acc[0][0:12, 0:384])
                nc.vector.tensor_copy(rv[0:8, 1, :], acc[1][0:8, 0:384]).then_inc(rv_ready, 1)
                nc.vector.tensor_copy(pos2[:].rearrange("p i v j -> p (i v j)"), acc[2][:, 0:64])
                step(nc.vector.tensor_copy(TC, acc[3][:, 0:240].rearrange("p (n h) -> p h n", h=8)))
                dve.sem_inc(tab_dve, 1)
                dve.wait_ge(tab_dve, seen.next(tab_dve))
                dve.wait_ge(tab_act, seen.next(tab_act))
                for i in range(2):
                    step(nc.vector.tensor_tensor(neglam[:, i:i + 1], ssh[:, 5 + 2 * i:6 + 2 * i], ssh[:, 4 + 2 * i:5 + 2 * i],
                                                 ALU.subtract))
                    step(nc.vector.tensor_scalar(neglam[:, i:i + 1], neglam[:, i:i + 1], -LAM_INIT[i], None, ALU.add))
                for g in range(10):
                    dve.wait_ge(tab_pe, seen.next(tab_pe))
                    nc.vector.tensor_copy(T[:, 2 * g:2 * g + 2, :].rearrange("p h j -> p (h j)"),
                                          acc[g % 4][:]).then_inc(tab_dve, 1)
                    dve.wait_ge(tab_dve, seen.next(tab_dve))

            def mix(s, n0, bank0):
                n = n0
                bank = [bank0]

                def out(dst):
                    step(nc.vector.tensor_copy(dst, up[bank[0] % 4][:]))
                    bank[0] += 1
                    dve.sem_inc(bank_free, 1)

                def flat(v):
                    return v.rearrange("p k n -> p (k n)")

                consumed(n)
                out(flat(KC))
                dve.sem_inc(kc_ready, 1)
                for j, dst in enumerate((AQ, AQ, AK, AK)):
                    consumed(n + 1 + j)
                    out(flat(dst[:, 2 * (j % 2):2 * (j % 2) + 2, :]))
                consumed(n + 5)
                consumed(n + 6)
                for t in range(NT):
                    out(AV[:, t, :])
                dve.wait_ge(kc2_in, seen.next(kc2_in, 16 * 8))
                for v in range(2):
                    for j in range(16):
                        last = nc.vector.tensor_scalar(
                            blk[:, v, j, :].rearrange("p (g b) -> p g b", g=2),
                            KC2[:, v, :, 2 * j:2 * j + 16 * (NCMP - 1) + 1:16], pos2[:, s[1], v, j:j + 1], None, ALU.add)
                    last.then_inc(blk_ready, 1)
                    dve.wait_ge(blkhi_ready, seen.next(blkhi_ready))
                    nc.vector.tensor_tensor(blk_lo[:, v], blk[:, v], blk_hi[:, v].bitcast(F32),
                                            ALU.subtract).then_inc(blklo_ready, 1)
                n += 7
                for j in range(2):
                    consumed(n + j)
                    out(flat(BQ[:, 2 * j:2 * j + 2, :]))
                consumed(n + 2)
                out(BS)
                consumed(n + 3)
                out(BW)
                consumed(n + 4)
                dve.wait_ge(gates_ready, seen.next(gates_ready))
                bank[0] += 1
                dve.sem_inc(bank_free, 1)
                n += 5
                for v in range(2):
                    consumed(n)
                    consumed(n + 1)
                    n += 2
                    dve.wait_ge(hid_ready, seen.next(hid_ready))
                    bank[0] += 2
                    dve.sem_inc(bank_free, 2)
                dve.wait_ge(cmp_done, seen.next(cmp_done))
                nc.vector.tensor_copy(kcT, up[bank[0] % 4][:, 0:2 * NCMP])
                bank[0] += 1
                step(nc.vector.tensor_copy(vc, up[bank[0] % 4][0:NCMP, 0:128]))
                bank[0] += 1
                dve.sem_inc(bank_free, 2)
                for j in range(2):
                    consumed(n + j)
                    out(flat(CQ[:, 2 * j:2 * j + 2, :]))
                consumed(n + 2)
                out(CKV)
                n += 3
                dve.sem_inc(proj_ready, 1)
                scale = 0.125
                for br in range(3):
                    units = branch_units(br)
                    for i in range(len(units) + 3):
                        if i < len(units):
                            kind, h = units[i][:2]
                            if kind == "cmp":
                                score_cmp(i, scale, TC[:, h, :])
                            else:
                                tab = T[:, (0, 4, 12)[br] + h, :]
                                at = 8 * s[1] + h
                                score_unit(i, scale, tab[:, 128:256], tab, negsinks[:, at:at + 1] if br == 2 else None)
                        if 0 <= i - 1 < len(units):
                            kind, h = units[i - 1][:2]
                            if br == 0:
                                norm_unit(i - 1, factor=neglam[:, s[1]:s[1] + 1] if kind == 1 else None)
                            elif br == 2:
                                norm_unit(i - 1, sink=True)
                            else:
                                col = 3 * h + ("cmp", "sel", "win").index(kind)
                                gates = gB[:, :, col]
                                if kind == "cmp":
                                    norm_cmp(i - 1, gates)
                                else:
                                    norm_unit(i - 1, gates=gates)
                        if 0 <= i - 3 < len(units) and units[i - 3][2]:
                            h = units[i - 3][1]
                            if br == 0:
                                dve.wait_ge(oa_done, seen.next(oa_done))
                                for t in range(NT):
                                    last = nc.vector.tensor_copy(YA[:, t, P * h:P * h + P], up[2 * (h % 2) + t][:, 0:P])
                                last.then_inc(ya_copied, 1)
                                dve.wait_ge(ya_copied, seen.next(ya_copied))
                            else:
                                j = h // 2
                                dve.wait_ge(ohi_ready, seen.next(ohi_ready))
                                nc.vector.tensor_tensor(yT_lo[:, j, :], up[2 + j % 2][:, 0:TOK],
                                                        yT_hi[:, j, :].bitcast(F32), ALU.subtract).then_inc(olo_ready, 1)
                    dve.wait_ge(turned, seen.next(turned, 2))
                    if br == 0:
                        ya = YA.rearrange("p t (h e) -> p (t h) e", h=4)
                        sq = carve(5376, 8, P)
                        step(nc.vector.tensor_tensor(sq, ya, ya, ALU.mult))
                        step(nc.vector.tensor_reduce(ssh[:, 0:8], sq, AX.X, ALU.add))
                        rsqrt(rsh[:, 0:8], ssh[:, 0:8], 1.0 / P, 8)
                        step(nc.vector.tensor_tensor(ya, ya, rsh[:, 0:8].rearrange("p (a o) -> p a o", o=1)
                                                     .broadcast_to([P, 8, P]), ALU.mult))
                        dve.sem_inc(ya_ready, NT)
                        parts_lo(4, 0, yT_lo, yT_hi, subln[:, s[1]:s[1] + 1])
                    for c in range(2):
                        b = bank0 + 21 + 8 * br + 4 * c
                        for j in range(2):
                            consumed(n)
                            n += 1
                            dve.wait_ge(gate_ready, seen.next(gate_ready))
                            dve.sem_inc(bank_free, 1)
                        consumed(n)
                        n += 1
                        for j, g in enumerate((gate, prod)):
                            dst = flat(merged[:, 4 * c + 2 * j:4 * c + 2 * j + 2, :])
                            ps = up[(b + 2 + j) % 4][:]
                            if br == 0:
                                step(nc.vector.tensor_tensor(dst, g[:], ps, ALU.mult))
                            else:
                                step(nc.vector.tensor_tensor(g[:], g[:], ps, ALU.mult))
                            dve.sem_inc(bank_free, 1)
                            if br:
                                step(nc.vector.tensor_tensor(dst, dst, g[:], ALU.add))
                        dve.sem_inc(merge_step, 1)
                for j in range(4):
                    if j >= 2:
                        consumed(n)
                        n += 1
                    dve.wait_ge(mhi_ready, seen.next(mhi_ready))
                    nc.vector.tensor_tensor(hT_lo[:, j % 2], merged[:, 2 * j:2 * j + 2, :], hT_hi[:, j % 2].bitcast(F32),
                                            ALU.subtract).then_inc(mlo_ready, 1)
                consumed(n)
                consumed(n + 1)
                residual(1.0)

            def score_cmp(u, scale, tab):
                b = u % 2
                if u >= 2:
                    dve.wait_ge(turned, seen.next(turned))
                dve.wait_ge(scores_done, seen.next(scores_done))
                nc.vector.scalar_tensor_tensor(S[b][:, 0:2 * NCMP], acc[b][:, 0:2 * NCMP], scale, tab, ALU.mult,
                                               ALU.add).then_inc(s_ready, 1)
                dve.wait_ge(s_ready, seen.next(s_ready))
                nc.vector.tensor_reduce(nmax[b][:], S[b][:, 0:2 * NCMP].rearrange("p (t n) -> p t n", t=2), AX.X,
                                        ALU.max, negate=True).then_inc(nmax_ready, 1)

            def norm_cmp(u, gates):
                b = u % 2
                row_factors(u, gates=gates)
                for t in range(NT):
                    cols = slice(NCMP * t, NCMP * t + NCMP)
                    last = nc.vector.scalar_tensor_tensor(S[b][:, cols], S[b][:, cols], rsum[b][:, t:t + 1],
                                                          consts[:, C_CMPOK + NCMP * t:C_CMPOK + NCMP * t + NCMP],
                                                          ALU.mult, ALU.mult)
                last.then_inc(p_ready, 1)

            def ple(s, n0, bank0):
                dve.wait_ge(xhi_ready, seen.next(xhi_ready))
                nc.vector.tensor_tensor(hT_lo[:, 0], acc[0][:].rearrange("p (k n) -> p k n", k=2),
                                        hT_hi[:, 0].bitcast(F32), ALU.subtract).then_inc(xlo_ready, 1)
                for c in range(2):
                    consumed(n0 + 3 * c)
                    consumed(n0 + 3 * c + 1)
                    dve.wait_ge(gate_ready, seen.next(gate_ready))
                    dve.sem_inc(bank_free, 2)
                    consumed(n0 + 3 * c + 2)
                    for t, g in enumerate((gate, prod)):
                        step(nc.vector.tensor_tensor(g[:], g[:], up[(bank0 + 4 * c + 2 + t) % 4][:], ALU.mult))
                        dve.sem_inc(bank_free, 1)
                        cols = slice(512 * c, 512 * c + 512)
                        step(nc.vector.tensor_tensor(x[:, t, cols], x[:, t, cols], g[:], ALU.add))
                    dve.sem_inc(merge_step, 1)
                dve.sem_inc(x_ready, NT)
                dve.wait_ge(x_ready, seen.next(x_ready, NT))

            def final():
                dve.wait_ge(ss_ready, seen.next(ss_ready, NT))
                rsqrt(rstd[:, 0:NT], ss[:, 0:NT], 1.0 / D, NT)
                dve.wait_ge(fin_in, seen.next(fin_in, 16))
                for t in range(NT):
                    last = nc.vector.scalar_tensor_tensor(xn[:, t, :], x[:, t, :], rstd[:, t:t + 1], gfin, ALU.mult,
                                                          ALU.mult)
                last.then_inc(fin_ready, 1)

            dve.wait_ge(misc_in, seen.next(misc_in, 48))
            dve.wait_ge(const_in, seen.next(const_in, 32))
            trig_arguments()
            for n in range(RING):
                split_lo(n)
            dve.wait_ge(trig_done, seen.next(trig_done))
            dve.wait_ge(setup_pe, seen.next(setup_pe))
            nc.vector.tensor_copy(gains[:, :, 0:G_ROWS],
                                  up[3][:, 0:KD * G_ROWS].rearrange("p (k r) -> p k r", k=KD)).then_inc(setup_dve, 1)
            dve.wait_ge(setup_dve, seen.next(setup_dve))
            dve.sem_inc(x_ready, NT)
            dve.wait_ge(x_ready, seen.next(x_ready, NT))
            bank = 0
            for s, n0 in zip(plan, first):
                if s[0] == "norm":
                    norm(s[1])
                elif s[0] == "ffn":
                    ffn(s, n0, bank)
                    bank = (bank + 2 * NCH) % 4
                elif s[0] == "conv":
                    conv(s, n0, bank)
                    bank = (bank + 12) % 4
                elif s[0] == "mla":
                    mla(s, n0, bank)
                    bank = (bank + 16) % 4
                elif s[0] == "sg":
                    sg(s, n0, bank)
                    bank = (bank + 12) % 4
                elif s[0] == "tables":
                    tables()
                elif s[0] == "mix":
                    mix(s, n0, bank)
                    bank = (bank + MIX_BANKS) % 4
                elif s[0] == "ple":
                    ple(s, n0, bank)
                    bank = (bank + 8) % 4
                elif s[0] == "final":
                    final()

        @block.tensor
        def _(pe):
            seen = Seen()
            banks, credit = [0], [4]

            def matmul3(ps, lh, ll, rh, rl, start, stop):
                pe.matmul(ps, lh, rh, start=start, stop=False)
                pe.matmul(ps, lh, rl, start=False, stop=False)
                return pe.matmul(ps, ll, rh, start=False, stop=stop)

            def take_bank():
                if credit[0]:
                    credit[0] -= 1
                else:
                    pe.wait_ge(bank_free, seen.next(bank_free))
                banks[0] += 1
                return (banks[0] - 1) % 4

            def drain_banks():
                pe.wait_ge(bank_free, seen.next(bank_free, 4 - credit[0]))
                credit[0] = 4

            def up_matmuls(n, b):
                wh, wl = tview(w_hi[n % RING], KD, CW), tview(w_lo[n % RING], KD, CW)
                for m in range(2):
                    for k in range(KD):
                        last = matmul3(up[b][:, m * TOK:(m + 1) * TOK], wh[:, k, m * P:(m + 1) * P],
                                       wl[:, k, m * P:(m + 1) * P], xT_hi[:, k, :], xT_lo[:, k, :],
                                       k == 0, k == KD - 1)
                last.then_inc(tile_used, 1)

            def down_matmuls(n, lh, ll, start, stop):
                wh, wl = tview(w_hi[n % RING], 2, D), tview(w_lo[n % RING], 2, D)
                for t in range(NT):
                    for h in range(2):
                        for k in range(2):
                            cols = slice(512 * h, 512 * h + 512)
                            last = matmul3(acc[2 * t + h][:], lh[:, k, t * P:(t + 1) * P], ll[:, k, t * P:(t + 1) * P],
                                           wh[:, k, cols], wl[:, k, cols], start and k == 0, stop and k == 1)
                last.then_inc(tile_used, 1)

            def turn(src, nk, ready):
                for t in range(NT):
                    pe.wait_ge(ready, seen.next(ready))
                    for k in range(nk):
                        last = pe.transpose(acc[k // 2][:, (k % 2) * TOK + t * P:(k % 2) * TOK + (t + 1) * P],
                                            src[:, t, k * P:(k + 1) * P], ident)
                        if t == NT - 1 and (k % 2 or k == nk - 1):
                            last.then_inc(xT_ready, 1)

            def token_matmuls(n, nk, ncol, col, width, k0, ps, start, stop):
                wh, wl = tview(w_hi[n % RING], nk, ncol), tview(w_lo[n % RING], nk, ncol)
                for t in range(NT):
                    for k in range(nk):
                        last = matmul3(ps[t], xT_hi[:, k0 + k, t * P:(t + 1) * P], xT_lo[:, k0 + k, t * P:(t + 1) * P],
                                       wh[:, k, col:col + width], wl[:, k, col:col + width],
                                       start and k == 0, stop and k == nk - 1)
                return last

            def ups(n, wait=True):
                pe.wait_ge(lo_ready, seen.next(lo_ready))
                up_matmuls(n, take_bank())

            def down(n, c, start, stop):
                pe.wait_ge(lo_ready, seen.next(lo_ready))
                pe.wait_ge(hlo_ready, seen.next(hlo_ready))
                down_matmuls(n, hT_hi[:, c % 2], hT_lo[:, c % 2], start, stop)
                if stop:
                    pe.sem_inc(acc_done, 1)

            def conv(s, n0):
                pe.wait_ge(xlo_ready, seen.next(xlo_ready, KD // 2))
                n = n0
                for c in range(4):
                    for _ in range(3):
                        ups(n)
                        n += 1
                    if c:
                        down(n, c - 1, c == 1, False)
                        n += 1
                down(n, 3, False, True)

            def scores(u, q, k):
                if u >= 2:
                    pe.wait_ge(s_ready, seen.next(s_ready))
                ps = acc[u % 2]
                pe.matmul(ps[:, 0:256], q[:, P:TOK], k, start=True, stop=True)
                pe.matmul(ps[:, 256:384], q[:, 0:P], k[:, 0:P], start=True, stop=True).then_inc(scores_done, 1)

            def turn_unit(u):
                pe.wait_ge(p_ready, seen.next(p_ready))
                b, ps = u % 2, acc[2 + u % 2]
                pe.transpose(ps[:, 0:P], S[b][:, 256:384], ident)
                pe.transpose(ps[:, P:2 * P], S[b][:, 0:P], ident)
                pe.transpose(ps[:, 2 * P:3 * P], S[b][:, P:2 * P], ident).then_inc(turned, 1)

            def mla(s, n0):
                pe.wait_ge(xlo_ready, seen.next(xlo_ready, KD // 2))
                ps = [up[take_bank()][:, 0:QL + KVL + ROPE] for _ in range(NT)]
                for h in range(2):
                    pe.wait_ge(lo_ready, seen.next(lo_ready))
                    token_matmuls(n0 + h, 4, QL + KVL + ROPE, 0, QL + KVL + ROPE, 4 * h, ps, h == 0, h == 1
                                  ).then_inc(tile_used, 1)
                turn(cn, 3, cn_ready)
                pe.wait_ge(xlo_ready, seen.next(xlo_ready, 2))
                for tile, groups in ((n0 + 2, 2), (n0 + 3, 1)):
                    pe.wait_ge(lo_ready, seen.next(lo_ready))
                    for g in range(groups):
                        ps = [up[take_bank()][:] for _ in range(NT)]
                        last = token_matmuls(tile, 2, 512 * groups, 512 * g, 512, 0, ps, True, True)
                    last.then_inc(tile_used, 1)
                pe.wait_ge(lo_ready, seen.next(lo_ready))
                for g in range(4):
                    ps = [up[take_bank()][:] for _ in range(NT)]
                    last = token_matmuls(n0 + 4, 1, 2048, 512 * g, 512, 2, ps, True, True)
                    last.then_inc(group_done if g < 3 else tile_used, 1)
                pe.wait_ge(qk_ready, seen.next(qk_ready))
                drain_banks()
                def turn_head(h):
                    b = h % 2
                    for i, v in enumerate((Q, KF)):
                        for t in range(NT):
                            last = pe.transpose(up[b][0:QKH, i * TOK + t * P:i * TOK + (t + 1) * P], v[:, t, h, :], ident)
                    last.then_inc(headT_done, 1)

                def values(h):
                    if h % 2 == 0 and h >= 4:
                        pe.wait_ge(olo_ready, seen.next(olo_ready))
                    ps = up[2 + h // 2 % 2][64 * (h % 2):64 * (h % 2) + VH, 0:TOK]
                    pe.wait_ge(pt_ready, seen.next(pt_ready))
                    pe.matmul(ps, KV[:, 0, h, NOPE:], PT[h % 2][:, 0:256], start=True, stop=False)
                    last = pe.matmul(ps[:, P:TOK], KV[:, 1, h, NOPE:], PT[h % 2][:, 256:384], start=False, stop=True)
                    if h % 2:
                        last.then_inc(o_done, 1)

                for i in range(MH + 3):
                    if i < MH:
                        turn_head(i)
                        pe.wait_ge(headT_ready, seen.next(headT_ready))
                        scores(i, headT[i % 2][0:QKH, 0:TOK], headT[i % 2][0:QKH, TOK:2 * TOK])
                    if 0 <= i - 1 < MH:
                        turn_unit(i - 1)
                    if 0 <= i - 2 < MH:
                        values(i - 2)
                pe.wait_ge(s_ready, seen.next(s_ready, 2))
                pe.wait_ge(olo_ready, seen.next(olo_ready, 2))
                for j in range(4):
                    pe.wait_ge(lo_ready, seen.next(lo_ready))
                    down_matmuls(n0 + 5 + j, xT_hi[:, 2 * j:2 * j + 2], xT_lo[:, 2 * j:2 * j + 2], j == 0, j == 3)
                pe.sem_inc(acc_done, 1)

            def sg(s, n0):
                pe.wait_ge(ws_in, seen.next(ws_in, 32))
                pe.wait_ge(xlo_ready, seen.next(xlo_ready, KD // 2))
                for g in range(8):
                    last = pe.transpose(acc[g // 4][:, (g % 4) * P:(g % 4 + 1) * P], wsr[:, g, :], ident)
                    if g % 4 == 3:
                        last.then_inc(ws_turned, 1)
                for g in range(2):
                    ps = [up[take_bank()][:] for _ in range(NT)]
                    for h in range(2):
                        pe.wait_ge(lo_ready, seen.next(lo_ready))
                        token_matmuls(n0 + 2 * g + h, 4, 512, 0, 512, 4 * h, ps, h == 0, h == 1).then_inc(tile_used, 1)
                pe.wait_ge(ws_ready, seen.next(ws_ready))
                n = n0 + 4
                for c in range(4):
                    ups(n)
                    n += 1
                    if c == 0:
                        pe.wait_ge(vn_ready, seen.next(vn_ready))
                    b = take_bank()
                    for m in range(2):
                        g = 2 * c + m
                        for t in range(NT):
                            last = pe.matmul(up[b][:, m * TOK + t * P:m * TOK + (t + 1) * P],
                                             xn[:, t, g * P:(g + 1) * P], wsT[:, g, :], start=True, stop=True)
                    last.then_inc(mix_done, 1)
                    if c:
                        down(n, c - 1, c == 1, False)
                        n += 1
                down(n, 3, False, True)

            def ffn(s, n0):
                def gate_up(n, c, b, loop=False):
                    for j in range(2):
                        pe.wait_ge(lo_ready, seen.next(lo_ready))
                        if loop:
                            pe.wait_ge(bank_free, seen.next(bank_free))
                        else:
                            assert take_bank() == (b + j) % 4
                        up_matmuls(n + j, (b + j) % 4)

                b = banks[0] % 4
                pe.wait_ge(xlo_ready, seen.next(xlo_ready, KD // 2))
                gate_up(n0, 0, b)
                gate_up(n0 + 2, 1, b + 2)
                down(n0 + 4, 0, True, False)
                with pe.Fori(0, 4) as i:
                    seen.enter(i, [(lo_ready, 6), (bank_free, 4), (hlo_ready, 2)])
                    gate_up(n0 + 5, 2, b, True)
                    down(n0 + 7, 1, False, False)
                    gate_up(n0 + 8, 3, b + 2, True)
                    down(n0 + 10, 2, False, False)
                    seen.leave(4)
                banks[0] += 16
                gate_up(n0 + 29, 10, b)
                down(n0 + 31, 9, False, False)
                down(n0 + 32, 10, False, True)

            def tables():
                pe.wait_ge(tables_in, seen.next(tables_in, 16 * 7))
                pe.wait_ge(tab_dve, seen.next(tab_dve))
                pe.matmul(acc[0][0:12, 0:384], relb[:, 0:12], consts[0:33, C_OHREV:C_OHREV + 384], start=True, stop=True)
                pe.matmul(acc[1][0:8, 0:384], relb[:, 12:20], consts[0:33, C_OHREV + 384:C_OHREV + 768], start=True,
                          stop=True)
                pe.transpose(acc[2][:, 0:64], prows, ident[0:64, 0:64])
                for t in range(NT):
                    for b in range(NCMP):
                        at = C_OHF + 256 + P * t - 16 * b - 31
                        i = NCMP * t + b
                        last = pe.matmul(acc[3][:, 8 * i:8 * i + 8], consts[0:33, at:at + P], relb[:, 4:12], start=True,
                                         stop=True)
                last.then_inc(tab_pe, 1)
                pe.wait_ge(u_in, seen.next(u_in, 16))
                pe.wait_ge(tab_dve, seen.next(tab_dve))
                for g in range(10):
                    if g >= 4:
                        pe.wait_ge(tab_dve, seen.next(tab_dve))
                    pe.matmul(acc[g % 4][:], consts[:, C_FLIP:C_FLIP + P],
                              U[:, 2 * g:2 * g + 2, :].rearrange("p h j -> p (h j)"), start=True,
                              stop=True).then_inc(tab_pe, 1)
                pe.wait_ge(tab_dve, seen.next(tab_dve, 4))

            def mix(s, n0):
                pe.wait_ge(xlo_ready, seen.next(xlo_ready, KD // 2))
                n = n0
                for _ in range(5):
                    ups(n)
                    n += 1
                ps = [up[take_bank()][:] for _ in range(NT)]
                for h in range(2):
                    pe.wait_ge(lo_ready, seen.next(lo_ready))
                    token_matmuls(n, 4, 512, 0, 512, 4 * h, ps, h == 0, h == 1).then_inc(tile_used, 1)
                    n += 1
                ups(n)
                ups(n + 1)
                n += 2

                def key_value(n):
                    pe.wait_ge(lo_ready, seen.next(lo_ready))
                    ps = up[take_bank()]
                    wh, wl = tview(w_hi[n % RING], KD, CW), tview(w_lo[n % RING], KD, CW)
                    for k in range(KD):
                        matmul3(ps[:, 0:TOK], wh[:, k, 0:P], wl[:, k, 0:P], xT_hi[:, k, :], xT_lo[:, k, :],
                                k == 0, k == KD - 1)
                    token_matmuls(n, KD, CW, P, P, 0, [ps[:, TOK:TOK + P], ps[:, TOK + P:2 * TOK]], True, True
                                  ).then_inc(tile_used, 1)

                key_value(n)
                key_value(n + 1)
                n += 2
                pe.wait_ge(lo_ready, seen.next(lo_ready))
                ps = up[take_bank()]
                token_matmuls(n, KD, 24, 0, 24, 0, [ps[:, 0:24], ps[:, 24:48]], True, True).then_inc(tile_used, 1)
                n += 1
                for v in range(2):
                    pe.wait_ge(blklo_ready, seen.next(blklo_ready))
                    banks2 = [up[take_bank()] for _ in range(2)]
                    for h in range(2):
                        pe.wait_ge(lo_ready, seen.next(lo_ready))
                        wh, wl = tview(w_hi[n % RING], KD, CW), tview(w_lo[n % RING], KD, CW)
                        for m in range(2):
                            for k in range(KD):
                                last = matmul3(banks2[m][:, 0:2 * NCMP], wh[:, k, m * P:(m + 1) * P],
                                               wl[:, k, m * P:(m + 1) * P], blk_hi[:, v, 8 * h + k, :],
                                               blk_lo[:, v, 8 * h + k, :], h == 0 and k == 0, h == 1 and k == KD - 1)
                        last.then_inc(tile_used, 1)
                        n += 1
                pe.wait_ge(hid_ready, seen.next(hid_ready, 2))
                if s[1] == 0:
                    pe.wait_ge(w2_in, seen.next(w2_in, 64))
                kb, vb = up[take_bank()], up[take_bank()]
                for base in (0, 64):
                    for m in range(2):
                        pe.matmul(kb[base:base + 64, 0:2 * NCMP], w2[:, s[1], 0, m, :], hidT[:, 0, m, :], start=m == 0,
                                  stop=m == 1)
                for g in range(2):
                    for m in range(2):
                        last = pe.matmul(vb[0:NCMP, 64 * g:64 * g + 64], hidT[:, 1, m, NCMP * g:NCMP * g + NCMP],
                                         w2[:, s[1], 1, m, :], start=m == 0, stop=m == 1)
                last.then_inc(cmp_done, 1)
                ups(n)
                ups(n + 1)
                key_value(n + 2)
                n += 3
                pe.wait_ge(proj_ready, seen.next(proj_ready))

                def operands(br, kind, h):
                    g, r = h // 4, h % 4
                    rows = slice(64 * g, 64 * g + 64)
                    if br == 0:
                        rows = slice(64 * kind, 64 * kind + 64)
                        return AQ[rows, h, :], AK[rows, h, :]
                    if br == 2:
                        return CQ[rows, r, :], CKV[rows, 0:TOK]
                    q = BQ[rows, r, :]
                    if kind == "cmp":
                        return q, kcT[rows, NCMP * g:NCMP * g + NCMP]
                    return q, (BS if kind == "sel" else BW)[rows, 0:TOK]

                def values_a(u, c, h):
                    pe.wait_ge(pt_ready, seen.next(pt_ready))
                    if c == 0 and h >= 2:
                        pe.wait_ge(ya_copied, seen.next(ya_copied))
                    o = [up[2 * (h % 2) + t][:, 0:P] for t in range(NT)]
                    cols = slice(P * h, P * h + P)
                    pe.matmul(o[0], PT[u % 2][:, 0:P], AV[:, 0, cols], start=c == 0, stop=c == 1)
                    pe.matmul(o[1], PT[u % 2][:, P:2 * P], AV[:, 0, cols], start=c == 0, stop=False)
                    last = pe.matmul(o[1], PT[u % 2][:, 2 * P:3 * P], AV[:, 1, cols], start=False, stop=c == 1)
                    if c == 1:
                        last.then_inc(oa_done, 1)

                def values_bc(u, br, kind, h, ends):
                    pe.wait_ge(pt_ready, seen.next(pt_ready))
                    starts = kind == "sel" or br == 2
                    stops = kind == "cmp" or br == 2
                    if starts and h % 2 == 0 and h >= 4:
                        pe.wait_ge(olo_ready, seen.next(olo_ready))
                    g = h // 4
                    o = up[2 + h // 2 % 2][64 * (h % 2):64 * (h % 2) + 64, 0:TOK]
                    cols = slice(TOK + 64 * g, TOK + 64 * g + 64)
                    cols1 = slice(TOK + P + 64 * g, TOK + P + 64 * g + 64)
                    if kind == "cmp":
                        last = pe.matmul(o, vc[:, 64 * g:64 * g + 64], PT[u % 2][0:NCMP, 0:TOK], start=False, stop=True)
                    else:
                        kv = CKV if br == 2 else BS if kind == "sel" else BW
                        pe.matmul(o, kv[:, cols], PT[u % 2][:, 0:TOK], start=starts, stop=False)
                        last = pe.matmul(o[:, P:TOK], kv[:, cols1], PT[u % 2][:, TOK:384], start=False, stop=stops)
                    if ends:
                        last.then_inc(o_done, 1)

                for br in range(3):
                    drain_banks()
                    units = branch_units(br)
                    nu = len(units)
                    for i in range(nu + 2):
                        if i < nu:
                            kind, h = units[i][:2]
                            q, k = operands(br, kind, h)
                            if kind == "cmp":
                                scores_cmp(i, q, k)
                            else:
                                scores(i, q, k)
                        if 0 <= i - 1 < nu:
                            if units[i - 1][0] == "cmp":
                                turn_cmp(i - 1)
                            else:
                                turn_unit(i - 1)
                        if 0 <= i - 2 < nu:
                            kind, h, ends = units[i - 2]
                            if br == 0:
                                values_a(i - 2, kind, h)
                            else:
                                values_bc(i - 2, br, kind, h, ends)
                    pe.wait_ge(s_ready, seen.next(s_ready, 2))
                    if br == 0:
                        pe.wait_ge(ya_copied, seen.next(ya_copied, 2))
                        turn(YA, 4, ya_ready)
                        pe.wait_ge(xlo_ready, seen.next(xlo_ready, 2))
                    else:
                        pe.wait_ge(olo_ready, seen.next(olo_ready, 2))
                    for c in range(2):
                        for _ in range(2):
                            ups(n)
                            n += 1
                        pe.wait_ge(lo_ready, seen.next(lo_ready))
                        wh, wl = tview(w_hi[n % RING], 4, 512), tview(w_lo[n % RING], 4, 512)
                        for j in range(2):
                            b = take_bank()
                            for m in range(2):
                                cols = slice(CW * j + P * m, CW * j + P * m + P)
                                for k in range(4):
                                    last = matmul3(up[b][:, m * TOK:(m + 1) * TOK], wh[:, k, cols], wl[:, k, cols],
                                                   yT_hi[:, k, :], yT_lo[:, k, :], k == 0, k == 3)
                        last.then_inc(tile_used, 1)
                        n += 1
                for j in range(4):
                    pe.wait_ge(lo_ready, seen.next(lo_ready))
                    pe.wait_ge(mlo_ready, seen.next(mlo_ready))
                    down_matmuls(n, hT_hi[:, j % 2], hT_lo[:, j % 2], j == 0, j == 3)
                    n += 1
                pe.sem_inc(acc_done, 1)

            def scores_cmp(u, q, k):
                if u >= 2:
                    pe.wait_ge(s_ready, seen.next(s_ready))
                for t in range(NT):
                    last = pe.matmul(acc[u % 2][:, NCMP * t:NCMP * t + NCMP], q[:, P * t:P * t + P], k, start=True,
                                     stop=True)
                last.then_inc(scores_done, 1)

            def turn_cmp(u):
                pe.wait_ge(p_ready, seen.next(p_ready))
                for t in range(NT):
                    last = pe.transpose(acc[2 + u % 2][0:NCMP, P * t:P * t + P], S[u % 2][:, NCMP * t:NCMP * t + NCMP],
                                        ident)
                last.then_inc(turned, 1)

            def ple(s, n0):
                pe.wait_ge(xlo_ready, seen.next(xlo_ready, KD // 2))
                pe.wait_ge(ple_arrived, seen.next(ple_arrived, 16))
                for t in range(NT):
                    for k in range(2):
                        last = pe.transpose(acc[0][:, k * TOK + t * P:k * TOK + (t + 1) * P],
                                            ple_in[:, t, k * P:(k + 1) * P], ident)
                last.then_inc(xT_ready, 1)
                n = n0
                for c in range(2):
                    ps = [up[take_bank()][:] for _ in range(NT)]
                    for h in range(2):
                        pe.wait_ge(lo_ready, seen.next(lo_ready))
                        token_matmuls(n, 4, 512, 0, 512, 4 * h, ps, h == 0, h == 1).then_inc(tile_used, 1)
                        n += 1
                    ps = [up[take_bank()][:] for _ in range(NT)]
                    pe.wait_ge(lo_ready, seen.next(lo_ready))
                    if c == 0:
                        pe.wait_ge(xlo_ready, seen.next(xlo_ready))
                    wh, wl = tview(w_hi[n % RING], 2, 512), tview(w_lo[n % RING], 2, 512)
                    for t in range(NT):
                        for k in range(2):
                            tok = slice(t * P, (t + 1) * P)
                            last = matmul3(ps[t], hT_hi[:, 0, k, tok], hT_lo[:, 0, k, tok], wh[:, k, :], wl[:, k, :],
                                           k == 0, k == 1)
                    last.then_inc(tile_used, 1)
                    n += 1

            pe.wait_ge(const_in, seen.next(const_in, 32))
            pe.wait_ge(gain_in, seen.next(gain_in, 112))
            for k in range(KD):
                last = pe.transpose(up[3][:, k * G_ROWS:(k + 1) * G_ROWS], g_rows[:, k * P:(k + 1) * P],
                                    ident[0:G_ROWS, 0:G_ROWS])
            last.then_inc(setup_pe, 1)
            for s, n0 in zip(plan, first):
                if s[0] == "norm":
                    turn(xn, KD, xn_ready)
                elif s[0] == "ffn":
                    ffn(s, n0)
                elif s[0] == "conv":
                    conv(s, n0)
                elif s[0] == "mla":
                    mla(s, n0)
                elif s[0] == "sg":
                    sg(s, n0)
                elif s[0] == "tables":
                    tables()
                elif s[0] == "mix":
                    mix(s, n0)
                elif s[0] == "ple":
                    ple(s, n0)

        @block.gpsimd
        def _(pool):
            pool.memset(g_rows, 0.0).then_inc(rows_clear, 1)
            pool.wait_ge(rows_clear, 1)
            pool.dma_start(g_rows[0:12, :], A["norm_g"].rearrange("i j d -> (i j) d")).then_inc(gain_in, 16)
            pool.dma_start(g_rows[12:20, :], A["norm_g_2"].rearrange("i j d -> (i j) d")).then_inc(gain_in, 16)
            pool.dma_start(g_rows[G_SGV:G_SGV + 1, :], A["sg_v_norm"]).then_inc(gain_in, 16)
            pool.dma_start(g_rows[G_CONV:G_CONV + 6, :], A["conv_k"].rearrange("i j d -> (i j) d")).then_inc(gain_in, 16)
            pool.dma_start(g_rows[G_MISC:G_MISC + 1, 0:QL], A["mla_q_norm"]).then_inc(gain_in, 16)
            pool.dma_start(g_rows[G_MISC:G_MISC + 1, QL:QL + KVL], A["mla_kv_norm"]).then_inc(gain_in, 16)
            pool.dma_start(g_rows[G_MISC:G_MISC + 1, QL + KVL:QL + KVL + 256],
                           A["diff_subln_2"].rearrange("(o i) d -> o (i d)", o=1)).then_inc(gain_in, 16)
            pool.dma_start(pos[:], A["positions"][0].rearrange("(t p) -> p t", p=P), allow_slow_non_contiguous=True).then_inc(misc_in, 16)
            pool.dma_start(g96[:, 0, :], A["mla_q_gain"].partition_broadcast(P)).then_inc(misc_in, 16)
            pool.dma_start(g96[:, 1, :], A["mla_k_gain"].partition_broadcast(P)).then_inc(misc_in, 16)
            if any(s[0] == "sg" for s in plan):
                if any(s[0] == "mla" for s in plan):
                    pool.wait_ge(x_ready, NT * (2 + [s[0] for s in plan if s[0] not in ("norm",)].index("mla")))
                pool.dma_start(sgb, A["sg_b"][0].rearrange("g t -> (g t)").partition_broadcast(P)).then_inc(ws_in, 16)
                pool.dma_start(wsr, A["sg_w_s"][0].rearrange("g t s -> t g s")).then_inc(ws_in, 16)
            if any(s[0] == "tables" for s in plan):
                for i in range(2):
                    for v in range(2):
                        pool.dma_start(w2[:, i, v], A["nsa_cmp_w2_2"][i, v].rearrange("(m p) d -> p m d", p=P)
                                       ).then_inc(w2_in, 16)
                pool.wait_ge(arena_free, 1)
                pool.dma_start(relb[0:32, :], A["rel_bias_2"]).then_inc(tables_in, 16)
                pool.dma_start(lp.rearrange("p i a d -> p (i a d)"),
                               A["diff_lambda_2"].rearrange("i a d -> (i a d)").partition_broadcast(P)
                               ).then_inc(tables_in, 16)
                pool.dma_start(sinks[:], A["swa_sinks_2"].rearrange("i h -> (i h)").partition_broadcast(P)
                               ).then_inc(tables_in, 16)
                for i in range(2):
                    for v in range(2):
                        at = 32 * i + 16 * v
                        pool.dma_start(prows[at:at + 16, :],
                                       A["nsa_cmp_pos_2"][i, v].rearrange("(j q) d -> j (q d)", q=2)
                                       ).then_inc(tables_in, 16)
                pool.wait_ge(rv_ready, 1)
                pool.dma_start(scratch[0:12, :], rv[0:12, 0, :]).then_inc(rv_stored, 16)
                pool.dma_start(scratch[12:20, :], rv[0:8, 1, :]).then_inc(rv_stored, 16)
                pool.wait_ge(rv_stored, 32)
                askew = bass.AP(scratch.tensor, 0, [[1, P], [384, 20], [1, 256]])
                pool.dma_start(U, askew).then_inc(u_in, 16)
            mixes = 0
            ples = 0
            residuals = 0
            for s in plan:
                if s[0] == "mix":
                    mixes += 1
                    pool.wait_ge(kc_ready, mixes)
                    for v in range(2):
                        for g in range(2):
                            src = KC[64 * g:64 * g + 64, v, :]
                            pool.dma_start(KC2[0:64, v, g, :], src).then_inc(kc2_in, 16)
                            pool.dma_start(KC2[64:128, v, g, 0:TOK - 1], src[:, 1:TOK]).then_inc(kc2_in, 16)
                if s[0] == "ple":
                    if ples:
                        pool.wait_ge(x_ready, NT * (1 + residuals))
                    pool.dma_start(ple_in[:], A["p_2"][s[1], 0].rearrange("(t p) d -> p t d", p=P)
                                   ).then_inc(ple_arrived, 16)
                    ples += 1
                residuals += s[0] not in ("norm", "tables", "final")
            if plan[-1][0] == "final":
                pool.wait_ge(x_ready, NT * (residuals - 1))
                pool.dma_start(gfin, A["final_norm_2"].partition_broadcast(P)).then_inc(fin_in, 16)


_INS = ["x", "positions", "norm_g", "ffn_gate", "ffn_up", "ffn_down", "conv_w_in", "conv_k", "conv_w_out", "mla_w_a",
        "mla_q_norm", "mla_w_uq", "mla_kv_norm", "mla_w_ukv", "mla_q_gain", "mla_k_gain", "mla_w_o", "sg_w_in",
        "sg_v_norm", "sg_w_s", "sg_b", "sg_w_out", "p_2", "norm_g_2", "ffn1_wi_2", "ffn1_wo_2", "w_in_2",
        "diff_lambda_2", "diff_subln_2", "nsa_cmp_pos_2", "nsa_cmp_w1_2", "nsa_cmp_w2_2", "swa_sinks_2",
        "w_branch_2", "w_out_2", "ffn2_wi_2", "ffn2_wo_2", "w_ple_2", "w_ple_gate_2", "rel_bias_2", "final_norm_2"]


def shape_constants():
    c = np.zeros((P, C_END), np.float32)
    q = np.arange(P)[:, None]
    c[:, C_ID:C_ID + P] = np.eye(P)
    c[:, C_FLIP:C_FLIP + P] = np.eye(P)[::-1]
    c[:, C_CAUSAL:C_CAUSAL + 2 * P] = np.where(P + q - np.arange(2 * P)[None] >= 0, 0.0, NEG)
    c[:, C_LOWT:C_LOWT + P] = (q <= np.arange(P)[None])
    for t in range(2):
        c[:, C_CMPOK + 15 * t:C_CMPOK + 15 * t + 15] = (P * t + q - 16 * np.arange(15)[None] - 31 >= 0)
    f = np.arange(0, ROPE, 2, dtype=np.float32) / np.float32(ROPE)
    c[:, C_FREQ:C_FREQ + 16] = np.float32(1.0) / np.float32(10000.0) ** f

    def one_hot(dist, masked):
        n = np.maximum(dist, 0)
        nf = np.maximum(n, 1).astype(np.float32)
        large = 16 + (np.log(nf / np.float32(16)) / np.float32(np.log(8.0)) * np.float32(16)).astype(np.int32)
        b = np.where(n < 16, n, np.minimum(large, 31))
        o = np.zeros((33, dist.size), np.float32)
        o[np.where(masked, 32, b), np.arange(dist.size)] = 1.0
        return o

    d = 255 - np.arange(384)
    c[0:33, C_OHREV:C_OHREV + 384] = one_hot(d, d < 0)
    c[0:33, C_OHREV + 384:C_OHREV + 768] = one_hot(d, (d < 0) | (d >= 128))
    d = np.arange(512) - 256
    c[0:33, C_OHF:C_OHF + 512] = one_hot(d, d < 0)
    return c


def kernel(**inputs):
    import concourse.bacc as bacc
    from concourse.bass_utils import run_bass_kernel_spmd

    nc = bacc.Bacc("TRN2", target_bir_lowering=False, num_devices=1)
    arrays, A = {}, {}
    for name in _INS + ["consts"]:
        a = shape_constants() if name == "consts" else np.ascontiguousarray(inputs[name])
        arrays[f"in_{name}"] = a
        A[name] = nc.dram_tensor(f"in_{name}", a.shape, mybir.dt.from_np(a.dtype), kind="ExternalInput").ap()
    out = nc.dram_tensor("out_0", (1, TOK, D), F32, kind="ExternalOutput").ap()
    build(nc, A, out)
    r = run_bass_kernel_spmd(nc, [arrays], core_ids=[0])
    return r.results[0]["out_0"]
```

```python
from contextlib import ExitStack

import numpy as np

import concourse.bass as bass
from concourse import mybir

ALU = mybir.AluOpType
ACT = mybir.ActivationFunctionType
AX = mybir.AxisListType
F32 = mybir.dt.float32
F32R = mybir.dt.float32r
I32 = mybir.dt.int32

P = 128
TOK = 256
NT = TOK // P
D = 1024
KD = D // P
FF = 2816
EPS = 1e-6
TILE = 2048
RING = 3
CW = 256
NCH = FF // CW
QUARTERS = 4
HSCALE = 0.125
BIG = 3.0e38
DEEP = 4
NORM_FILL = 18
NEG = -1e30
QL, KVL, ROPE, NOPE, VH, QKH, MH = 256, 128, 32, 64, 64, 96, 16
RSQRT_MAGIC = float(0x5F3759DF)
TWO_PI = (6.28125, 0.0019340515136718750, 1.255665914356996e-06)
PI_IN = 3.1415925

C_ID = 0
C_FLIP = 128
C_CAUSAL = 256
C_LOWT = 512
C_CMPOK = 640
C_FREQ = 672
C_KEPT = 688
C_OHREV = C_KEPT
C_OHF = C_OHREV + 768
C_END = C_OHF + 512
ARENA = 15880

G_SGV = 20
G_CONV = 21
G_MISC = 27
G_ROWS = 28


W_AQ, W_AK, W_AV, W_BQ, W_BC, W_BS, W_BW, W_BG = 0, 512, 1024, 1536, 2048, 2304, 2560, 2816
W_CQ, W_CKV, W_G = 2840, 3352, 3608
NCMP = 15
LAM_INIT = [0.8 - 0.6 * float(np.exp(-0.3 * i)) for i in range(2)]


class Seen:

    def __init__(self):
        self.n, self.turn, self.rate, self.before = {}, None, {}, {}

    def next(self, sem, k=1):
        self.n[sem.name] = self.n.get(sem.name, 0) + k
        v = self.n[sem.name]
        if self.turn is not None:
            v = self.turn * self.rate[sem.name] + v
        return v

    def enter(self, turn, rate):
        self.turn, self.rate, self.before = turn, {s.name: r for s, r in rate}, dict(self.n)

    def leave(self, turns):
        for name, r in self.rate.items():
            assert self.n.get(name, 0) - self.before.get(name, 0) == r, (name, r)
            self.n[name] += (turns - 1) * r
        self.turn = None


def full_plan():
    plan = []
    for i in range(4):
        plan += [("norm", 3 * i), ("ffn", 1, i, 0), ("norm", 3 * i + 1)]
        plan += [("conv", i // 3)] if i % 3 == 0 else [("mla",)] if i == 1 else [("sg",)]
        plan += [("norm", 3 * i + 2), ("ffn", 1, i, 1)]
    at = plan.index(("norm", 9))
    plan[at:at] = [("tables", 0)]
    at = plan.index(("norm", 10))
    plan[at:at] = [("tables", 1)]
    plan += [("tables", 2)]
    for i in range(2):
        plan += [("norm", 12 + 4 * i), ("ffn", 2, i, 0), ("norm", 13 + 4 * i), ("mix", i)]
        plan += [("norm", 14 + 4 * i), ("ffn", 2, i, 1), ("norm", 15 + 4 * i), ("ple", i)]
    return plan + [("final",)]


def build(nc, A, out, plan=None):
    plan = plan or full_plan()
    with ExitStack() as ctx:
        def sb(name, shape, dt=F32):
            return ctx.enter_context(nc.sbuf_tensor(name, shape, dt))

        def sem(name):
            return ctx.enter_context(nc.semaphore(name))

        MIX_BANKS = 21 + 24
        raw = [sb(f"raw{i}", [P, TILE]) for i in range(RING)]
        w_hi = [sb(f"w_hi{i}", [P, TILE], F32R) for i in range(RING)]
        w_lo = [sb(f"w_lo{i}", [P, TILE], F32R) for i in range(RING)]
        xT_hi = sb("xT_hi", [P, KD, TOK], F32R)
        xT_lo = sb("xT_lo", [P, KD, TOK], F32R)
        hT_hi = sb("hT_hi", [P, 2, 2, TOK], F32R)
        hT_lo = sb("hT_lo", [P, 2, 2, TOK], F32R)
        yT_hi = sb("yT_hi", [P, 4, TOK], F32R)
        yT_lo = sb("yT_lo", [P, 4, TOK], F32R)
        x = sb("x", [P, NT, D])
        xn = sb("xn", [P, NT, D])
        gate = sb("gate", [P, 512])
        prod = sb("prod", [P, 512])
        consts = sb("consts", [P, C_KEPT])
        gains = sb("gains", [P, KD, 32])
        ss = sb("ss", [P, 8])
        nwt = sb("nwt", [P, 64])
        nwv = sb("nwv", [P, 64])
        rstd = sb("rstd", [P, 8])
        diag = sb("diag", [P, NT, P])
        arena = sb("arena", [P, ARENA])
        pos = sb("pos", [P, NT], I32)
        cos = sb("cos", [P, NT, 16])
        sin = sb("sin", [P, NT, 16])
        g96 = sb("g96", [P, 2, QKH])

        def carve(at, *shape):
            n = int(np.prod(shape))
            v = arena[:, at:at + n]
            names = " ".join("abcd"[:len(shape)])
            dims = {"abcd"[i]: shape[i] for i in range(len(shape) - 1)}
            return v.rearrange(f"p ({names}) -> p {names}", **dims) if len(shape) > 1 else v

        g_rows = arena[0:G_ROWS, 0:D]
        zconv = carve(0, 2, TOK + 2)
        yconv = carve(520, 2, TOK)
        Q = carve(0, NT, MH, QKH)
        KV = carve(3072, NT, MH, NOPE + VH)
        KF = carve(7168, NT, MH, QKH)
        squares = carve(7168, NT, MH, QKH)
        latent = carve(10240, NT, QL + KVL + ROPE)
        cn = carve(11072, NT, QL + KVL)
        kpe = carve(11840, NT, ROPE)
        rtmp = carve(11904, 4, NT * MH, 16)
        headT = [carve(13952 + 512 * i, 512) for i in range(2)]
        units_buf = sb("units", [P, DEEP, 384])
        S = [units_buf[:, i, :] for i in range(DEEP)]
        PT = [sb(f"PT{i}", [P, 384]) for i in range(2)]
        nmax = [sb(f"nmax{i}", [P, 2]) for i in range(DEEP)]
        esum = [sb(f"esum{i}", [P, 2]) for i in range(DEEP)]
        rsum = [sb(f"rsum{i}", [P, 2]) for i in range(DEEP)]
        ssh = sb("ssh", [P, 64])
        rsh = sb("rsh", [P, 64])
        esink = [sb(f"esink{i}", [P, 2]) for i in range(DEEP)]
        T = carve(0, 20, 256)
        TC = carve(5120, 8, 2 * NCMP)
        U = carve(5376, 20, 256)
        rv = carve(10496, 2, 384)
        lp = carve(11264, 2, 4, 64)
        prows = arena[0:64, 11776:11904]
        relb = arena[0:33, 11904:11924]
        one_hots = arena[0:33, 11924:11924 + C_END - C_KEPT]
        AQ, AK, AV = carve(5376, 4, TOK), carve(6400, 4, TOK), carve(7424, NT, 512)
        BQ, CQ = carve(8448, 4, TOK), carve(11008, 4, TOK)
        KC = carve(9472, 2, TOK)
        BS, BW, CKV = carve(9984, 512), carve(10496, 512), carve(12032, 512)
        gB = carve(12544, NT, 24)
        KC2 = carve(12592, 2, 2, TOK)
        blk = carve(13616, 2, 16, 2 * NCMP)
        hidT = carve(14576, 2, 2, 2 * NCMP)
        kcT = carve(14696, 2 * NCMP)
        vc = arena[0:NCMP, 14726:14854]
        YA = carve(14854, NT, 512)
        merged = xn[:].rearrange("p t (m n) -> p (t m) n", n=TOK)
        blk_hi = yT_hi[:].rearrange("p k n -> p (k n)")[:, 0:960].rearrange("p (v j n) -> p v j n", v=2, j=16)
        blk_lo = yT_lo[:].rearrange("p k n -> p (k n)")[:, 0:960].rearrange("p (v j n) -> p v j n", v=2, j=16)
        pos2 = sb("pos2", [P, 2, 2, 16])
        w2 = sb("w2", [P, 2, 2, 2, 64])
        neglam = sb("neglam", [P, 2])
        sinks = sb("sinks", [P, 16])
        negsinks = sb("negsinks", [P, 16])
        subln = sb("subln", [P, 2])
        ple_in = units_buf[:].rearrange("p a b -> p (a b)")[:, 0:512].rearrange("p (t d) -> p t d", t=NT)
        gfin = carve(0, D)
        wsT = carve(0, 8, P)
        wsr = carve(1024, 8, P)
        mixed = carve(2048, 2, TOK)
        sgb = carve(2560, D)

        ident = consts[:, C_ID:C_ID + P]

        acc = [ctx.enter_context(nc.psum_tensor(f"acc{i}", [P, 512], F32)) for i in range(4)]
        up = [ctx.enter_context(nc.psum_tensor(f"up{i}", [P, 512], F32)) for i in range(4)]

        landed = [sem(f"landed{i}") for i in range(RING)]
        const_in = sem("const_in")
        x_in = sem("x_in")
        gain_in = sem("gain_in")
        rows_clear = sem("rows_clear")
        hi_ready = sem("hi_ready")
        lo_ready = sem("lo_ready")
        tile_used = sem("tile_used")
        bank_free = sem("bank_free")
        setup_pe = sem("setup_pe")
        setup_dve = sem("setup_dve")
        x_ready = sem("x_ready")
        ss_ready = sem("ss_ready")
        diag_ready = sem("diag_ready")
        xT_ready = sem("xT_ready")
        xhi_ready = sem("xhi_ready")
        xlo_ready = sem("xlo_ready")
        gate_ready = sem("gate_ready")
        prod_ready = sem("prod_ready")
        hhi_ready = sem("hhi_ready")
        hlo_ready = sem("hlo_ready")
        acc_done = sem("acc_done")
        dve_step = sem("dve_step")
        act_step = sem("act_step")
        misc_in = sem("misc_in")
        trig_arg = sem("trig_arg")
        trig_done = sem("trig_done")
        cn_ready = sem("cn_ready")
        group_done = sem("group_done")
        kv_copied = sem("kv_copied")
        qk_ready = sem("qk_ready")
        headT_done = sem("headT_done")
        headT_ready = sem("headT_ready")
        scores_done = sem("scores_done")
        nmax_ready = sem("nmax_ready")
        exp_ready = sem("exp_ready")
        rsum_ready = sem("rsum_ready")
        pool_step = sem("pool_step")
        p_ready = sem("p_ready")
        turned = sem("turned")
        pt_ready = sem("pt_ready")
        o_done, oa_done = sem("o_done"), sem("oa_done")
        ohi_ready = sem("ohi_ready")
        olo_ready = sem("olo_ready")
        ws_in = sem("ws_in")
        ws_turned = sem("ws_turned")
        ws_ready = sem("ws_ready")
        v_ready = sem("v_ready")
        mix_done = sem("mix_done")
        tables_in = sem("tables_in")
        arena_free = sem("arena_free")
        tab_pe = sem("tab_pe")
        tab_dve = sem("tab_dve")
        tab_act = sem("tab_act")
        rv_stored = sem("rv_stored")
        rv_ready = sem("rv_ready")
        u_in = sem("u_in")
        gates_ready = sem("gates_ready")
        kc_ready = sem("kc_ready")
        kc2_in = sem("kc2_in")
        blk_ready = sem("blk_ready")
        blkhi_ready = sem("blkhi_ready")
        blklo_ready = sem("blklo_ready")
        hid_ready = sem("hid_ready")
        cmp_done = sem("cmp_done")
        cmp_ready = sem("cmp_ready")
        proj_ready = sem("proj_ready")
        ya_copied = sem("ya_copied")
        ya_ready = sem("ya_ready")
        merge_step = sem("merge_step")
        ple_added = sem("ple_added")
        mhi_ready = sem("mhi_ready")
        mlo_ready = sem("mlo_ready")
        ple_arrived = sem("ple_arrived")
        fin_in = sem("fin_in")
        w2_in = sem("w2_in")
        fin_ready = sem("fin_ready")
        scratch = nc.dram_tensor("bias_rows", (20, 384), F32, kind="Internal").ap()
        vn_ready = sem("vn_ready")
        stored = sem("stored")

        def kpn(w):
            return w.rearrange("(k p) n -> p k n", p=P)

        def tview(buf, nk, n):
            return buf[:, 0:nk * n].rearrange("p (k n) -> p k n", k=nk)

        def ffn_weights(s):
            _, blk, i, j = s
            if blk == 1:
                return A["ffn_gate"][i, j], A["ffn_up"][i, j], A["ffn_down"][i, j]
            wi = A["ffn1_wi_2" if j == 0 else "ffn2_wi_2"][i]
            wo = A["ffn1_wo_2" if j == 0 else "ffn2_wo_2"][i]
            return wi[:, 0:FF], wi[:, FF:2 * FF], wo

        def up_tile(w, col):
            return (KD, CW, [(slice(None), kpn(w)[:, :, col:col + CW])])

        def query_tile(w, col, j):
            return (KD, CW, [(slice(P * r + 64 * g, P * r + 64 * g + 64),
                              kpn(w)[:, :, col + 256 * g + 64 * (2 * j + r):col + 256 * g + 64 * (2 * j + r) + 64])
                             for r in range(2) for g in range(2)])

        def cols_tile(w, nk, col, n):
            return (nk, n, [(slice(None), kpn(w)[:, :, col:col + n])])

        def down_tile(w, row):
            return (2, D, [(slice(None), kpn(w[row:row + 2 * P, :]))])

        def tiles_of(s):
            if s[0] == "conv":
                w, wo = A["conv_w_in"][s[1]], A["conv_w_out"][s[1]]
                t = []
                for c in range(4):
                    t += [up_tile(w, D * m + CW * c) for m in (1, 2, 0)]
                    if c:
                        t.append(down_tile(wo, CW * (c - 1)))
                return t + [down_tile(wo, CW * 3)]
            if s[0] == "mla":
                wa, wq, wkv, wo = A["mla_w_a"][0], A["mla_w_uq"][0], A["mla_w_ukv"][0], A["mla_w_o"][0]
                t = [cols_tile(wa[512 * h:512 * h + 512, :], 4, 0, QL + KVL + ROPE) for h in range(2)]
                t += [cols_tile(wq, 2, 0, 1024), cols_tile(wq, 2, 1024, 512), cols_tile(wkv, 1, 0, 2048)]
                return t + [down_tile(wo, CW * i) for i in range(4)]
            if s[0] == "sg":
                w, wo = A["sg_w_in"][0], A["sg_w_out"][0]
                t = [cols_tile(w[512 * h:512 * h + 512, :], 4, D + 512 * g, 512) for g in range(2) for h in range(2)]
                for c in range(4):
                    t.append(up_tile(w, CW * c))
                    if c:
                        t.append(down_tile(wo, CW * (c - 1)))
                return t + [down_tile(wo, CW * 3)]
            if s[0] == "mix":
                w, w1 = A["w_in_2"][s[1]], A["nsa_cmp_w1_2"][s[1]]
                wb, wo = A["w_branch_2"][s[1]], A["w_out_2"][s[1]]
                t = [up_tile(w, W_BC)] + [up_tile(w, W_AQ + CW * j) for j in range(4)]
                t += [cols_tile(w[512 * h:512 * h + 512, :], 4, W_AV, 512) for h in range(2)]
                t += [query_tile(w, W_BQ, j) for j in range(2)] + [up_tile(w, W_BS), up_tile(w, W_BW)]
                t += [cols_tile(w, KD, W_BG, 24)]
                t += [up_tile(w1[v, 1024 * h:1024 * h + 1024, :], 0) for v in range(2) for h in range(2)]
                t += [query_tile(w, W_CQ, j) for j in range(2)] + [up_tile(w, W_CKV)]
                for br in range(3):
                    for c in range(2):
                        t += [up_tile(w, W_G + D * br + 512 * c + CW * j) for j in range(2)]
                        t += [cols_tile(wb[br], 4, 512 * c, 512)]
                return t + [down_tile(wo, CW * j) for j in range(4)]
            if s[0] == "ple":
                wg, wp = A["w_ple_gate_2"][s[1]], A["w_ple_2"][s[1]]
                t = []
                for c in range(2):
                    t += [cols_tile(wg[512 * h:512 * h + 512, :], 4, 512 * c, 512) for h in range(2)]
                    t += [cols_tile(wp, 2, 512 * c, 512)]
                return t
            return []

        def branch_units(br):
            if br == 0:
                return [(c, h, c == 1) for h in range(4) for c in range(2)]
            if br == 1:
                return [(k, h, h % 2 == 1 and k == "cmp") for h in range(8) for k in ("sel", "win", "cmp")]
            return [("win", h, h % 2 == 1) for h in range(8)]

        first = []
        count = 0
        for s in plan:
            first.append(count)
            count += 3 * NCH if s[0] == "ffn" else len(tiles_of(s))
        n_tiles = count

        block = ctx.enter_context(nc.Block())

        @block.sync
        def _(sp):
            seen = Seen()
            sp.dma_start(x[:], A["x"][0].rearrange("(t p) d -> p t d", p=P)).then_inc(x_in, 16)
            sp.wait_ge(rows_clear, seen.next(rows_clear))
            sp.dma_start(g_rows[0:12, :], A["norm_g"].rearrange("i j d -> (i j) d")).then_inc(gain_in, 16)
            sp.dma_start(g_rows[12:20, :], A["norm_g_2"].rearrange("i j d -> (i j) d")).then_inc(gain_in, 16)
            sp.dma_start(g_rows[G_SGV:G_SGV + 1, :], A["sg_v_norm"]).then_inc(gain_in, 16)
            sp.dma_start(g_rows[G_CONV:G_CONV + 6, :], A["conv_k"].rearrange("i j d -> (i j) d")).then_inc(gain_in, 16)
            sp.dma_start(g_rows[G_MISC:G_MISC + 1, 0:QL], A["mla_q_norm"]).then_inc(gain_in, 16)
            sp.dma_start(g_rows[G_MISC:G_MISC + 1, QL:QL + KVL], A["mla_kv_norm"]).then_inc(gain_in, 16)
            sp.dma_start(g_rows[G_MISC:G_MISC + 1, QL + KVL:QL + KVL + 256],
                          A["diff_subln_2"].rearrange("(o i) d -> o (i d)", o=1)).then_inc(gain_in, 16)

            def slot_free(n):
                if n >= RING:
                    sp.wait_ge(lo_ready, seen.next(lo_ready))

            def load(n, t):
                slot_free(n)
                nk, ncol, parts = t
                dst = tview(raw[n % RING], nk, ncol)
                for cols, src in parts:
                    sp.dma_start(dst[:, :, cols], src).then_inc(landed[n % RING], 16)

            def ffn(s, n0):
                wg, wu, wd = ffn_weights(s)
                G = [up_tile(wg, CW * c) for c in range(NCH)]
                U = [up_tile(wu, CW * c) for c in range(NCH)]
                Dn = [down_tile(wd, CW * c) for c in range(NCH)]
                for j, t in enumerate([G[0], U[0], G[1], U[1], Dn[0]]):
                    load(n0 + j, t)
                base = n0 + 5
                with sp.Fori(0, 4) as i:
                    seen.enter(i, [(lo_ready, 6)])
                    for c in range(2):
                        for j, w in enumerate((wg, wu)):
                            n = base + 3 * c + j
                            slot_free(n)
                            sp.dma_start(tview(raw[n % RING], KD, CW),
                                         kpn(w)[:, :, bass.ds(i * (2 * CW) + (2 + c) * CW, CW)]
                                         ).then_inc(landed[n % RING], 16)
                        n = base + 3 * c + 2
                        slot_free(n)
                        sp.dma_start(tview(raw[n % RING], 2, D),
                                     wd[bass.ds(i * (2 * CW) + (1 + c) * CW, CW), :].rearrange("(k p) n -> p k n", p=P)
                                     ).then_inc(landed[n % RING], 16)
                    seen.leave(4)
                for j, t in enumerate([G[10], U[10], Dn[9], Dn[10]]):
                    load(n0 + 29 + j, t)

            for s, n0 in zip(plan, first):
                if s[0] == "ffn":
                    ffn(s, n0)
                else:
                    for j, t in enumerate(tiles_of(s)):
                        load(n0 + j, t)
            if plan[-1][0] == "final":
                sp.wait_ge(fin_ready, seen.next(fin_ready))
                res = xn
            else:
                sp.wait_ge(x_ready, QUARTERS * (1 + sum(s[0] not in ("norm", "tables", "final") for s in plan)))
                res = x
            sp.dma_start(out[0].rearrange("(t p) d -> p t d", p=P), res[:]).then_inc(stored, 16)
            sp.wait_ge(stored, 16)

        @block.scalar
        def _(act):
            seen = Seen()
            act.dma_start(consts[:], A["consts"][:, 0:C_KEPT]).then_inc(const_in, 16)
            parts_of = {}
            for s, n0 in zip(plan, first):
                for j, t in enumerate(tiles_of(s)):
                    parts_of[n0 + j] = len(t[2])

            def split_hi(n):
                if n >= n_tiles:
                    return
                act.wait_ge(landed[n % RING], seen.next(landed[n % RING], 16 * parts_of.get(n, 1)))
                nc.scalar.activation(w_hi[n % RING][:], raw[n % RING][:], ACT.Copy).then_inc(hi_ready, 1)

            def consumed(n):
                act.wait_ge(tile_used, seen.next(tile_used))
                split_hi(n + RING)

            def parts_hi(nk, row, dst=xT_hi, same=None):
                for k in range(nk):
                    if k % 2 == 0:
                        act.wait_ge(xT_ready, seen.next(xT_ready))
                    g = gains[:, k, row:row + 1] if same is None else same
                    last = nc.scalar.activation(dst[:, k, :], acc[k // 2][:, (k % 2) * TOK:(k % 2 + 1) * TOK],
                                                ACT.Copy, scale=g)
                    if k % 2 or k == nk - 1:
                        last.then_inc(xhi_ready, 1)

            owed = []

            def settle():
                if owed:
                    act.wait_ge(acc_done, seen.next(acc_done, QUARTERS))
                    split_hi(owed.pop() + RING)

            def mean_squares():
                for t in range(NT):
                    for h in range(2):
                        cols = slice(512 * h, 512 * h + 512)
                        act.wait_ge(x_ready, seen.next(x_ready))
                        nc.scalar.activation(xn[:, t, cols], x[:, t, cols], ACT.Square, scale=float(D) ** -0.5,
                                             accum_out=ss[:, 2 * t + h:2 * t + h + 1]).then_inc(ss_ready, 1)

            starting = [True]

            def norm(row):
                mean_squares()
                settle()
                if starting[0]:
                    split_hi(0)
                    act.wait_ge(setup_dve, 1)
                parts_hi(KD, row)
                if starting[0]:
                    for n in range(1, RING):
                        split_hi(n)
                    starting[0] = False

            def product_hi(par):
                act.wait_ge(prod_ready, seen.next(prod_ready))
                nc.scalar.activation(hT_hi[:, par], prod[:].rearrange("p (k n) -> p k n", k=2),
                                     ACT.Copy).then_inc(hhi_ready, 1)

            def ffn(s, n0, bank0):
                def chunk(n, c, down):
                    consumed(n)
                    b = (bank0 + 2 * c) % 4
                    nc.scalar.activation(gate[:], up[b][:], ACT.Silu).then_inc(gate_ready, 1)
                    consumed(n + 1)
                    product_hi(c % 2)
                    if down:
                        consumed(n + 2)

                chunk(n0, 0, False)
                chunk(n0 + 2, 1, True)
                with act.Fori(0, 4) as i:
                    seen.enter(i, [(landed[r], 32) for r in range(RING)] + [(tile_used, 6), (prod_ready, 2)])
                    chunk(n0 + 5, 2, True)
                    chunk(n0 + 8, 3, True)
                    seen.leave(4)
                chunk(n0 + 29, 10, True)
                owed.append(n0 + 32)

            def conv(s, n0, bank0):
                for c in range(4):
                    n = n0 + 4 * c - (c > 0)
                    b = (bank0 + 3 * c) % 4
                    consumed(n)
                    nc.scalar.activation(gate[:], up[b][:], ACT.Copy).then_inc(gate_ready, 1)
                    consumed(n + 1)
                    consumed(n + 2)
                    product_hi(c % 2)
                    if c:
                        consumed(n + 3)
                owed.append(n0 + 15)

            def exp_unit(u, widths=((1, 0, 256), (0, 256, 384)), sink=None):
                b = u % DEEP
                act.wait_ge(nmax_ready, seen.next(nmax_ready))
                for i, lo, hi in widths:
                    last = nc.scalar.activation(S[b][:, lo:hi], S[b][:, lo:hi], ACT.Exp, bias=nmax[b][:, i:i + 1],
                                                scale=-1.0, accum_out=esum[b][:, i:i + 1])
                if sink is not None:
                    last = nc.scalar.activation(esink[b][:], nmax[b][:], ACT.Exp, bias=sink)
                last.then_inc(exp_ready, 1)

            def copy_turned(u, rows=P, width=384):
                act.wait_ge(turned, seen.next(turned))
                nc.scalar.activation(PT[u % 2][0:rows, 0:width], acc[2 + u % 2][0:rows, 0:width],
                                     ACT.Copy).then_inc(pt_ready, 1)

            def mla(s, n0, bank0):
                act.wait_ge(trig_arg, seen.next(trig_arg))
                nc.scalar.activation(sin[:], sin[:], ACT.Sin)
                nc.scalar.activation(cos[:], cos[:], ACT.Sin).then_inc(trig_done, 1)
                consumed(n0)
                consumed(n0 + 1)
                parts_hi(3, G_MISC)
                consumed(n0 + 2)
                consumed(n0 + 3)
                b = (bank0 + 8) % 4
                for g in range(4):
                    if g < 3:
                        act.wait_ge(group_done, seen.next(group_done))
                    else:
                        consumed(n0 + 4)
                    for t in range(NT):
                        last = nc.scalar.activation(
                            arena[:, 3072 + 2048 * t + 512 * g:3072 + 2048 * t + 512 * g + 512],
                            up[(b + 2 * g + t) % 4][:], ACT.Copy)
                    last.then_inc(kv_copied, 1)

                def o_hi(j):
                    act.wait_ge(o_done, seen.next(o_done))
                    nc.scalar.activation(xT_hi[:, j, :], up[2 + j % 2][:, 0:TOK],
                                         ACT.Copy).then_inc(ohi_ready, 1)

                for i in range(1, MH + 7):
                    if i - 1 < MH:
                        exp_unit(i - 1)
                    if 0 <= i - 4 < MH:
                        copy_turned(i - 4)
                    if 0 <= i - 6 < MH and (i - 6) % 2:
                        o_hi((i - 6) // 2)
                for j in range(3):
                    consumed(n0 + 5 + j)
                owed.append(n0 + 8)

            def sg(s, n0, bank0):
                for g in range(2):
                    consumed(n0 + 2 * g)
                    consumed(n0 + 2 * g + 1)
                    for t in range(NT):
                        last = nc.scalar.activation(xn[:, t, 512 * g:512 * g + 512],
                                                    up[(bank0 + 2 * g + t) % 4][:], ACT.Gelu_apprx_tanh)
                    last.then_inc(v_ready, 1)
                for c in range(4):
                    n = n0 + 4 + 2 * c - (c > 0)
                    consumed(n)
                    nc.scalar.activation(gate[:], up[(bank0 + 4 + 2 * c) % 4][:],
                                         ACT.Gelu_apprx_tanh).then_inc(gate_ready, 1)
                    product_hi(c % 2)
                    if c:
                        consumed(n + 1)
                owed.append(n0 + 11)

            def tables(part):
                settle()
                if part != 1:
                    return
                act.wait_ge(tab_dve, seen.next(tab_dve))
                nc.scalar.activation(ssh[:, 4:8], ssh[:, 0:4], ACT.Exp).then_inc(tab_act, 1)

            def mix(s, n0, bank0):
                n = n0
                for i in range(11):
                    consumed(n)
                    n += 1
                    if i == 6:
                        for v in range(2):
                            act.wait_ge(blk_ready, seen.next(blk_ready))
                            nc.scalar.activation(blk_hi[:, v], blk[:, v], ACT.Copy).then_inc(blkhi_ready, 1)
                consumed(n)
                nc.scalar.activation(gB.rearrange("p t h -> p (t h)"), up[(bank0 + 11) % 4][:, 0:48],
                                     ACT.Sigmoid).then_inc(gates_ready, 1)
                n += 1
                for v in range(2):
                    consumed(n)
                    consumed(n + 1)
                    n += 2
                    for m in range(2):
                        last = nc.scalar.activation(hidT[:, v, m, :], up[(bank0 + 12 + 2 * v + m) % 4][:, 0:2 * NCMP],
                                                    ACT.Gelu_apprx_tanh)
                    last.then_inc(hid_ready, 1)
                for _ in range(3):
                    consumed(n)
                    n += 1
                for br in range(3):
                    units = branch_units(br)
                    for i in range(len(units) + 5):
                        if i < len(units):
                            kind, h = units[i][:2]
                            if kind == "cmp":
                                exp_unit(i, ((0, 0, NCMP), (1, NCMP, 2 * NCMP)))
                            else:
                                exp_unit(i, sink=sinks[:, 8 * s[1] + h:8 * s[1] + h + 1] if br == 2 else None)
                        if 0 <= i - 3 < len(units):
                            if units[i - 3][0] == "cmp":
                                copy_turned(i - 3, NCMP, 256)
                            else:
                                copy_turned(i - 3)
                        if br and 0 <= i - 5 < len(units) and units[i - 5][2]:
                            j = units[i - 5][1] // 2
                            act.wait_ge(o_done, seen.next(o_done))
                            nc.scalar.activation(yT_hi[:, j, :], up[2 + j % 2][:, 0:TOK],
                                                 ACT.Copy).then_inc(ohi_ready, 1)
                    if br == 0:
                        parts_hi(4, 0, yT_hi, subln[:, s[1]:s[1] + 1])
                    for c in range(2):
                        if br or c:
                            act.wait_ge(merge_step, seen.next(merge_step))
                        for j, dst in enumerate((gate, prod)):
                            consumed(n)
                            n += 1
                            nc.scalar.activation(dst[:], up[(bank0 + 21 + 8 * br + 4 * c + j) % 4][:],
                                                 ACT.Sigmoid).then_inc(gate_ready, 1)
                        consumed(n)
                        n += 1
                act.wait_ge(merge_step, seen.next(merge_step))
                for j in range(4):
                    if j >= 2:
                        consumed(n)
                        n += 1
                    nc.scalar.activation(hT_hi[:, j % 2], merged[:, 2 * j:2 * j + 2, :], ACT.Copy).then_inc(mhi_ready, 1)
                consumed(n)
                owed.append(n + 1)

            def ple(s, n0, bank0):
                act.wait_ge(xT_ready, seen.next(xT_ready))
                nc.scalar.activation(hT_hi[:, 0], acc[0][:].rearrange("p (k n) -> p k n", k=2),
                                     ACT.Copy).then_inc(xhi_ready, 1)
                for c in range(2):
                    consumed(n0 + 3 * c)
                    consumed(n0 + 3 * c + 1)
                    if c:
                        act.wait_ge(merge_step, seen.next(merge_step))
                    for t, dst in enumerate((gate, prod)):
                        last = nc.scalar.activation(dst[:], up[(bank0 + 4 * c + t) % 4][:], ACT.Sigmoid)
                    last.then_inc(gate_ready, 1)
                    if c == 0:
                        consumed(n0 + 2)
                owed.append(n0 + 5)

            bank = 0
            for s, n0 in zip(plan, first):
                if s[0] == "norm":
                    norm(s[1])
                elif s[0] == "ffn":
                    ffn(s, n0, bank)
                    bank = (bank + 2 * NCH) % 4
                elif s[0] == "conv":
                    conv(s, n0, bank)
                    bank = (bank + 12) % 4
                elif s[0] == "mla":
                    mla(s, n0, bank)
                    bank = (bank + 16) % 4
                elif s[0] == "sg":
                    sg(s, n0, bank)
                    bank = (bank + 12) % 4
                elif s[0] == "tables":
                    tables(s[1])
                elif s[0] == "mix":
                    mix(s, n0, bank)
                    bank = (bank + MIX_BANKS) % 4
                elif s[0] == "ple":
                    ple(s, n0, bank)
                    bank = (bank + 8) % 4
                elif s[0] == "final":
                    mean_squares()

        @block.vector
        def _(dve):
            seen = Seen()

            def step(ins):
                ins.then_inc(dve_step, 1)
                dve.wait_ge(dve_step, seen.next(dve_step))

            def split_lo(n):
                if n >= n_tiles:
                    return
                dve.wait_ge(hi_ready, seen.next(hi_ready))
                nc.vector.tensor_tensor(w_lo[n % RING][:], raw[n % RING][:], w_hi[n % RING][:].bitcast(F32),
                                        ALU.subtract).then_inc(lo_ready, 1)

            def consumed(n):
                dve.wait_ge(tile_used, seen.next(tile_used))
                split_lo(n + RING)

            def rsqrt(y, v):
                t = nwt[:, 0:y.shape[1]]
                step(nc.vector.tensor_single_scalar(t.bitcast(I32), v.bitcast(I32), 1, ALU.logical_shift_right))
                step(nc.vector.tensor_scalar(y.bitcast(I32), t.bitcast(I32), -1.0, RSQRT_MAGIC, ALU.mult, ALU.add))
                step(nc.vector.tensor_tensor(t, y, y, ALU.mult))
                step(nc.vector.tensor_tensor(t, t, v, ALU.mult))
                step(nc.vector.scalar_tensor_tensor(t, t, -10.0 / 3.0, t, ALU.add, ALU.mult))
                step(nc.vector.scalar_tensor_tensor(y, t, 5.0, y, ALU.add, ALU.mult))
                step(nc.vector.tensor_tensor(t, y, y, ALU.mult))
                step(nc.vector.scalar_tensor_tensor(t, t, -0.5 * 0.375 ** 3, v, ALU.mult, ALU.mult))
                step(nc.vector.scalar_tensor_tensor(y, t, 1.5 * 0.375, y, ALU.add, ALU.mult))

            def rsqrt_mean(y, sums, scale):
                v = nwv[:, 0:y.shape[1]]
                step(nc.vector.tensor_scalar(v, sums, scale, EPS, ALU.mult, ALU.add))
                rsqrt(y, v)

            def parts_lo(nk, row, dst=xT_lo, hi=xT_hi, same=None):
                for k in range(nk):
                    if k % 2 == 0:
                        dve.wait_ge(xhi_ready, seen.next(xhi_ready))
                    g = gains[:, k, row:row + 1] if same is None else same
                    last = nc.vector.scalar_tensor_tensor(
                        dst[:, k, :], acc[k // 2][:, (k % 2) * TOK:(k % 2 + 1) * TOK], g,
                        hi[:, k, :].bitcast(F32), ALU.mult, ALU.subtract)
                    if k % 2 or k == nk - 1:
                        last.then_inc(xlo_ready, 1)

            owed = []

            def settle():
                if owed:
                    split_lo(owed.pop() + RING)

            def row_scales():
                dve.wait_ge(ss_ready, seen.next(ss_ready, QUARTERS))
                halves = ss[:, 0:QUARTERS].rearrange("p (t h) -> p t h", h=2)
                v = nwv[:, 0:NT]
                step(nc.vector.scalar_tensor_tensor(v.rearrange("p (t o) -> p t o", o=1), halves[:, :, 0:1], EPS,
                                                    halves[:, :, 1:2], ALU.add, ALU.add))
                rsqrt(rstd[:, 0:NT], v)

            starting = [True]

            def norm(row):
                row_scales()
                if starting[0]:
                    dve.wait_ge(const_in, 16)
                for t in range(NT):
                    last = nc.vector.tensor_scalar(diag[:, t, :], ident, rstd[:, t:t + 1], None, ALU.mult)
                last.then_inc(diag_ready, 1)
                if starting[0]:
                    dve.wait_ge(setup_pe, seen.next(setup_pe))
                    nc.vector.tensor_copy(gains[:, :, 0:G_ROWS],
                                          up[3][:, 0:KD * G_ROWS].rearrange("p (k r) -> p k r", k=KD)).then_inc(setup_dve, 1)
                    dve.wait_ge(setup_dve, 1)
                    split_lo(0)
                parts_lo(KD, row)
                if starting[0]:
                    for n in range(1, RING):
                        split_lo(n)
                    starting[0] = False
                settle()

            def residual(scale):
                for t in range(NT):
                    for h in range(2):
                        cols = slice(512 * h, 512 * h + 512)
                        dve.wait_ge(acc_done, seen.next(acc_done))
                        nc.vector.scalar_tensor_tensor(x[:, t, cols], acc[2 * t + h][:], scale, x[:, t, cols],
                                                       ALU.mult, ALU.add).then_inc(x_ready, 1)
                dve.wait_ge(x_ready, seen.next(x_ready, QUARTERS))

            def product_parts(c):
                dve.wait_ge(hhi_ready, seen.next(hhi_ready))
                nc.vector.tensor_tensor(hT_lo[:, c % 2], prod[:].rearrange("p (k n) -> p k n", k=2),
                                        hT_hi[:, c % 2].bitcast(F32), ALU.subtract).then_inc(hlo_ready, 1)
                dve.wait_ge(hlo_ready, seen.next(hlo_ready))

            def ffn(s, n0, bank0):
                def chunk(n, c, down):
                    consumed(n)
                    consumed(n + 1)
                    dve.wait_ge(gate_ready, seen.next(gate_ready))
                    nc.vector.tensor_tensor(prod[:], gate[:], up[(bank0 + 2 * c + 1) % 4][:],
                                            ALU.mult).then_inc(prod_ready, 1)
                    dve.wait_ge(prod_ready, seen.next(prod_ready))
                    dve.sem_inc(bank_free, 2)
                    product_parts(c)
                    if down:
                        consumed(n + 2)

                chunk(n0, 0, False)
                chunk(n0 + 2, 1, True)
                with dve.Fori(0, 4) as i:
                    seen.enter(i, [(hi_ready, 6), (tile_used, 6), (gate_ready, 2), (prod_ready, 2), (hhi_ready, 2),
                                   (hlo_ready, 2)])
                    chunk(n0 + 5, 2, True)
                    chunk(n0 + 8, 3, True)
                    seen.leave(4)
                chunk(n0 + 29, 10, True)
                owed.append(n0 + 32)
                residual(0.5)

            def conv(s, n0, bank0):
                step(nc.vector.memset(zconv[:, :, 0:2], 0.0))
                for c in range(4):
                    n = n0 + 4 * c - (c > 0)
                    b = bank0 + 3 * c
                    consumed(n)
                    consumed(n + 1)
                    dve.wait_ge(gate_ready, seen.next(gate_ready))
                    step(nc.vector.tensor_tensor(zconv[:, :, 2:], gate[:].rearrange("p (k n) -> p k n", k=2),
                                                 up[(b + 1) % 4][:].rearrange("p (k n) -> p k n", k=2), ALU.mult))
                    dve.sem_inc(bank_free, 2)
                    for j in (2, 1, 0):
                        for m in range(2):
                            tap = gains[:, 2 * c + m, G_CONV + 3 * s[1] + j:G_CONV + 3 * s[1] + j + 1]
                            z = zconv[:, m, j:j + TOK]
                            if j == 2:
                                last = nc.vector.tensor_scalar(yconv[:, m, :], z, tap, None, ALU.mult)
                            else:
                                last = nc.vector.scalar_tensor_tensor(yconv[:, m, :], z, tap, yconv[:, m, :],
                                                                      ALU.mult, ALU.add)
                        step(last)
                    consumed(n + 2)
                    nc.vector.tensor_tensor(prod[:], yconv[:].rearrange("p k n -> p (k n)"), up[(b + 2) % 4][:],
                                            ALU.mult).then_inc(prod_ready, 1)
                    dve.wait_ge(prod_ready, seen.next(prod_ready))
                    dve.sem_inc(bank_free, 1)
                    product_parts(c)
                    if c:
                        consumed(n + 3)
                owed.append(n0 + 15)
                residual(1.0)

            def trig_arguments():
                posf, k = rsh[:, 0:NT], nwt[:, 0:32]
                dve.wait_ge(misc_in, seen.next(misc_in, 48))
                step(nc.vector.tensor_copy(posf, pos[:]))
                for t in range(NT):
                    last = nc.vector.tensor_scalar(sin[:, t, :], consts[:, C_FREQ:C_FREQ + 16], posf[:, t:t + 1], None,
                                                   ALU.mult)
                step(last)
                ang = sin[:].rearrange("p t f -> p (t f)")
                shifted = cos[:].rearrange("p t f -> p (t f)")
                big = 1.5 * 2.0 ** 23
                step(nc.vector.tensor_scalar(k, ang, 1.0 / (2 * np.pi), big, ALU.mult, ALU.add))
                step(nc.vector.tensor_scalar(k, k, big, None, ALU.subtract))
                for part in TWO_PI:
                    step(nc.vector.scalar_tensor_tensor(ang, k, -part, ang, ALU.mult, ALU.add))
                step(nc.vector.tensor_scalar(shifted, ang, np.pi / 2, None, ALU.add))
                step(nc.vector.tensor_scalar(k, shifted, np.pi, -2 * np.pi, ALU.is_gt, ALU.mult))
                step(nc.vector.tensor_tensor(shifted, shifted, k, ALU.add))
                step(nc.vector.tensor_scalar(shifted, shifted, PI_IN, -PI_IN, ALU.min, ALU.max))
                nc.vector.tensor_scalar(ang, ang, PI_IN, -PI_IN, ALU.min, ALU.max).then_inc(trig_arg, 1)

            def score_unit(u, scale, near, far, negsink=BIG):
                b = u % DEEP
                if u >= DEEP:
                    dve.wait_ge(turned, seen.next(turned))
                dve.wait_ge(scores_done, seen.next(scores_done))
                nc.vector.tensor_tensor_reduce(S[b][:, 0:256], acc[u % 2][:, 0:256], far, -scale, negsink, ALU.add, ALU.min,
                                               nmax[b][:, 1:2])
                nc.vector.tensor_tensor_reduce(S[b][:, 256:384], acc[u % 2][:, 256:384], near, -scale, negsink, ALU.add,
                                               ALU.min, nmax[b][:, 0:1]).then_inc(nmax_ready, 1)

            def row_sums(u, sink=False):
                b = u % DEEP
                dve.wait_ge(exp_ready, seen.next(exp_ready))
                if sink:
                    step(nc.vector.tensor_tensor(esum[b][:], esum[b][:], esink[b][:], ALU.add))
                nc.vector.reciprocal(rsum[b][:], esum[b][:]).then_inc(rsum_ready, 1)

            def rope(dst, src, w):
                def table(v):
                    if w is None:
                        return v
                    return v.rearrange("p t (o f) -> p t o f", o=1).broadcast_to([P, NT, w, 16])
                c, sn = table(cos[:]), table(sin[:])
                n = NT * (w or 1)
                tmp = [rtmp[:, i, 0:n, :] for i in range(4)]
                if w is not None:
                    tmp = [v.rearrange("p (t h) f -> p t h f", t=NT) for v in tmp]
                a1, a2 = src[..., 0:16], src[..., 16:32]
                nc.vector.tensor_tensor(tmp[0], a1, c, ALU.mult)
                nc.vector.tensor_tensor(tmp[1], a2, sn, ALU.mult)
                nc.vector.tensor_tensor(tmp[2], a2, c, ALU.mult)
                step(nc.vector.tensor_tensor(tmp[3], a1, sn, ALU.mult))
                nc.vector.tensor_tensor(dst[..., 0:16], tmp[0], tmp[1], ALU.subtract)
                step(nc.vector.tensor_tensor(dst[..., 16:32], tmp[2], tmp[3], ALU.add))

            def mla(s, n0, bank0):
                trig_arguments()
                consumed(n0)
                consumed(n0 + 1)
                for t in range(NT):
                    last = nc.vector.tensor_copy(latent[:, t, :], up[(bank0 + t) % 4][:, 0:QL + KVL + ROPE])
                step(last)
                dve.sem_inc(bank_free, NT)
                for t in range(NT):
                    nc.vector.tensor_tensor_reduce(cn[:, t, 0:QL], latent[:, t, 0:QL], latent[:, t, 0:QL], 1.0, 0.0,
                                                   ALU.mult, ALU.add, ssh[:, t:t + 1])
                    last = nc.vector.tensor_tensor_reduce(cn[:, t, QL:QL + KVL], latent[:, t, QL:QL + KVL],
                                                          latent[:, t, QL:QL + KVL], QL / KVL, 0.0,
                                                          ALU.mult, ALU.add, ssh[:, 2 + t:3 + t])
                step(last)
                rsqrt_mean(rsh[:, 0:4], ssh[:, 0:4], 1.0 / QL)
                for t in range(NT):
                    nc.vector.tensor_scalar(cn[:, t, 0:QL], latent[:, t, 0:QL], rsh[:, t:t + 1], None, ALU.mult)
                    nc.vector.tensor_scalar(cn[:, t, QL:], latent[:, t, QL:QL + KVL], rsh[:, 2 + t:3 + t], None,
                                            ALU.mult).then_inc(cn_ready, 1)
                parts_lo(3, G_MISC)
                pe_in = latent[:, :, QL + KVL:]
                nc.vector.tensor_tensor(rtmp[:, 0, 0:2, :].rearrange("p a b -> p (a b)"), pe_in[:, 0, :],
                                        pe_in[:, 0, :], ALU.mult)
                step(nc.vector.tensor_tensor(rtmp[:, 0, 2:4, :].rearrange("p a b -> p (a b)"), pe_in[:, 1, :],
                                             pe_in[:, 1, :], ALU.mult))
                step(nc.vector.tensor_reduce(ss[:, 4:6], rtmp[:, 0, 0:4, :].rearrange("p (t a) b -> p t (a b)", t=NT),
                                             AX.X, ALU.add))
                for t in range(NT):
                    last = nc.vector.tensor_tensor(kpe[:, t, :], pe_in[:, t, :], g96[:, 1, NOPE:], ALU.mult)
                step(last)
                dve.wait_ge(trig_done, seen.next(trig_done))
                rope(kpe, kpe, None)
                for i, (tile, groups) in enumerate(((n0 + 2, (0, 1)), (n0 + 3, (2,)))):
                    consumed(tile)
                    for g in groups:
                        for t in range(NT):
                            last = nc.vector.tensor_copy(arena[:, 1536 * t + 512 * g:1536 * t + 512 * g + 512],
                                                         up[(bank0 + 2 + 2 * g + t) % 4][:])
                    step(last)
                    dve.sem_inc(bank_free, NT * len(groups))
                dve.wait_ge(kv_copied, seen.next(kv_copied, 2))
                dve.sem_inc(bank_free, 4)
                consumed(n0 + 4)

                def flat(v):
                    return v.rearrange("p t h d -> p (t h) d")

                def over(v, n):
                    return v.rearrange("p (a o) -> p a o", o=1).broadcast_to([P, NT * MH, n])

                def gain(v, n):
                    return v.rearrange("p (o d) -> p o d", o=1).broadcast_to([P, NT * MH, n])

                step(nc.vector.tensor_tensor(squares, Q, Q, ALU.mult))
                step(nc.vector.tensor_reduce(ssh[:, 0:32], flat(squares), AX.X, ALU.add))
                dve.wait_ge(kv_copied, seen.next(kv_copied, 2))
                dve.sem_inc(bank_free, 4)
                kn = KV[:, :, :, 0:NOPE]
                step(nc.vector.tensor_tensor(squares[:, :, :, 0:NOPE], kn, kn, ALU.mult))
                step(nc.vector.tensor_reduce(ssh[:, 32:64], flat(squares)[:, :, 0:NOPE], AX.X, ALU.add))
                for t in range(NT):
                    last = nc.vector.tensor_scalar(ssh[:, 32 + MH * t:48 + MH * t], ssh[:, 32 + MH * t:48 + MH * t],
                                                   ss[:, 4 + t:5 + t], None, ALU.add)
                step(last)
                rsqrt_mean(rsh[:], ssh[:], 1.0 / QKH)
                nc.vector.tensor_tensor(flat(Q), flat(Q), over(rsh[:, 0:32], QKH), ALU.mult)
                nc.vector.tensor_tensor(flat(KF)[:, :, 0:NOPE], flat(KV)[:, :, 0:NOPE], over(rsh[:, 32:64], NOPE), ALU.mult)
                for t in range(NT):
                    last = nc.vector.tensor_tensor(
                        KF[:, t, :, NOPE:], kpe[:, t, :].rearrange("p (o d) -> p o d", o=1).broadcast_to([P, MH, ROPE]),
                        rsh[:, 32 + MH * t:48 + MH * t].rearrange("p (h o) -> p h o", o=1).broadcast_to([P, MH, ROPE]),
                        ALU.mult)
                step(last)
                nc.vector.tensor_tensor(flat(KF)[:, :, 0:NOPE], flat(KF)[:, :, 0:NOPE], gain(g96[:, 1, 0:NOPE], NOPE),
                                        ALU.mult)
                step(nc.vector.tensor_tensor(flat(Q), flat(Q), gain(g96[:, 0, :], QKH), ALU.mult))
                rope(Q[:, :, :, NOPE:], Q[:, :, :, NOPE:], MH)
                dve.sem_inc(qk_ready, 1)
                scale = float(QKH) ** -0.5
                far, near = consts[:, C_CAUSAL:C_CAUSAL + 256], consts[:, C_CAUSAL + 128:C_CAUSAL + 256]

                def o_lo(j):
                    dve.wait_ge(ohi_ready, seen.next(ohi_ready))
                    nc.vector.tensor_tensor(xT_lo[:, j, :], up[2 + j % 2][:, 0:TOK],
                                            xT_hi[:, j, :].bitcast(F32), ALU.subtract).then_inc(olo_ready, 1)
                    dve.wait_ge(olo_ready, seen.next(olo_ready))

                for i in range(MH + 7):
                    if i < MH:
                        dve.wait_ge(headT_done, seen.next(headT_done))
                        nc.vector.tensor_copy(headT[i % 2][0:QKH, :], up[i % 2][0:QKH, :]).then_inc(headT_ready, 1)
                    if 0 <= i - 1 < MH:
                        score_unit(i - 1, scale, near, far)
                    if 0 <= i - 2 < MH:
                        row_sums(i - 2)
                    if 0 <= i - 6 < MH and (i - 6) % 2:
                        o_lo((i - 6) // 2)
                dve.wait_ge(turned, seen.next(turned, DEEP))
                for j in range(3):
                    consumed(n0 + 5 + j)
                owed.append(n0 + 8)
                residual(1.0)

            def sg(s, n0, bank0):
                for h in range(2):
                    dve.wait_ge(ws_turned, seen.next(ws_turned))
                    last = nc.vector.tensor_tensor(
                        wsT[:, 4 * h:4 * h + 4, :], acc[h][:].rearrange("p (g t) -> p g t", g=4),
                        consts[:, C_LOWT:C_LOWT + P].rearrange("p (o t) -> p o t", o=1).broadcast_to([P, 4, P]),
                        ALU.mult)
                last.then_inc(ws_ready, 1)
                for g in range(2):
                    consumed(n0 + 2 * g)
                    consumed(n0 + 2 * g + 1)
                    dve.wait_ge(v_ready, seen.next(v_ready))
                    dve.sem_inc(bank_free, NT)
                    for t in range(NT):
                        last = nc.vector.tensor_tensor_reduce(prod[:], xn[:, t, 512 * g:512 * g + 512],
                                                              xn[:, t, 512 * g:512 * g + 512], 1.0, 0.0, ALU.mult,
                                                              ALU.add, ssh[:, 2 * g + t:2 * g + t + 1])
                        step(last)
                step(nc.vector.tensor_tensor(ssh[:, 0:2], ssh[:, 0:2], ssh[:, 2:4], ALU.add))
                rsqrt_mean(rsh[:, 0:2], ssh[:, 0:2], 1.0 / D)
                for t in range(NT):
                    last = nc.vector.tensor_scalar(xn[:, t, :], xn[:, t, :], rsh[:, t:t + 1], None, ALU.mult)
                last.then_inc(vn_ready, 1)
                for c in range(4):
                    n = n0 + 4 + 2 * c - (c > 0)
                    consumed(n)
                    dve.wait_ge(mix_done, seen.next(mix_done))
                    dve.wait_ge(gate_ready, seen.next(gate_ready))
                    ps = up[(bank0 + 5 + 2 * c) % 4]
                    for m in range(2):
                        g = 2 * c + m
                        for t in range(NT):
                            last = nc.vector.scalar_tensor_tensor(
                                mixed[:, m, t * P:(t + 1) * P], ps[:, m * TOK + t * P:m * TOK + (t + 1) * P],
                                gains[:, g, G_SGV:G_SGV + 1], sgb[:, g * P:(g + 1) * P], ALU.mult, ALU.add)
                    step(last)
                    dve.sem_inc(bank_free, 2)
                    nc.vector.tensor_tensor(prod[:], gate[:], mixed.rearrange("p m t -> p (m t)"),
                                            ALU.mult).then_inc(prod_ready, 1)
                    dve.wait_ge(prod_ready, seen.next(prod_ready))
                    product_parts(c)
                    if c:
                        consumed(n + 1)
                owed.append(n0 + 11)
                residual(1.0)

            def tables(part):
                settle()
                if part == 0:
                    nc.vector.memset(relb, NEG).then_inc(arena_free, 1)
                    return
                if part == 2:
                    flipped_tables()
                    return
                dve.wait_ge(tables_in, seen.next(tables_in, 16 * 8))
                for i in range(2):
                    for j in range(2):
                        last = nc.vector.tensor_tensor_reduce(nwt[:], lp[:, i, 2 * j, :], lp[:, i, 2 * j + 1, :], 1.0, 0.0,
                                                              ALU.mult, ALU.add, ssh[:, 2 * i + j:2 * i + j + 1])
                        step(last)
                    step(nc.vector.tensor_scalar(subln[:, i:i + 1], gains[:, 3 + i, G_MISC:G_MISC + 1],
                                                 1.0 - LAM_INIT[i], None, ALU.mult))
                nc.vector.tensor_scalar(negsinks[:], sinks[:], -1.0, None, ALU.mult).then_inc(tab_dve, 1)
                dve.wait_ge(tab_dve, seen.next(tab_dve))
                dve.wait_ge(tab_pe, seen.next(tab_pe))
                nc.vector.tensor_copy(rv[0:12, 0, :], acc[0][0:12, 0:384])
                nc.vector.tensor_copy(rv[0:8, 1, :], acc[1][0:8, 0:384]).then_inc(rv_ready, 1)
                nc.vector.tensor_copy(pos2[:].rearrange("p i v j -> p (i v j)"), acc[2][:, 0:64])
                step(nc.vector.tensor_scalar(TC, acc[3][:, 0:240].rearrange("p (n h) -> p h n", h=8), 1.0 / HSCALE, None,
                                             ALU.mult))
                dve.sem_inc(tab_dve, 1)
                dve.wait_ge(tab_dve, seen.next(tab_dve))
                dve.wait_ge(tab_act, seen.next(tab_act))
                for i in range(2):
                    step(nc.vector.tensor_tensor(neglam[:, i:i + 1], ssh[:, 5 + 2 * i:6 + 2 * i], ssh[:, 4 + 2 * i:5 + 2 * i],
                                                 ALU.subtract))
                    step(nc.vector.tensor_scalar(neglam[:, i:i + 1], neglam[:, i:i + 1], -LAM_INIT[i], None, ALU.add))

            def flipped_tables():
                for g in range(10):
                    dve.wait_ge(tab_pe, seen.next(tab_pe))
                    nc.vector.tensor_scalar(T[:, 2 * g:2 * g + 2, :].rearrange("p h j -> p (h j)"), acc[g % 4][:],
                                            1.0 / HSCALE, None, ALU.mult).then_inc(tab_dve, 1)
                    dve.wait_ge(tab_dve, seen.next(tab_dve))

            def mix(s, n0, bank0):
                n = n0
                bank = [bank0]

                def out(dst):
                    step(nc.vector.tensor_copy(dst, up[bank[0] % 4][:]))
                    bank[0] += 1
                    dve.sem_inc(bank_free, 1)

                def flat(v):
                    return v.rearrange("p k n -> p (k n)")

                consumed(n)
                out(flat(KC))
                dve.sem_inc(kc_ready, 1)
                for j, dst in enumerate((AQ, AQ, AK, AK)):
                    consumed(n + 1 + j)
                    out(flat(dst[:, 2 * (j % 2):2 * (j % 2) + 2, :]))
                consumed(n + 5)
                consumed(n + 6)
                for t in range(NT):
                    out(AV[:, t, :])
                dve.wait_ge(kc2_in, seen.next(kc2_in, 16 * 8))
                for v in range(2):
                    for j in range(16):
                        last = nc.vector.tensor_scalar(
                            blk[:, v, j, :].rearrange("p (g b) -> p g b", g=2),
                            KC2[:, v, :, 2 * j:2 * j + 16 * (NCMP - 1) + 1:16], pos2[:, s[1], v, j:j + 1], None, ALU.add)
                    last.then_inc(blk_ready, 1)
                    dve.wait_ge(blkhi_ready, seen.next(blkhi_ready))
                    nc.vector.tensor_tensor(blk_lo[:, v], blk[:, v], blk_hi[:, v].bitcast(F32),
                                            ALU.subtract).then_inc(blklo_ready, 1)
                n += 7
                for j in range(2):
                    consumed(n + j)
                    out(flat(BQ[:, 2 * j:2 * j + 2, :]))
                consumed(n + 2)
                out(BS)
                consumed(n + 3)
                out(BW)
                consumed(n + 4)
                dve.wait_ge(gates_ready, seen.next(gates_ready))
                bank[0] += 1
                dve.sem_inc(bank_free, 1)
                n += 5
                for v in range(2):
                    consumed(n)
                    consumed(n + 1)
                    n += 2
                    dve.wait_ge(hid_ready, seen.next(hid_ready))
                    bank[0] += 2
                    dve.sem_inc(bank_free, 2)
                dve.wait_ge(cmp_done, seen.next(cmp_done))
                nc.vector.tensor_copy(kcT, up[bank[0] % 4][:, 0:2 * NCMP])
                bank[0] += 1
                step(nc.vector.tensor_copy(vc, up[bank[0] % 4][0:NCMP, 0:128]))
                bank[0] += 1
                dve.sem_inc(bank_free, 2)
                for j in range(2):
                    consumed(n + j)
                    out(flat(CQ[:, 2 * j:2 * j + 2, :]))
                consumed(n + 2)
                out(CKV)
                n += 3
                dve.sem_inc(proj_ready, 1)
                scale = HSCALE
                for br in range(3):
                    units = branch_units(br)
                    for i in range(len(units) + 5):
                        if i < len(units):
                            kind, h = units[i][:2]
                            if kind == "cmp":
                                score_cmp(i, scale, TC[:, h, :])
                            else:
                                tab = T[:, (0, 4, 12)[br] + h, :]
                                at = 8 * s[1] + h
                                score_unit(i, scale, tab[:, 128:256], tab, negsinks[:, at:at + 1] if br == 2 else BIG)
                        if 0 <= i - 1 < len(units):
                            row_sums(i - 1, sink=br == 2)
                        if 0 <= i - 5 < len(units) and units[i - 5][2]:
                            h = units[i - 5][1]
                            if br == 0:
                                dve.wait_ge(oa_done, seen.next(oa_done))
                                for t in range(NT):
                                    last = nc.vector.tensor_copy(YA[:, t, P * h:P * h + P], up[2 * (h % 2) + t][:, 0:P])
                                last.then_inc(ya_copied, 1)
                                dve.wait_ge(ya_copied, seen.next(ya_copied))
                            else:
                                j = h // 2
                                dve.wait_ge(ohi_ready, seen.next(ohi_ready))
                                nc.vector.tensor_tensor(yT_lo[:, j, :], up[2 + j % 2][:, 0:TOK],
                                                        yT_hi[:, j, :].bitcast(F32), ALU.subtract).then_inc(olo_ready, 1)
                    dve.wait_ge(turned, seen.next(turned, DEEP))
                    if br == 0:
                        ya = YA.rearrange("p t (h e) -> p (t h) e", h=4)
                        sq = carve(5376, 8, P)
                        step(nc.vector.tensor_tensor(sq, ya, ya, ALU.mult))
                        step(nc.vector.tensor_reduce(ssh[:, 0:8], sq, AX.X, ALU.add))
                        rsqrt_mean(rsh[:, 0:8], ssh[:, 0:8], 1.0 / P)
                        step(nc.vector.tensor_tensor(ya, ya, rsh[:, 0:8].rearrange("p (a o) -> p a o", o=1)
                                                     .broadcast_to([P, 8, P]), ALU.mult))
                        dve.sem_inc(ya_ready, NT)
                        parts_lo(4, 0, yT_lo, yT_hi, subln[:, s[1]:s[1] + 1])
                    for c in range(2):
                        b = bank0 + 21 + 8 * br + 4 * c
                        for j in range(2):
                            consumed(n)
                            n += 1
                            dve.wait_ge(gate_ready, seen.next(gate_ready))
                            dve.sem_inc(bank_free, 1)
                        consumed(n)
                        n += 1
                        for j, g in enumerate((gate, prod)):
                            dst = flat(merged[:, 4 * c + 2 * j:4 * c + 2 * j + 2, :])
                            ps = up[(b + 2 + j) % 4][:]
                            if br == 0:
                                step(nc.vector.tensor_tensor(dst, g[:], ps, ALU.mult))
                            else:
                                step(nc.vector.tensor_tensor(g[:], g[:], ps, ALU.mult))
                            dve.sem_inc(bank_free, 1)
                            if br:
                                step(nc.vector.tensor_tensor(dst, dst, g[:], ALU.add))
                        dve.sem_inc(merge_step, 1)
                for j in range(4):
                    if j >= 2:
                        consumed(n)
                        n += 1
                    dve.wait_ge(mhi_ready, seen.next(mhi_ready))
                    nc.vector.tensor_tensor(hT_lo[:, j % 2], merged[:, 2 * j:2 * j + 2, :], hT_hi[:, j % 2].bitcast(F32),
                                            ALU.subtract).then_inc(mlo_ready, 1)
                consumed(n)
                owed.append(n + 1)
                residual(1.0)

            def score_cmp(u, scale, tab):
                b = u % DEEP
                if u >= DEEP:
                    dve.wait_ge(turned, seen.next(turned))
                dve.wait_ge(scores_done, seen.next(scores_done))
                for t in range(NT):
                    cols = slice(NCMP * t, NCMP * t + NCMP)
                    last = nc.vector.tensor_tensor_reduce(S[b][:, cols], acc[u % 2][:, cols], tab[:, cols], -scale, BIG,
                                                          ALU.add, ALU.min, nmax[b][:, t:t + 1])
                last.then_inc(nmax_ready, 1)

            def ple(s, n0, bank0):
                dve.wait_ge(xhi_ready, seen.next(xhi_ready))
                nc.vector.tensor_tensor(hT_lo[:, 0], acc[0][:].rearrange("p (k n) -> p k n", k=2),
                                        hT_hi[:, 0].bitcast(F32), ALU.subtract).then_inc(xlo_ready, 1)
                for c in range(2):
                    consumed(n0 + 3 * c)
                    consumed(n0 + 3 * c + 1)
                    dve.wait_ge(gate_ready, seen.next(gate_ready))
                    dve.sem_inc(bank_free, 2)
                    if c == 0:
                        consumed(n0 + 2)
                    for t, g in enumerate((gate, prod)):
                        if c:
                            dve.wait_ge(acc_done, seen.next(acc_done, QUARTERS // NT))
                        step(nc.vector.tensor_tensor(g[:], g[:], up[(bank0 + 4 * c + 2 + t) % 4][:], ALU.mult))
                        dve.sem_inc(bank_free, 1)
                        cols = slice(512 * c, 512 * c + 512)
                        nc.vector.tensor_tensor(x[:, t, cols], x[:, t, cols], g[:], ALU.add).then_inc(ple_added, 1)
                        dve.wait_ge(ple_added, seen.next(ple_added))
                        if c:
                            dve.sem_inc(x_ready, QUARTERS // NT)
                    if c == 0:
                        dve.sem_inc(merge_step, 1)
                owed.append(n0 + 5)
                dve.wait_ge(x_ready, seen.next(x_ready, QUARTERS))

            def final():
                row_scales()
                dve.wait_ge(fin_in, seen.next(fin_in, 16))
                for t in range(NT):
                    last = nc.vector.scalar_tensor_tensor(xn[:, t, :], x[:, t, :], rstd[:, t:t + 1], gfin, ALU.mult,
                                                          ALU.mult)
                last.then_inc(fin_ready, 1)

            nc.vector.memset(g_rows, 0.0).then_inc(rows_clear, 1)
            dve.wait_ge(x_in, 16)
            dve.sem_inc(x_ready, QUARTERS)
            dve.wait_ge(x_ready, seen.next(x_ready, QUARTERS))
            bank = 0
            for s, n0 in zip(plan, first):
                if s[0] == "norm":
                    norm(s[1])
                elif s[0] == "ffn":
                    ffn(s, n0, bank)
                    bank = (bank + 2 * NCH) % 4
                elif s[0] == "conv":
                    conv(s, n0, bank)
                    bank = (bank + 12) % 4
                elif s[0] == "mla":
                    mla(s, n0, bank)
                    bank = (bank + 16) % 4
                elif s[0] == "sg":
                    sg(s, n0, bank)
                    bank = (bank + 12) % 4
                elif s[0] == "tables":
                    tables(s[1])
                elif s[0] == "mix":
                    mix(s, n0, bank)
                    bank = (bank + MIX_BANKS) % 4
                elif s[0] == "ple":
                    ple(s, n0, bank)
                    bank = (bank + 8) % 4
                elif s[0] == "final":
                    final()

        @block.tensor
        def _(pe):
            seen = Seen()
            banks, credit, pairs_to_come = [0], [4], [0]
            residuals = [0]

            def matmul3(ps, lh, ll, rh, rl, start, stop):
                pe.matmul(ps, lh, rh, start=start, stop=False)
                pe.matmul(ps, lh, rl, start=False, stop=False)
                return pe.matmul(ps, ll, rh, start=False, stop=stop)

            def take_bank():
                if credit[0]:
                    credit[0] -= 1
                else:
                    pe.wait_ge(bank_free, seen.next(bank_free))
                banks[0] += 1
                return (banks[0] - 1) % 4

            def drain_banks():
                pe.wait_ge(bank_free, seen.next(bank_free, 4 - credit[0]))
                credit[0] = 4

            def up_matmuls(n, b):
                wh, wl = tview(w_hi[n % RING], KD, CW), tview(w_lo[n % RING], KD, CW)
                for m in range(2):
                    for k in range(KD):
                        if k % 2 == 0:
                            next_pair()
                        last = matmul3(up[b][:, m * TOK:(m + 1) * TOK], wh[:, k, m * P:(m + 1) * P],
                                       wl[:, k, m * P:(m + 1) * P], xT_hi[:, k, :], xT_lo[:, k, :],
                                       k == 0, k == KD - 1)
                last.then_inc(tile_used, 1)

            def down_matmuls(n, lh, ll, start, stop):
                wh, wl = tview(w_hi[n % RING], 2, D), tview(w_lo[n % RING], 2, D)
                for t in range(NT):
                    for h in range(2):
                        for k in range(2):
                            cols = slice(512 * h, 512 * h + 512)
                            last = matmul3(acc[2 * t + h][:], lh[:, k, t * P:(t + 1) * P], ll[:, k, t * P:(t + 1) * P],
                                           wh[:, k, cols], wl[:, k, cols], start and k == 0, stop and k == 1)
                        if stop:
                            last.then_inc(acc_done, 1)
                if not stop:
                    last.then_inc(tile_used, 1)

            def turn(src, nk, ready):
                for t in range(NT):
                    pe.wait_ge(ready, seen.next(ready))
                    for k in range(nk):
                        last = pe.transpose(acc[k // 2][:, (k % 2) * TOK + t * P:(k % 2) * TOK + (t + 1) * P],
                                            src[:, t, k * P:(k + 1) * P], ident)
                        if t == NT - 1 and (k % 2 or k == nk - 1):
                            last.then_inc(xT_ready, 1)

            def keep_clock(n):
                drain_banks()
                for _ in range(n):
                    pe.matmul(up[banks[0] % 4][:, 0:P], ident, ident, start=True, stop=True)

            def turn_norm():
                keep_clock(NORM_FILL)
                pe.wait_ge(diag_ready, seen.next(diag_ready))
                for k in range(KD):
                    for t in range(NT):
                        last = pe.matmul(acc[k // 2][:, (k % 2) * TOK + t * P:(k % 2) * TOK + (t + 1) * P],
                                         x[:, t, k * P:(k + 1) * P], diag[:, t, :], start=True, stop=True)
                    if k % 2:
                        last.then_inc(xT_ready, 1)
                pairs_to_come[0] = KD // 2

            def next_pair():
                if pairs_to_come[0]:
                    pe.wait_ge(xlo_ready, seen.next(xlo_ready))
                    pairs_to_come[0] -= 1

            def token_matmuls(n, nk, ncol, col, width, k0, ps, start, stop):
                wh, wl = tview(w_hi[n % RING], nk, ncol), tview(w_lo[n % RING], nk, ncol)
                for t in range(NT):
                    for k in range(nk):
                        if k % 2 == 0:
                            next_pair()
                        last = matmul3(ps[t], xT_hi[:, k0 + k, t * P:(t + 1) * P], xT_lo[:, k0 + k, t * P:(t + 1) * P],
                                       wh[:, k, col:col + width], wl[:, k, col:col + width],
                                       start and k == 0, stop and k == nk - 1)
                return last

            def ups(n, wait=True):
                pe.wait_ge(lo_ready, seen.next(lo_ready))
                up_matmuls(n, take_bank())

            def down(n, c, start, stop):
                pe.wait_ge(lo_ready, seen.next(lo_ready))
                pe.wait_ge(hlo_ready, seen.next(hlo_ready))
                down_matmuls(n, hT_hi[:, c % 2], hT_lo[:, c % 2], start, stop)

            def conv(s, n0):
                n = n0
                for c in range(4):
                    for _ in range(3):
                        ups(n)
                        n += 1
                    if c:
                        down(n, c - 1, c == 1, False)
                        n += 1
                down(n, 3, False, True)

            def scores(u, q, k):
                if u >= 2:
                    pe.wait_ge(nmax_ready, seen.next(nmax_ready))
                ps = acc[u % 2]
                pe.matmul(ps[:, 0:256], q[:, P:TOK], k, start=True, stop=True)
                pe.matmul(ps[:, 256:384], q[:, 0:P], k[:, 0:P], start=True, stop=True).then_inc(scores_done, 1)

            def turn_unit(u):
                pe.wait_ge(p_ready, seen.next(p_ready))
                b, ps = u % DEEP, acc[2 + u % 2]
                pe.transpose(ps[:, 0:P], S[b][:, 256:384], ident)
                pe.transpose(ps[:, P:2 * P], S[b][:, 0:P], ident)
                pe.transpose(ps[:, 2 * P:3 * P], S[b][:, P:2 * P], ident).then_inc(turned, 1)

            def mla(s, n0):
                ps = [up[take_bank()][:, 0:QL + KVL + ROPE] for _ in range(NT)]
                for h in range(2):
                    pe.wait_ge(lo_ready, seen.next(lo_ready))
                    token_matmuls(n0 + h, 4, QL + KVL + ROPE, 0, QL + KVL + ROPE, 4 * h, ps, h == 0, h == 1
                                  ).then_inc(tile_used, 1)
                turn(cn, 3, cn_ready)
                pe.wait_ge(xlo_ready, seen.next(xlo_ready, 2))
                for tile, groups in ((n0 + 2, 2), (n0 + 3, 1)):
                    pe.wait_ge(lo_ready, seen.next(lo_ready))
                    for g in range(groups):
                        ps = [up[take_bank()][:] for _ in range(NT)]
                        last = token_matmuls(tile, 2, 512 * groups, 512 * g, 512, 0, ps, True, True)
                    last.then_inc(tile_used, 1)
                pe.wait_ge(lo_ready, seen.next(lo_ready))
                for g in range(4):
                    ps = [up[take_bank()][:] for _ in range(NT)]
                    last = token_matmuls(n0 + 4, 1, 2048, 512 * g, 512, 2, ps, True, True)
                    last.then_inc(group_done if g < 3 else tile_used, 1)
                pe.wait_ge(qk_ready, seen.next(qk_ready))
                drain_banks()
                def turn_head(h):
                    b = h % 2
                    for i, v in enumerate((Q, KF)):
                        for t in range(NT):
                            last = pe.transpose(up[b][0:QKH, i * TOK + t * P:i * TOK + (t + 1) * P], v[:, t, h, :], ident)
                    last.then_inc(headT_done, 1)

                def values(h):
                    if h % 2 == 0 and h >= 4:
                        pe.wait_ge(olo_ready, seen.next(olo_ready))
                    ps = up[2 + h // 2 % 2][64 * (h % 2):64 * (h % 2) + VH, 0:TOK]
                    pe.wait_ge(pt_ready, seen.next(pt_ready))
                    pe.matmul(ps, KV[:, 0, h, NOPE:], PT[h % 2][:, 0:256], start=True, stop=False)
                    last = pe.matmul(ps[:, P:TOK], KV[:, 1, h, NOPE:], PT[h % 2][:, 256:384], start=False, stop=True)
                    if h % 2:
                        last.then_inc(o_done, 1)

                for i in range(MH + 5):
                    if i < MH:
                        turn_head(i)
                    if 0 <= i - 1 < MH:
                        pe.wait_ge(headT_ready, seen.next(headT_ready))
                        scores(i - 1, headT[(i - 1) % 2][0:QKH, 0:TOK], headT[(i - 1) % 2][0:QKH, TOK:2 * TOK])
                    if 0 <= i - 4 < MH:
                        turn_unit(i - 4)
                    if 0 <= i - 5 < MH:
                        values(i - 5)
                pe.wait_ge(nmax_ready, seen.next(nmax_ready, 2))
                pe.wait_ge(olo_ready, seen.next(olo_ready, 2))
                for j in range(4):
                    pe.wait_ge(lo_ready, seen.next(lo_ready))
                    down_matmuls(n0 + 5 + j, xT_hi[:, 2 * j:2 * j + 2], xT_lo[:, 2 * j:2 * j + 2], j == 0, j == 3)

            def sg(s, n0):
                pe.wait_ge(ws_in, seen.next(ws_in, 32))
                for _ in range(KD // 2):
                    next_pair()
                for g in range(8):
                    last = pe.transpose(acc[g // 4][:, (g % 4) * P:(g % 4 + 1) * P], wsr[:, g, :], ident)
                    if g % 4 == 3:
                        last.then_inc(ws_turned, 1)
                for g in range(2):
                    ps = [up[take_bank()][:] for _ in range(NT)]
                    for h in range(2):
                        pe.wait_ge(lo_ready, seen.next(lo_ready))
                        token_matmuls(n0 + 2 * g + h, 4, 512, 0, 512, 4 * h, ps, h == 0, h == 1).then_inc(tile_used, 1)
                pe.wait_ge(ws_ready, seen.next(ws_ready))
                n = n0 + 4
                for c in range(4):
                    ups(n)
                    n += 1
                    if c == 0:
                        pe.wait_ge(vn_ready, seen.next(vn_ready))
                    b = take_bank()
                    for m in range(2):
                        g = 2 * c + m
                        for t in range(NT):
                            last = pe.matmul(up[b][:, m * TOK + t * P:m * TOK + (t + 1) * P],
                                             xn[:, t, g * P:(g + 1) * P], wsT[:, g, :], start=True, stop=True)
                    last.then_inc(mix_done, 1)
                    if c:
                        down(n, c - 1, c == 1, False)
                        n += 1
                down(n, 3, False, True)

            def ffn(s, n0):
                def gate_up(n, c, b, loop=False):
                    for j in range(2):
                        pe.wait_ge(lo_ready, seen.next(lo_ready))
                        if loop:
                            pe.wait_ge(bank_free, seen.next(bank_free))
                        else:
                            assert take_bank() == (b + j) % 4
                        up_matmuls(n + j, (b + j) % 4)

                b = banks[0] % 4
                gate_up(n0, 0, b)
                gate_up(n0 + 2, 1, b + 2)
                down(n0 + 4, 0, True, False)
                with pe.Fori(0, 4) as i:
                    seen.enter(i, [(lo_ready, 6), (bank_free, 4), (hlo_ready, 2)])
                    gate_up(n0 + 5, 2, b, True)
                    down(n0 + 7, 1, False, False)
                    gate_up(n0 + 8, 3, b + 2, True)
                    down(n0 + 10, 2, False, False)
                    seen.leave(4)
                banks[0] += 16
                gate_up(n0 + 29, 10, b)
                down(n0 + 31, 9, False, False)
                down(n0 + 32, 10, False, True)

            def tables(part):
                if part == 0:
                    return
                if part == 2:
                    flipped_tables()
                    return
                pe.wait_ge(tables_in, seen.next(tables_in, 16 * 8))
                pe.wait_ge(tab_dve, seen.next(tab_dve))
                pe.matmul(acc[0][0:12, 0:384], relb[:, 0:12], one_hots[:, 0:384], start=True, stop=True)
                pe.matmul(acc[1][0:8, 0:384], relb[:, 12:20], one_hots[:, 384:768], start=True,
                          stop=True)
                pe.transpose(acc[2][:, 0:64], prows, ident[0:64, 0:64])
                for t in range(NT):
                    for b in range(NCMP):
                        at = C_OHF - C_KEPT + 256 + P * t - 16 * b - 31
                        i = NCMP * t + b
                        last = pe.matmul(acc[3][:, 8 * i:8 * i + 8], one_hots[:, at:at + P], relb[:, 4:12], start=True,
                                         stop=True)
                last.then_inc(tab_pe, 1)
                pe.wait_ge(tab_dve, seen.next(tab_dve))

            def flipped_tables():
                pe.wait_ge(u_in, seen.next(u_in, 16))
                pe.wait_ge(x_ready, QUARTERS * (1 + residuals[0]))
                for g in range(10):
                    if g >= 4:
                        pe.wait_ge(tab_dve, seen.next(tab_dve))
                    pe.matmul(acc[g % 4][:], consts[:, C_FLIP:C_FLIP + P],
                              U[:, 2 * g:2 * g + 2, :].rearrange("p h j -> p (h j)"), start=True,
                              stop=True).then_inc(tab_pe, 1)
                pe.wait_ge(tab_dve, seen.next(tab_dve, 4))

            def mix(s, n0):
                n = n0
                for _ in range(5):
                    ups(n)
                    n += 1
                ps = [up[take_bank()][:] for _ in range(NT)]
                for h in range(2):
                    pe.wait_ge(lo_ready, seen.next(lo_ready))
                    token_matmuls(n, 4, 512, 0, 512, 4 * h, ps, h == 0, h == 1).then_inc(tile_used, 1)
                    n += 1
                ups(n)
                ups(n + 1)
                n += 2

                def key_value(n):
                    pe.wait_ge(lo_ready, seen.next(lo_ready))
                    ps = up[take_bank()]
                    wh, wl = tview(w_hi[n % RING], KD, CW), tview(w_lo[n % RING], KD, CW)
                    for k in range(KD):
                        matmul3(ps[:, 0:TOK], wh[:, k, 0:P], wl[:, k, 0:P], xT_hi[:, k, :], xT_lo[:, k, :],
                                k == 0, k == KD - 1)
                    token_matmuls(n, KD, CW, P, P, 0, [ps[:, TOK:TOK + P], ps[:, TOK + P:2 * TOK]], True, True
                                  ).then_inc(tile_used, 1)

                key_value(n)
                key_value(n + 1)
                n += 2
                pe.wait_ge(lo_ready, seen.next(lo_ready))
                ps = up[take_bank()]
                token_matmuls(n, KD, 24, 0, 24, 0, [ps[:, 0:24], ps[:, 24:48]], True, True).then_inc(tile_used, 1)
                n += 1
                for v in range(2):
                    pe.wait_ge(blklo_ready, seen.next(blklo_ready))
                    banks2 = [up[take_bank()] for _ in range(2)]
                    for h in range(2):
                        pe.wait_ge(lo_ready, seen.next(lo_ready))
                        wh, wl = tview(w_hi[n % RING], KD, CW), tview(w_lo[n % RING], KD, CW)
                        for m in range(2):
                            for k in range(KD):
                                last = matmul3(banks2[m][:, 0:2 * NCMP], wh[:, k, m * P:(m + 1) * P],
                                               wl[:, k, m * P:(m + 1) * P], blk_hi[:, v, 8 * h + k, :],
                                               blk_lo[:, v, 8 * h + k, :], h == 0 and k == 0, h == 1 and k == KD - 1)
                        last.then_inc(tile_used, 1)
                        n += 1
                pe.wait_ge(hid_ready, seen.next(hid_ready, 2))
                if s[1] == 0:
                    pe.wait_ge(w2_in, seen.next(w2_in, 64))
                kb, vb = up[take_bank()], up[take_bank()]
                for base in (0, 64):
                    for m in range(2):
                        pe.matmul(kb[base:base + 64, 0:2 * NCMP], w2[:, s[1], 0, m, :], hidT[:, 0, m, :], start=m == 0,
                                  stop=m == 1)
                for g in range(2):
                    for m in range(2):
                        last = pe.matmul(vb[0:NCMP, 64 * g:64 * g + 64], hidT[:, 1, m, NCMP * g:NCMP * g + NCMP],
                                         w2[:, s[1], 1, m, :], start=m == 0, stop=m == 1)
                last.then_inc(cmp_done, 1)
                ups(n)
                ups(n + 1)
                key_value(n + 2)
                n += 3
                pe.wait_ge(proj_ready, seen.next(proj_ready))

                def operands(br, kind, h):
                    g, r = h // 4, h % 4
                    rows = slice(64 * g, 64 * g + 64)
                    if br == 0:
                        rows = slice(64 * kind, 64 * kind + 64)
                        return AQ[rows, h, :], AK[rows, h, :]
                    if br == 2:
                        return CQ[rows, r, :], CKV[rows, 0:TOK]
                    q = BQ[rows, r, :]
                    if kind == "cmp":
                        return q, kcT[rows, NCMP * g:NCMP * g + NCMP]
                    return q, (BS if kind == "sel" else BW)[rows, 0:TOK]

                def values_a(u, c, h):
                    pe.wait_ge(pt_ready, seen.next(pt_ready))
                    if c == 0 and h >= 2:
                        pe.wait_ge(ya_copied, seen.next(ya_copied))
                    o = [up[2 * (h % 2) + t][:, 0:P] for t in range(NT)]
                    cols = slice(P * h, P * h + P)
                    pe.matmul(o[0], PT[u % 2][:, 0:P], AV[:, 0, cols], start=c == 0, stop=c == 1)
                    pe.matmul(o[1], PT[u % 2][:, P:2 * P], AV[:, 0, cols], start=c == 0, stop=False)
                    last = pe.matmul(o[1], PT[u % 2][:, 2 * P:3 * P], AV[:, 1, cols], start=False, stop=c == 1)
                    if c == 1:
                        last.then_inc(oa_done, 1)

                def values_bc(u, br, kind, h, ends):
                    pe.wait_ge(pt_ready, seen.next(pt_ready))
                    starts = kind == "sel" or br == 2
                    stops = kind == "cmp" or br == 2
                    if starts and h % 2 == 0 and h >= 4:
                        pe.wait_ge(olo_ready, seen.next(olo_ready))
                    g = h // 4
                    o = up[2 + h // 2 % 2][64 * (h % 2):64 * (h % 2) + 64, 0:TOK]
                    cols = slice(TOK + 64 * g, TOK + 64 * g + 64)
                    cols1 = slice(TOK + P + 64 * g, TOK + P + 64 * g + 64)
                    if kind == "cmp":
                        last = pe.matmul(o, vc[:, 64 * g:64 * g + 64], PT[u % 2][0:NCMP, 0:TOK], start=False, stop=True)
                    else:
                        kv = CKV if br == 2 else BS if kind == "sel" else BW
                        pe.matmul(o, kv[:, cols], PT[u % 2][:, 0:TOK], start=starts, stop=False)
                        last = pe.matmul(o[:, P:TOK], kv[:, cols1], PT[u % 2][:, TOK:384], start=False, stop=stops)
                    if ends:
                        last.then_inc(o_done, 1)

                for br in range(3):
                    drain_banks()
                    units = branch_units(br)
                    nu = len(units)
                    for i in range(nu + 4):
                        if i < nu:
                            kind, h = units[i][:2]
                            q, k = operands(br, kind, h)
                            if kind == "cmp":
                                scores_cmp(i, q, k)
                            else:
                                scores(i, q, k)
                        if 0 <= i - 3 < nu:
                            if units[i - 3][0] == "cmp":
                                turn_cmp(i - 3)
                            else:
                                turn_unit(i - 3)
                        if 0 <= i - 4 < nu:
                            kind, h, ends = units[i - 4]
                            if br == 0:
                                values_a(i - 4, kind, h)
                            else:
                                values_bc(i - 4, br, kind, h, ends)
                    pe.wait_ge(nmax_ready, seen.next(nmax_ready, 2))
                    if br == 0:
                        pe.wait_ge(ya_copied, seen.next(ya_copied, 2))
                        turn(YA, 4, ya_ready)
                        pe.wait_ge(xlo_ready, seen.next(xlo_ready, 2))
                    else:
                        pe.wait_ge(olo_ready, seen.next(olo_ready, 2))
                    for c in range(2):
                        for _ in range(2):
                            ups(n)
                            n += 1
                        pe.wait_ge(lo_ready, seen.next(lo_ready))
                        wh, wl = tview(w_hi[n % RING], 4, 512), tview(w_lo[n % RING], 4, 512)
                        for j in range(2):
                            b = take_bank()
                            for m in range(2):
                                cols = slice(CW * j + P * m, CW * j + P * m + P)
                                for k in range(4):
                                    last = matmul3(up[b][:, m * TOK:(m + 1) * TOK], wh[:, k, cols], wl[:, k, cols],
                                                   yT_hi[:, k, :], yT_lo[:, k, :], k == 0, k == 3)
                        last.then_inc(tile_used, 1)
                        n += 1
                for j in range(4):
                    pe.wait_ge(lo_ready, seen.next(lo_ready))
                    pe.wait_ge(mlo_ready, seen.next(mlo_ready))
                    down_matmuls(n, hT_hi[:, j % 2], hT_lo[:, j % 2], j == 0, j == 3)
                    n += 1

            def scores_cmp(u, q, k):
                if u >= 2:
                    pe.wait_ge(nmax_ready, seen.next(nmax_ready))
                for t in range(NT):
                    last = pe.matmul(acc[u % 2][:, NCMP * t:NCMP * t + NCMP], q[:, P * t:P * t + P], k, start=True,
                                     stop=True)
                last.then_inc(scores_done, 1)

            def turn_cmp(u):
                pe.wait_ge(p_ready, seen.next(p_ready))
                for t in range(NT):
                    last = pe.transpose(acc[2 + u % 2][0:NCMP, P * t:P * t + P], S[u % DEEP][:, NCMP * t:NCMP * t + NCMP],
                                        ident)
                last.then_inc(turned, 1)

            def ple(s, n0):
                for _ in range(KD // 2):
                    next_pair()
                pe.wait_ge(ple_arrived, seen.next(ple_arrived, 16))
                for t in range(NT):
                    for k in range(2):
                        last = pe.transpose(acc[0][:, k * TOK + t * P:k * TOK + (t + 1) * P],
                                            ple_in[:, t, k * P:(k + 1) * P], ident)
                last.then_inc(xT_ready, 1)
                n = n0
                for c in range(2):
                    ps = [up[take_bank()][:] for _ in range(NT)]
                    for h in range(2):
                        pe.wait_ge(lo_ready, seen.next(lo_ready))
                        token_matmuls(n, 4, 512, 0, 512, 4 * h, ps, h == 0, h == 1).then_inc(tile_used, 1)
                        n += 1
                    ps = [up[take_bank()][:] for _ in range(NT)]
                    pe.wait_ge(lo_ready, seen.next(lo_ready))
                    if c == 0:
                        pe.wait_ge(xlo_ready, seen.next(xlo_ready))
                    wh, wl = tview(w_hi[n % RING], 2, 512), tview(w_lo[n % RING], 2, 512)
                    for t in range(NT):
                        for k in range(2):
                            tok = slice(t * P, (t + 1) * P)
                            last = matmul3(ps[t], hT_hi[:, 0, k, tok], hT_lo[:, 0, k, tok], wh[:, k, :], wl[:, k, :],
                                           k == 0, k == 1)
                        if c:
                            last.then_inc(acc_done, QUARTERS // NT)
                    if c == 0:
                        last.then_inc(tile_used, 1)
                    n += 1

            pe.wait_ge(const_in, seen.next(const_in, 16))
            pe.wait_ge(gain_in, seen.next(gain_in, 112))
            for k in range(KD):
                last = pe.transpose(up[3][:, k * G_ROWS:(k + 1) * G_ROWS], g_rows[:, k * P:(k + 1) * P],
                                    ident[0:G_ROWS, 0:G_ROWS])
            last.then_inc(setup_pe, 1)
            for s, n0 in zip(plan, first):
                if s[0] == "norm":
                    turn_norm()
                elif s[0] == "ffn":
                    ffn(s, n0)
                elif s[0] == "conv":
                    conv(s, n0)
                elif s[0] == "mla":
                    mla(s, n0)
                elif s[0] == "sg":
                    sg(s, n0)
                elif s[0] == "tables":
                    tables(s[1])
                elif s[0] == "mix":
                    mix(s, n0)
                elif s[0] == "ple":
                    ple(s, n0)
                residuals[0] += s[0] not in ("norm", "tables", "final")

        @block.gpsimd
        def _(pool):
            pool.dma_start(pos[:], A["positions"][0].rearrange("(t p) -> p t", p=P), allow_slow_non_contiguous=True).then_inc(misc_in, 16)
            pool.dma_start(g96[:, 0, :], A["mla_q_gain"].partition_broadcast(P)).then_inc(misc_in, 16)
            pool.dma_start(g96[:, 1, :], A["mla_k_gain"].partition_broadcast(P)).then_inc(misc_in, 16)
            seen = Seen()

            def probabilities(u, factors=(None, None)):
                b = u % DEEP
                pool.wait_ge(rsum_ready, seen.next(rsum_ready))
                for t, lo, hi in ((1, 0, 256), (0, 256, 384)):
                    last = pool.tensor_scalar(S[b][:, lo:hi], S[b][:, lo:hi], rsum[b][:, t:t + 1], factors[t], ALU.mult,
                                              ALU.mult if factors[t] is not None else ALU.bypass)
                last.then_inc(p_ready, 1)

            def probabilities_cmp(u, factors):
                b = u % DEEP
                pool.wait_ge(rsum_ready, seen.next(rsum_ready))
                for t in range(NT):
                    cols = slice(NCMP * t, NCMP * t + NCMP)
                    last = pool.tensor_scalar(S[b][:, cols], S[b][:, cols], rsum[b][:, t:t + 1], factors[t], ALU.mult,
                                              ALU.mult)
                last.then_inc(pool_step, 1)
                pool.wait_ge(pool_step, seen.next(pool_step))
                pool.tensor_tensor(S[b][:, 0:2 * NCMP], S[b][:, 0:2 * NCMP], consts[:, C_CMPOK:C_CMPOK + 2 * NCMP],
                                   ALU.mult).then_inc(p_ready, 1)

            def sg():
                if any(s[0] == "mla" for s in plan):
                    pool.wait_ge(x_ready, QUARTERS * (2 + [s[0] for s in plan if s[0] not in ("norm",)].index("mla")))
                pool.dma_start(sgb, A["sg_b"][0].rearrange("g t -> (g t)").partition_broadcast(P)).then_inc(ws_in, 16)
                pool.dma_start(wsr, A["sg_w_s"][0].rearrange("g t s -> t g s")).then_inc(ws_in, 16)

            def tables():
                for i in range(2):
                    for v in range(2):
                        pool.dma_start(w2[:, i, v], A["nsa_cmp_w2_2"][i, v].rearrange("(m p) d -> p m d", p=P)
                                       ).then_inc(w2_in, 16)
                pool.wait_ge(arena_free, 1)
                pool.dma_start(relb[0:32, :], A["rel_bias_2"]).then_inc(tables_in, 16)
                pool.dma_start(one_hots, A["consts"][0:33, C_KEPT:]).then_inc(tables_in, 16)
                pool.dma_start(lp.rearrange("p i a d -> p (i a d)"),
                               A["diff_lambda_2"].rearrange("i a d -> (i a d)").partition_broadcast(P)
                               ).then_inc(tables_in, 16)
                pool.dma_start(sinks[:], A["swa_sinks_2"].rearrange("i h -> (i h)").partition_broadcast(P)
                               ).then_inc(tables_in, 16)
                for i in range(2):
                    for v in range(2):
                        at = 32 * i + 16 * v
                        pool.dma_start(prows[at:at + 16, :],
                                       A["nsa_cmp_pos_2"][i, v].rearrange("(j q) d -> j (q d)", q=2)
                                       ).then_inc(tables_in, 16)
                pool.wait_ge(rv_ready, 1)
                pool.dma_start(scratch[0:12, :], rv[0:12, 0, :]).then_inc(rv_stored, 16)
                pool.dma_start(scratch[12:20, :], rv[0:8, 1, :]).then_inc(rv_stored, 16)
                pool.wait_ge(rv_stored, 32)
                askew = bass.AP(scratch.tensor, 0, [[1, P], [384, 20], [1, 256]])
                pool.dma_start(U, askew).then_inc(u_in, 16)

            def mix(s):
                pool.wait_ge(kc_ready, seen.next(kc_ready))
                for v in range(2):
                    for g in range(2):
                        src = KC[64 * g:64 * g + 64, v, :]
                        pool.dma_start(KC2[0:64, v, g, :], src).then_inc(kc2_in, 16)
                        pool.dma_start(KC2[64:128, v, g, 0:TOK - 1], src[:, 1:TOK]).then_inc(kc2_in, 16)
                pool.wait_ge(gates_ready, seen.next(gates_ready))
                for br in range(3):
                    for i, (kind, h, _) in enumerate(branch_units(br)):
                        if br == 0:
                            probabilities(i, (neglam[:, s[1]:s[1] + 1],) * 2 if kind == 1 else (None, None))
                        elif br == 2:
                            probabilities(i)
                        else:
                            col = 3 * h + ("cmp", "sel", "win").index(kind)
                            factors = [gB[:, t, col:col + 1] for t in range(NT)]
                            if kind == "cmp":
                                probabilities_cmp(i, factors)
                            else:
                                probabilities(i, factors)

            residuals = 0
            for s in plan:
                if s[0] == "mla":
                    for h in range(MH):
                        probabilities(h)
                elif s[0] == "sg":
                    sg()
                elif s[0] == "tables":
                    if s[1] == 0:
                        tables()
                elif s[0] == "mix":
                    mix(s)
                elif s[0] == "ple":
                    pool.wait_ge(x_ready, QUARTERS * residuals)
                    pool.dma_start(ple_in, A["p_2"][s[1], 0].rearrange("(t p) d -> p t d", p=P)
                                   ).then_inc(ple_arrived, 16)
                residuals += s[0] not in ("norm", "tables", "final")
            if plan[-1][0] == "final":
                pool.wait_ge(x_ready, QUARTERS * (residuals - 1))
                pool.dma_start(gfin, A["final_norm_2"].partition_broadcast(P)).then_inc(fin_in, 16)


_INS = ["x", "positions", "norm_g", "ffn_gate", "ffn_up", "ffn_down", "conv_w_in", "conv_k", "conv_w_out", "mla_w_a",
        "mla_q_norm", "mla_w_uq", "mla_kv_norm", "mla_w_ukv", "mla_q_gain", "mla_k_gain", "mla_w_o", "sg_w_in",
        "sg_v_norm", "sg_w_s", "sg_b", "sg_w_out", "p_2", "norm_g_2", "ffn1_wi_2", "ffn1_wo_2", "w_in_2",
        "diff_lambda_2", "diff_subln_2", "nsa_cmp_pos_2", "nsa_cmp_w1_2", "nsa_cmp_w2_2", "swa_sinks_2",
        "w_branch_2", "w_out_2", "ffn2_wi_2", "ffn2_wo_2", "w_ple_2", "w_ple_gate_2", "rel_bias_2", "final_norm_2"]


def shape_constants():
    c = np.zeros((P, C_END), np.float32)
    q = np.arange(P)[:, None]
    c[:, C_ID:C_ID + P] = np.eye(P)
    c[:, C_FLIP:C_FLIP + P] = np.eye(P)[::-1]
    c[:, C_CAUSAL:C_CAUSAL + 2 * P] = np.where(P + q - np.arange(2 * P)[None] >= 0, 0.0, NEG)
    c[:, C_LOWT:C_LOWT + P] = (q <= np.arange(P)[None])
    for t in range(2):
        c[:, C_CMPOK + 15 * t:C_CMPOK + 15 * t + 15] = (P * t + q - 16 * np.arange(15)[None] - 31 >= 0)
    f = np.arange(0, ROPE, 2, dtype=np.float32) / np.float32(ROPE)
    c[:, C_FREQ:C_FREQ + 16] = np.float32(1.0) / np.float32(10000.0) ** f

    def one_hot(dist, masked):
        n = np.maximum(dist, 0)
        nf = np.maximum(n, 1).astype(np.float32)
        large = 16 + (np.log(nf / np.float32(16)) / np.float32(np.log(8.0)) * np.float32(16)).astype(np.int32)
        b = np.where(n < 16, n, np.minimum(large, 31))
        o = np.zeros((33, dist.size), np.float32)
        o[np.where(masked, 32, b), np.arange(dist.size)] = 1.0
        return o

    d = 255 - np.arange(384)
    c[0:33, C_OHREV:C_OHREV + 384] = one_hot(d, d < 0)
    c[0:33, C_OHREV + 384:C_OHREV + 768] = one_hot(d, (d < 0) | (d >= 128))
    d = np.arange(512) - 256
    c[0:33, C_OHF:C_OHF + 512] = one_hot(d, d < 0)
    return c


def kernel(**inputs):
    import concourse.bacc as bacc
    from concourse.bass_utils import run_bass_kernel_spmd

    nc = bacc.Bacc("TRN2", target_bir_lowering=False, num_devices=1)
    arrays, A = {}, {}
    for name in _INS + ["consts"]:
        a = shape_constants() if name == "consts" else np.ascontiguousarray(inputs[name])
        arrays[f"in_{name}"] = a
        A[name] = nc.dram_tensor(f"in_{name}", a.shape, mybir.dt.from_np(a.dtype), kind="ExternalInput").ap()
    out = nc.dram_tensor("out_0", (1, TOK, D), F32, kind="ExternalOutput").ap()
    build(nc, A, out)
    r = run_bass_kernel_spmd(nc, [arrays], core_ids=[0])
    return r.results[0]["out_0"]
```

```python
from contextlib import ExitStack

import numpy as np

import concourse.bass as bass
from concourse import mybir

ALU = mybir.AluOpType
ACT = mybir.ActivationFunctionType
AX = mybir.AxisListType
F32 = mybir.dt.float32
F32R = mybir.dt.float32r
I32 = mybir.dt.int32

P = 128
TOK = 256
NT = TOK // P
D = 1024
KD = D // P
FF = 2816
EPS = 1e-6
TILE = 2048
RING = 3
CW = 256
NCH = FF // CW
QUARTERS = 4
HSCALE = 0.125
BIG = 3.0e38
DEEP = 4
NORM_FILL = 18
NEG = -1e30
QL, KVL, ROPE, NOPE, VH, QKH, MH = 256, 128, 32, 64, 64, 96, 16
RSQRT_MAGIC = float(0x5F3759DF)
TWO_PI = (6.28125, 0.0019340515136718750, 1.255665914356996e-06)
PI_IN = 3.1415925

C_ID = 0
C_FLIP = 128
C_CAUSAL = 256
C_LOWT = 512
C_CMPOK = 640
C_FREQ = 672
C_KEPT = 688
C_OHREV = C_KEPT
C_OHF = C_OHREV + 768
C_END = C_OHF + 512
ARENA = 15880

G_SGV = 20
G_CONV = 21
G_MISC = 27
G_ROWS = 28


W_AQ, W_AK, W_AV, W_BQ, W_BC, W_BS, W_BW, W_BG = 0, 512, 1024, 1536, 2048, 2304, 2560, 2816
W_CQ, W_CKV, W_G = 2840, 3352, 3608
NCMP = 15
LAM_INIT = [0.8 - 0.6 * float(np.exp(-0.3 * i)) for i in range(2)]


class Seen:

    def __init__(self):
        self.n, self.turn, self.rate, self.before = {}, None, {}, {}

    def next(self, sem, k=1):
        self.n[sem.name] = self.n.get(sem.name, 0) + k
        v = self.n[sem.name]
        if self.turn is not None:
            v = self.turn * self.rate[sem.name] + v
        return v

    def enter(self, turn, rate):
        self.turn, self.rate, self.before = turn, {s.name: r for s, r in rate}, dict(self.n)

    def leave(self, turns):
        for name, r in self.rate.items():
            assert self.n.get(name, 0) - self.before.get(name, 0) == r, (name, r)
            self.n[name] += (turns - 1) * r
        self.turn = None


def full_plan():
    plan = []
    for i in range(4):
        plan += [("norm", 3 * i), ("ffn", 1, i, 0), ("norm", 3 * i + 1)]
        plan += [("conv", i // 3)] if i % 3 == 0 else [("mla",)] if i == 1 else [("sg",)]
        plan += [("norm", 3 * i + 2), ("ffn", 1, i, 1)]
    at = plan.index(("norm", 9))
    plan[at:at] = [("tables", 0)]
    at = plan.index(("norm", 10))
    plan[at:at] = [("tables", 1)]
    plan += [("tables", 2)]
    for i in range(2):
        plan += [("norm", 12 + 4 * i), ("ffn", 2, i, 0), ("norm", 13 + 4 * i), ("mix", i)]
        plan += [("norm", 14 + 4 * i), ("ffn", 2, i, 1), ("norm", 15 + 4 * i), ("ple", i)]
    return plan + [("final",)]


def build(nc, A, out, plan=None):
    plan = plan or full_plan()
    with ExitStack() as ctx:
        def sb(name, shape, dt=F32):
            return ctx.enter_context(nc.sbuf_tensor(name, shape, dt))

        def sem(name):
            return ctx.enter_context(nc.semaphore(name))

        MIX_BANKS = 17
        raw = [sb(f"raw{i}", [P, TILE]) for i in range(RING)]
        w_hi = [sb(f"w_hi{i}", [P, TILE], F32R) for i in range(RING)]
        w_lo = [sb(f"w_lo{i}", [P, TILE], F32R) for i in range(RING)]
        xT_hi = sb("xT_hi", [P, KD, TOK], F32R)
        xT_lo = sb("xT_lo", [P, KD, TOK], F32R)
        hT_hi = sb("hT_hi", [P, 2, 2, TOK], F32R)
        hT_lo = sb("hT_lo", [P, 2, 2, TOK], F32R)
        yT_hi = sb("yT_hi", [P, 4, TOK], F32R)
        yT_lo = sb("yT_lo", [P, 4, TOK], F32R)
        x = sb("x", [P, NT, D])
        xn = sb("xn", [P, NT, D])
        gate = sb("gate", [P, 512])
        prod = sb("prod", [P, 512])
        consts = sb("consts", [P, C_KEPT])
        gains = sb("gains", [P, KD, 32])
        ss = sb("ss", [P, 8])
        nwt = sb("nwt", [P, 64])
        nwv = sb("nwv", [P, 64])
        rstd = sb("rstd", [P, 8])
        diag = sb("diag", [P, NT, P])
        arena = sb("arena", [P, ARENA])
        pos = sb("pos", [P, NT], I32)
        cos = sb("cos", [P, NT, 16])
        sin = sb("sin", [P, NT, 16])
        g96 = sb("g96", [P, 2, QKH])

        def carve(at, *shape):
            n = int(np.prod(shape))
            v = arena[:, at:at + n]
            names = " ".join("abcd"[:len(shape)])
            dims = {"abcd"[i]: shape[i] for i in range(len(shape) - 1)}
            return v.rearrange(f"p ({names}) -> p {names}", **dims) if len(shape) > 1 else v

        g_rows = arena[0:G_ROWS, 0:D]
        zconv = carve(0, 2, TOK + 2)
        yconv = carve(520, 2, TOK)
        Q = carve(0, NT, MH, QKH)
        KV = carve(3072, NT, MH, NOPE + VH)
        KF = carve(7168, NT, MH, QKH)
        squares = carve(7168, NT, MH, QKH)
        latent = carve(10240, NT, QL + KVL + ROPE)
        cn = carve(11072, NT, QL + KVL)
        kpe = carve(11840, NT, ROPE)
        rtmp = carve(11904, 4, NT * MH, 16)
        headT = [carve(13952 + 512 * i, 512) for i in range(2)]
        units_buf = sb("units", [P, DEEP, 384])
        S = [units_buf[:, i, :] for i in range(DEEP)]
        PT = [sb(f"PT{i}", [P, 384]) for i in range(2)]
        nmax = [sb(f"nmax{i}", [P, 2]) for i in range(DEEP)]
        esum = [sb(f"esum{i}", [P, 2]) for i in range(DEEP)]
        rsum = [sb(f"rsum{i}", [P, 2]) for i in range(DEEP)]
        ssh = sb("ssh", [P, 64])
        qscale = sb("qscale", [P, NT * MH])
        rsh = sb("rsh", [P, 64])
        esink = [sb(f"esink{i}", [P, 2]) for i in range(DEEP)]
        T = carve(0, 20, 256)
        TC = carve(5120, 8, 2 * NCMP)
        U = carve(5376, 20, 256)
        rv = carve(10496, 2, 384)
        lp = carve(11264, 2, 4, 64)
        prows = arena[0:64, 11776:11904]
        relb = arena[0:33, 11904:11924]
        one_hots = arena[0:33, 11924:11924 + C_END - C_KEPT]
        AQ, AK, AV = carve(5376, 4, TOK), carve(6400, 4, TOK), carve(7424, NT, 512)
        BQ, CQ = carve(8448, 4, TOK), carve(11008, 4, TOK)
        KC = carve(9472, 2, TOK)
        BS, BW, CKV = carve(9984, 512), carve(10496, 512), carve(12032, 512)
        gB = carve(12544, NT, 24)
        KC2 = carve(12592, 2, 2, TOK)
        blk = carve(13616, 2, 16, 2 * NCMP)
        hid = arena[0:2 * NCMP, 14854:15366].rearrange("p (v n) -> p v n", v=2)
        hidT = carve(14576, 2, 2, 2 * NCMP)
        kcT = carve(14696, 2 * NCMP)
        vc = arena[0:NCMP, 14726:14854]
        YA = carve(14854, NT, 512)
        ya_junk = carve(12592, 8, P)
        yB_hi = hT_hi[:].rearrange("p a k n -> p (a k) n")
        yB_lo = hT_lo[:].rearrange("p a k n -> p (a k) n")
        merged = xn[:].rearrange("p t (m n) -> p (t m) n", n=TOK)
        blk_hi = yT_hi[:].rearrange("p k n -> p (k n)")[:, 0:960].rearrange("p (v j n) -> p v j n", v=2, j=16)
        blk_lo = yT_lo[:].rearrange("p k n -> p (k n)")[:, 0:960].rearrange("p (v j n) -> p v j n", v=2, j=16)
        pos2 = sb("pos2", [P, 2, 2, 16])
        w2 = sb("w2", [P, 2, 2, 2, 64])
        neglam = sb("neglam", [P, 2])
        sinks = sb("sinks", [P, 16])
        negsinks = sb("negsinks", [P, 16])
        subln = sb("subln", [P, 2])
        ple_in = units_buf[:].rearrange("p a b -> p (a b)")[:, 0:512].rearrange("p (t d) -> p t d", t=NT)
        gfin = carve(0, D)
        wsT = carve(0, 8, P)
        wsr = carve(1024, 8, P)
        mixed = carve(2048, 2, TOK)
        sgb = carve(2560, D)

        ident = consts[:, C_ID:C_ID + P]

        acc = [ctx.enter_context(nc.psum_tensor(f"acc{i}", [P, 512], F32)) for i in range(4)]
        up = [ctx.enter_context(nc.psum_tensor(f"up{i}", [P, 512], F32)) for i in range(4)]

        landed = [sem(f"landed{i}") for i in range(RING)]
        const_in = sem("const_in")
        x_in = sem("x_in")
        gain_in = sem("gain_in")
        rows_clear = sem("rows_clear")
        hi_ready = sem("hi_ready")
        lo_ready = sem("lo_ready")
        tile_used = sem("tile_used")
        bank_free = sem("bank_free")
        setup_pe = sem("setup_pe")
        setup_dve = sem("setup_dve")
        x_ready = sem("x_ready")
        ss_ready = sem("ss_ready")
        diag_ready = sem("diag_ready")
        xT_ready = sem("xT_ready")
        xhi_ready = sem("xhi_ready")
        xlo_ready = sem("xlo_ready")
        gate_ready = sem("gate_ready")
        prod_ready = sem("prod_ready")
        hhi_ready = sem("hhi_ready")
        hlo_ready = sem("hlo_ready")
        acc_done = sem("acc_done")
        dve_step = sem("dve_step")
        misc_in = sem("misc_in")
        trig_arg = sem("trig_arg")
        trig_done = sem("trig_done")
        cn_ready = sem("cn_ready")
        group_done = sem("group_done")
        kv_copied = sem("kv_copied")
        q_copied = sem("q_copied")
        qk_ready = sem("qk_ready")
        headT_done = sem("headT_done")
        headT_ready = sem("headT_ready")
        scores_done = sem("scores_done")
        nmax_ready = sem("nmax_ready")
        exp_ready = sem("exp_ready")
        rsum_ready = sem("rsum_ready")
        pool_step = sem("pool_step")
        p_ready = sem("p_ready")
        turned = sem("turned")
        pt_ready = sem("pt_ready")
        o_done, oa_done = sem("o_done"), sem("oa_done")
        ohi_ready = sem("ohi_ready")
        olo_ready = sem("olo_ready")
        ws_in = sem("ws_in")
        ws_turned = sem("ws_turned")
        ws_ready = sem("ws_ready")
        v_ready = sem("v_ready")
        mix_done = sem("mix_done")
        tables_in = sem("tables_in")
        arena_free = sem("arena_free")
        tab_pe = sem("tab_pe")
        tab_dve = sem("tab_dve")
        tab_act = sem("tab_act")
        rv_stored = sem("rv_stored")
        rv_ready = sem("rv_ready")
        u_in = sem("u_in")
        gates_ready = sem("gates_ready")
        kc_ready = sem("kc_ready")
        kc2_in = sem("kc2_in")
        blk_ready = sem("blk_ready")
        blkhi_ready = sem("blkhi_ready")
        blklo_ready = sem("blklo_ready")
        hid_ready = sem("hid_ready")
        hid_turned = sem("hid_turned")
        hidT_ready = sem("hidT_ready")
        cmp_done = sem("cmp_done")
        proj_ready = sem("proj_ready")
        ya_copied = sem("ya_copied")
        ya_ready = sem("ya_ready")
        merge_step = sem("merge_step")
        merge_gate = sem("merge_gate")
        ya_squares = sem("ya_squares")
        ya_scale = sem("ya_scale")
        ple_added, ple_step = sem("ple_added"), sem("ple_step")
        mhi_ready = sem("mhi_ready")
        mlo_ready = sem("mlo_ready")
        ple_arrived = sem("ple_arrived")
        fin_in = sem("fin_in")
        w2_in = sem("w2_in")
        fin_ready = sem("fin_ready")
        scratch = nc.dram_tensor("bias_rows", (20, 384), F32, kind="Internal").ap()
        vn_ready = sem("vn_ready")
        stored = sem("stored")

        def kpn(w):
            return w.rearrange("(k p) n -> p k n", p=P)

        def tview(buf, nk, n):
            return buf[:, 0:nk * n].rearrange("p (k n) -> p k n", k=nk)

        def ffn_weights(s):
            _, blk, i, j = s
            if blk == 1:
                return A["ffn_gate"][i, j], A["ffn_up"][i, j], A["ffn_down"][i, j]
            wi = A["ffn1_wi_2" if j == 0 else "ffn2_wi_2"][i]
            wo = A["ffn1_wo_2" if j == 0 else "ffn2_wo_2"][i]
            return wi[:, 0:FF], wi[:, FF:2 * FF], wo

        def up_tile(w, col):
            return (KD, CW, [(slice(None), kpn(w)[:, :, col:col + CW])])

        def query_tile(w, col, j):
            return (KD, CW, [(slice(P * r + 64 * g, P * r + 64 * g + 64),
                              kpn(w)[:, :, col + 256 * g + 64 * (2 * j + r):col + 256 * g + 64 * (2 * j + r) + 64])
                             for r in range(2) for g in range(2)])

        def cols_tile(w, nk, col, n):
            return (nk, n, [(slice(None), kpn(w)[:, :, col:col + n])])

        def down_tile(w, row):
            return (2, D, [(slice(None), kpn(w[row:row + 2 * P, :]))])

        def tiles_of(s):
            if s[0] == "conv":
                w, wo = A["conv_w_in"][s[1]], A["conv_w_out"][s[1]]
                t = []
                for c in range(4):
                    t += [up_tile(w, D * m + CW * c) for m in (1, 2, 0)]
                    if c:
                        t.append(down_tile(wo, CW * (c - 1)))
                return t + [down_tile(wo, CW * 3)]
            if s[0] == "mla":
                wa, wq, wkv, wo = A["mla_w_a"][0], A["mla_w_uq"][0], A["mla_w_ukv"][0], A["mla_w_o"][0]
                t = [cols_tile(wa[512 * h:512 * h + 512, :], 4, 0, QL + KVL + ROPE) for h in range(2)]
                t += [cols_tile(wq, 2, 0, 1024), cols_tile(wq, 2, 1024, 512), cols_tile(wkv, 1, 0, 2048)]
                return t + [down_tile(wo, CW * i) for i in range(4)]
            if s[0] == "sg":
                w, wo = A["sg_w_in"][0], A["sg_w_out"][0]
                t = [cols_tile(w[512 * h:512 * h + 512, :], 4, D + 512 * g, 512) for g in range(2) for h in range(2)]
                for c in range(4):
                    t.append(up_tile(w, CW * c))
                    if c:
                        t.append(down_tile(wo, CW * (c - 1)))
                return t + [down_tile(wo, CW * 3)]
            if s[0] == "mix":
                w, w1 = A["w_in_2"][s[1]], A["nsa_cmp_w1_2"][s[1]]
                wb, wo = A["w_branch_2"][s[1]], A["w_out_2"][s[1]]
                hidden = [up_tile(w1[v, 1024 * h:1024 * h + 1024, :], 0) for v in range(2) for h in range(2)]
                t = [up_tile(w, W_BC)] + [up_tile(w, W_AQ + CW * j) for j in range(4)]
                t += [cols_tile(w[512 * h:512 * h + 512, :], 4, W_AV, 512) for h in range(2)]
                t += [query_tile(w, W_BQ, j) for j in range(2)]
                t += [hidden[0], up_tile(w, W_BS), hidden[1], up_tile(w, W_BW), query_tile(w, W_CQ, 0)]
                t += [hidden[2], query_tile(w, W_CQ, 1), hidden[3], up_tile(w, W_CKV), cols_tile(w, KD, W_BG, 24)]
                for br in range(3):
                    for c in range(2):
                        t += [up_tile(w, W_G + D * br + 512 * c + CW * j) for j in range(2)]
                        t += [cols_tile(wb[br], 4, 512 * c, 512)]
                return t + [down_tile(wo, CW * j) for j in range(4)]
            if s[0] == "ple":
                wg, wp = A["w_ple_gate_2"][s[1]], A["w_ple_2"][s[1]]
                t = []
                for c in range(2):
                    t += [cols_tile(wg[512 * h:512 * h + 512, :], 4, 512 * c, 512) for h in range(2)]
                    t += [cols_tile(wp, 2, 512 * c, 512)]
                return t
            return []

        UNITS = [(0, c, h, c == 1) for h in range(4) for c in range(2)]
        UNITS += [(1, k, h, h % 2 == 1 and k == "cmp") for h in range(8) for k in ("sel", "win", "cmp")]
        UNITS += [(2, "win", h, h % 2 == 1) for h in range(8)]
        NU = len(UNITS)
        YA_STEP = 16
        STEPS = NU + 6
        PIECES = {}
        for q in range(24):
            step_of = YA_STEP + 1 + int(1.3 * q) if q < 16 else NU - 2 + q - 16
            PIECES[step_of] = (q // 12, q // 6 % 2, q % 6)
        MIX_PROJ = 19

        first = []
        count = 0
        for s in plan:
            first.append(count)
            count += 3 * NCH if s[0] == "ffn" else len(tiles_of(s))
        n_tiles = count

        block = ctx.enter_context(nc.Block())

        @block.sync
        def _(sp):
            seen = Seen()
            sp.dma_start(x[:], A["x"][0].rearrange("(t p) d -> p t d", p=P)).then_inc(x_in, 16)
            sp.wait_ge(rows_clear, seen.next(rows_clear))
            sp.dma_start(g_rows[0:12, :], A["norm_g"].rearrange("i j d -> (i j) d")).then_inc(gain_in, 16)
            sp.dma_start(g_rows[12:20, :], A["norm_g_2"].rearrange("i j d -> (i j) d")).then_inc(gain_in, 16)
            sp.dma_start(g_rows[G_SGV:G_SGV + 1, :], A["sg_v_norm"]).then_inc(gain_in, 16)
            sp.dma_start(g_rows[G_CONV:G_CONV + 6, :], A["conv_k"].rearrange("i j d -> (i j) d")).then_inc(gain_in, 16)
            sp.dma_start(g_rows[G_MISC:G_MISC + 1, 0:QL], A["mla_q_norm"]).then_inc(gain_in, 16)
            sp.dma_start(g_rows[G_MISC:G_MISC + 1, QL:QL + KVL], A["mla_kv_norm"]).then_inc(gain_in, 16)
            sp.dma_start(g_rows[G_MISC:G_MISC + 1, QL + KVL:QL + KVL + 256],
                          A["diff_subln_2"].rearrange("(o i) d -> o (i d)", o=1)).then_inc(gain_in, 16)

            def slot_free(n):
                if n >= RING:
                    sp.wait_ge(lo_ready, seen.next(lo_ready))

            def load(n, t):
                slot_free(n)
                nk, ncol, parts = t
                dst = tview(raw[n % RING], nk, ncol)
                for cols, src in parts:
                    sp.dma_start(dst[:, :, cols], src).then_inc(landed[n % RING], 16)

            def ffn(s, n0):
                wg, wu, wd = ffn_weights(s)
                G = [up_tile(wg, CW * c) for c in range(NCH)]
                U = [up_tile(wu, CW * c) for c in range(NCH)]
                Dn = [down_tile(wd, CW * c) for c in range(NCH)]
                for j, t in enumerate([G[0], U[0], G[1], U[1], Dn[0]]):
                    load(n0 + j, t)
                base = n0 + 5
                with sp.Fori(0, 4) as i:
                    seen.enter(i, [(lo_ready, 6)])
                    for c in range(2):
                        for j, w in enumerate((wg, wu)):
                            n = base + 3 * c + j
                            slot_free(n)
                            sp.dma_start(tview(raw[n % RING], KD, CW),
                                         kpn(w)[:, :, bass.ds(i * (2 * CW) + (2 + c) * CW, CW)]
                                         ).then_inc(landed[n % RING], 16)
                        n = base + 3 * c + 2
                        slot_free(n)
                        sp.dma_start(tview(raw[n % RING], 2, D),
                                     wd[bass.ds(i * (2 * CW) + (1 + c) * CW, CW), :].rearrange("(k p) n -> p k n", p=P)
                                     ).then_inc(landed[n % RING], 16)
                    seen.leave(4)
                for j, t in enumerate([G[10], U[10], Dn[9], Dn[10]]):
                    load(n0 + 29 + j, t)

            for s, n0 in zip(plan, first):
                if s[0] == "ffn":
                    ffn(s, n0)
                else:
                    for j, t in enumerate(tiles_of(s)):
                        load(n0 + j, t)
            if plan[-1][0] == "final":
                sp.wait_ge(fin_ready, seen.next(fin_ready))
                res = xn
            else:
                sp.wait_ge(x_ready, QUARTERS * (1 + sum(s[0] not in ("norm", "tables", "final") for s in plan)))
                res = x
            sp.dma_start(out[0].rearrange("(t p) d -> p t d", p=P), res[:]).then_inc(stored, 16)
            sp.wait_ge(stored, 16)

        @block.scalar
        def _(act):
            seen = Seen()
            act.dma_start(consts[:], A["consts"][:, 0:C_KEPT]).then_inc(const_in, 16)
            parts_of = {}
            for s, n0 in zip(plan, first):
                for j, t in enumerate(tiles_of(s)):
                    parts_of[n0 + j] = len(t[2])

            def split_hi(n):
                if n >= n_tiles:
                    return
                act.wait_ge(landed[n % RING], seen.next(landed[n % RING], 16 * parts_of.get(n, 1)))
                nc.scalar.activation(w_hi[n % RING][:], raw[n % RING][:], ACT.Copy).then_inc(hi_ready, 1)

            def consumed(n):
                act.wait_ge(tile_used, seen.next(tile_used))
                split_hi(n + RING)

            def parts_hi(nk, row, dst=xT_hi, same=None, src=acc):
                for k in range(nk):
                    if k % 2 == 0:
                        act.wait_ge(xT_ready, seen.next(xT_ready))
                    g = gains[:, k, row:row + 1] if same is None else same
                    last = nc.scalar.activation(dst[:, k, :], src[k // 2][:, (k % 2) * TOK:(k % 2 + 1) * TOK],
                                                ACT.Copy, scale=g)
                    if k % 2 or k == nk - 1:
                        last.then_inc(xhi_ready, 1)

            owed = []

            def settle():
                if owed:
                    act.wait_ge(acc_done, seen.next(acc_done, QUARTERS))
                    split_hi(owed.pop() + RING)

            def mean_squares():
                for t in range(NT):
                    for h in range(2):
                        cols = slice(512 * h, 512 * h + 512)
                        act.wait_ge(x_ready, seen.next(x_ready))
                        nc.scalar.activation(xn[:, t, cols], x[:, t, cols], ACT.Square, scale=float(D) ** -0.5,
                                             accum_out=ss[:, 2 * t + h:2 * t + h + 1]).then_inc(ss_ready, 1)

            starting = [True]

            def norm(row):
                mean_squares()
                settle()
                if starting[0]:
                    split_hi(0)
                    act.wait_ge(setup_dve, 1)
                parts_hi(KD, row)
                if starting[0]:
                    for n in range(1, RING):
                        split_hi(n)
                    starting[0] = False

            def product_hi(par):
                act.wait_ge(prod_ready, seen.next(prod_ready))
                nc.scalar.activation(hT_hi[:, par], prod[:].rearrange("p (k n) -> p k n", k=2),
                                     ACT.Copy).then_inc(hhi_ready, 1)

            def ffn(s, n0, bank0):
                def chunk(n, c, down):
                    consumed(n)
                    b = (bank0 + 2 * c) % 4
                    nc.scalar.activation(gate[:], up[b][:], ACT.Silu).then_inc(gate_ready, 1)
                    consumed(n + 1)
                    product_hi(c % 2)
                    if down:
                        consumed(n + 2)

                chunk(n0, 0, False)
                chunk(n0 + 2, 1, True)
                with act.Fori(0, 4) as i:
                    seen.enter(i, [(landed[r], 32) for r in range(RING)] + [(tile_used, 6), (prod_ready, 2)])
                    chunk(n0 + 5, 2, True)
                    chunk(n0 + 8, 3, True)
                    seen.leave(4)
                chunk(n0 + 29, 10, True)
                owed.append(n0 + 32)

            def conv(s, n0, bank0):
                for c in range(4):
                    n = n0 + 4 * c - (c > 0)
                    b = (bank0 + 3 * c) % 4
                    consumed(n)
                    nc.scalar.activation(gate[:], up[b][:], ACT.Copy).then_inc(gate_ready, 1)
                    consumed(n + 1)
                    consumed(n + 2)
                    product_hi(c % 2)
                    if c:
                        consumed(n + 3)
                owed.append(n0 + 15)

            def exp_unit(u, widths=((1, 0, 256), (0, 256, 384)), sink=None):
                b = u % DEEP
                act.wait_ge(nmax_ready, seen.next(nmax_ready))
                for i, lo, hi in widths:
                    last = nc.scalar.activation(S[b][:, lo:hi], S[b][:, lo:hi], ACT.Exp, bias=nmax[b][:, i:i + 1],
                                                scale=-1.0, accum_out=esum[b][:, i:i + 1])
                if sink is not None:
                    last = nc.scalar.activation(esink[b][:], nmax[b][:], ACT.Exp, bias=sink)
                last.then_inc(exp_ready, 1)

            def copy_turned(u, rows=P, width=384):
                act.wait_ge(turned, seen.next(turned))
                nc.scalar.activation(PT[u % 2][0:rows, 0:width], acc[2 + u % 2][0:rows, 0:width],
                                     ACT.Copy).then_inc(pt_ready, 1)

            def mla(s, n0, bank0):
                act.wait_ge(trig_arg, seen.next(trig_arg))
                nc.scalar.activation(sin[:], sin[:], ACT.Sin)
                nc.scalar.activation(cos[:], cos[:], ACT.Sin).then_inc(trig_done, 1)
                consumed(n0)
                consumed(n0 + 1)
                parts_hi(3, G_MISC)
                consumed(n0 + 2)
                consumed(n0 + 3)
                act.wait_ge(q_copied, seen.next(q_copied))
                for t in range(NT):
                    last = nc.scalar.activation(squares[:, t, :, :].rearrange("p h d -> p (h d)"),
                                                Q[:, t, :, :].rearrange("p h d -> p (h d)"), ACT.Square)
                b = (bank0 + 8) % 4
                for g in range(4):
                    if g < 3:
                        act.wait_ge(group_done, seen.next(group_done))
                    else:
                        consumed(n0 + 4)
                    for t in range(NT):
                        last = nc.scalar.activation(
                            arena[:, 3072 + 2048 * t + 512 * g:3072 + 2048 * t + 512 * g + 512],
                            up[(b + 2 * g + t) % 4][:], ACT.Copy)
                    last.then_inc(kv_copied, 1)

                def o_hi(j):
                    act.wait_ge(o_done, seen.next(o_done))
                    nc.scalar.activation(xT_hi[:, j, :], up[2 + j % 2][:, 0:TOK],
                                         ACT.Copy).then_inc(ohi_ready, 1)

                for i in range(1, MH + 7):
                    if i - 1 < MH:
                        exp_unit(i - 1)
                    if 0 <= i - 4 < MH:
                        copy_turned(i - 4)
                    if 0 <= i - 6 < MH and (i - 6) % 2:
                        o_hi((i - 6) // 2)
                for j in range(3):
                    consumed(n0 + 5 + j)
                owed.append(n0 + 8)

            def sg(s, n0, bank0):
                for g in range(2):
                    consumed(n0 + 2 * g)
                    consumed(n0 + 2 * g + 1)
                    for t in range(NT):
                        last = nc.scalar.activation(xn[:, t, 512 * g:512 * g + 512],
                                                    up[(bank0 + 2 * g + t) % 4][:], ACT.Gelu_apprx_tanh)
                    last.then_inc(v_ready, 1)
                for c in range(4):
                    n = n0 + 4 + 2 * c - (c > 0)
                    consumed(n)
                    nc.scalar.activation(gate[:], up[(bank0 + 4 + 2 * c) % 4][:],
                                         ACT.Gelu_apprx_tanh).then_inc(gate_ready, 1)
                    product_hi(c % 2)
                    if c:
                        consumed(n + 1)
                owed.append(n0 + 11)

            def tables(part):
                settle()
                if part != 1:
                    return
                act.wait_ge(tab_dve, seen.next(tab_dve))
                nc.scalar.activation(ssh[:, 4:8], ssh[:, 0:4], ACT.Exp).then_inc(tab_act, 1)

            def mix(s, n0, bank0):
                for i in range(7):
                    consumed(n0 + i)
                for v in range(2):
                    act.wait_ge(blk_ready, seen.next(blk_ready))
                    nc.scalar.activation(blk_hi[:, v], blk[:, v], ACT.Copy).then_inc(blkhi_ready, 1)
                for i in range(7, MIX_PROJ):
                    consumed(n0 + i)
                    if i in (11, 16):
                        v = int(i == 16)
                        nc.scalar.activation(hid[:, v, :], acc[2 * v][0:2 * NCMP, 0:CW],
                                             ACT.Gelu_apprx_tanh).then_inc(hid_ready, 1)
                nc.scalar.activation(gB.rearrange("p t h -> p (t h)"), up[(bank0 + 14) % 4][:, 0:48],
                                     ACT.Sigmoid).then_inc(gates_ready, 1)

                late = []

                def merge(br, c, piece):
                    if piece % 2 == 0:
                        return
                    g = piece // 2
                    n = n0 + MIX_PROJ + 6 * br + 3 * c + g
                    act.wait_ge(tile_used, seen.next(tile_used))
                    if g < 2:
                        if g == 0 and (br or c):
                            act.wait_ge(merge_step, seen.next(merge_step))
                            if (br, c) == (2, 1):
                                parts_of_merged(0)
                        nc.scalar.activation((gate, prod)[g][:], up[g][:], ACT.Sigmoid).then_inc(merge_gate, 1)
                    late.append(n)

                def parts_of_merged(c):
                    for j in range(2 * c, 2 * c + 2):
                        if j >= 2:
                            consumed(n0 + MIX_PROJ + 18 + j - 2)
                        nc.scalar.activation(hT_hi[:, j % 2], merged[:, 2 * j:2 * j + 2, :],
                                             ACT.Copy).then_inc(mhi_ready, 1)

                for i in range(STEPS):
                    if 0 <= i - 3 < NU:
                        if UNITS[i - 3][1] == "cmp":
                            copy_turned(i - 3, NCMP, 256)
                        else:
                            copy_turned(i - 3)
                    if i < NU:
                        br, kind, h, _ = UNITS[i]
                        if kind == "cmp":
                            exp_unit(i, ((0, 0, NCMP), (1, NCMP, 2 * NCMP)))
                        else:
                            exp_unit(i, sink=sinks[:, 8 * s[1] + h:8 * s[1] + h + 1] if br == 2 else None)
                    if 0 <= i - 5 < NU and UNITS[i - 5][3]:
                        br, _, h, _ = UNITS[i - 5]
                        if br:
                            j = h // 2
                            act.wait_ge(o_done, seen.next(o_done))
                            nc.scalar.activation((yB_hi if br == 1 else yT_hi)[:, j, :], up[2 + j % 2][:, 0:TOK],
                                                 ACT.Copy).then_inc(ohi_ready, 1)
                    if i >= 6 and i <= 12 and i % 2 == 0:
                        h = (i - 6) // 2
                        act.wait_ge(ya_copied, seen.next(ya_copied))
                        for t in range(NT):
                            last = nc.scalar.activation(ya_junk[:, 2 * h + t, :], YA[:, t, P * h:P * h + P],
                                                        ACT.Square, accum_out=ssh[:, 4 * t + h:4 * t + h + 1])
                        last.then_inc(ya_squares, 1)
                    if i == YA_STEP:
                        parts_hi(4, 0, yT_hi, subln[:, s[1]:s[1] + 1], up)
                    while late:
                        split_hi(late.pop() + RING)
                    if i in PIECES:
                        merge(*PIECES[i])
                    if i >= NU:
                        while late:
                            split_hi(late.pop() + RING)
                for c in range(2):
                    for piece in range(6):
                        merge(2, c, piece)
                        while late:
                            split_hi(late.pop() + RING)
                act.wait_ge(merge_step, seen.next(merge_step))
                parts_of_merged(1)
                consumed(n0 + MIX_PROJ + 20)
                owed.append(n0 + MIX_PROJ + 21)

            def ple(s, n0, bank0):
                act.wait_ge(xT_ready, seen.next(xT_ready))
                nc.scalar.activation(hT_hi[:, 0], acc[0][:].rearrange("p (k n) -> p k n", k=2),
                                     ACT.Copy).then_inc(xhi_ready, 1)
                for c in range(2):
                    consumed(n0 + 3 * c)
                    consumed(n0 + 3 * c + 1)
                    if c:
                        act.wait_ge(ple_step, seen.next(ple_step))
                    for t, dst in enumerate((gate, prod)):
                        last = nc.scalar.activation(dst[:], up[(bank0 + 4 * c + t) % 4][:], ACT.Sigmoid)
                    last.then_inc(gate_ready, 1)
                    if c == 0:
                        consumed(n0 + 2)
                owed.append(n0 + 5)

            bank = 0
            for s, n0 in zip(plan, first):
                if s[0] == "norm":
                    norm(s[1])
                elif s[0] == "ffn":
                    ffn(s, n0, bank)
                    bank = (bank + 2 * NCH) % 4
                elif s[0] == "conv":
                    conv(s, n0, bank)
                    bank = (bank + 12) % 4
                elif s[0] == "mla":
                    mla(s, n0, bank)
                    bank = (bank + 16) % 4
                elif s[0] == "sg":
                    sg(s, n0, bank)
                    bank = (bank + 12) % 4
                elif s[0] == "tables":
                    tables(s[1])
                elif s[0] == "mix":
                    mix(s, n0, bank)
                    bank = (bank + MIX_BANKS) % 4
                elif s[0] == "ple":
                    ple(s, n0, bank)
                    bank = (bank + 8) % 4
                elif s[0] == "final":
                    mean_squares()

        @block.vector
        def _(dve):
            seen = Seen()

            def step(ins):
                ins.then_inc(dve_step, 1)
                dve.wait_ge(dve_step, seen.next(dve_step))

            def split_lo(n):
                if n >= n_tiles:
                    return
                dve.wait_ge(hi_ready, seen.next(hi_ready))
                nc.vector.tensor_tensor(w_lo[n % RING][:], raw[n % RING][:], w_hi[n % RING][:].bitcast(F32),
                                        ALU.subtract).then_inc(lo_ready, 1)

            def consumed(n):
                dve.wait_ge(tile_used, seen.next(tile_used))
                split_lo(n + RING)

            def rsqrt(y, v):
                t = nwt[:, 0:y.shape[1]]
                step(nc.vector.tensor_single_scalar(t.bitcast(I32), v.bitcast(I32), 1, ALU.logical_shift_right))
                step(nc.vector.tensor_scalar(y.bitcast(I32), t.bitcast(I32), -1.0, RSQRT_MAGIC, ALU.mult, ALU.add))
                step(nc.vector.tensor_tensor(t, y, y, ALU.mult))
                step(nc.vector.tensor_tensor(t, t, v, ALU.mult))
                step(nc.vector.scalar_tensor_tensor(t, t, -10.0 / 3.0, t, ALU.add, ALU.mult))
                step(nc.vector.scalar_tensor_tensor(y, t, 5.0, y, ALU.add, ALU.mult))
                step(nc.vector.tensor_tensor(t, y, y, ALU.mult))
                step(nc.vector.scalar_tensor_tensor(t, t, -0.5 * 0.375 ** 3, v, ALU.mult, ALU.mult))
                step(nc.vector.scalar_tensor_tensor(y, t, 1.5 * 0.375, y, ALU.add, ALU.mult))

            def rsqrt_mean(y, sums, scale):
                v = nwv[:, 0:y.shape[1]]
                step(nc.vector.tensor_scalar(v, sums, scale, EPS, ALU.mult, ALU.add))
                rsqrt(y, v)

            def parts_lo(nk, row, dst=xT_lo, hi=xT_hi, same=None, src=acc):
                for k in range(nk):
                    if k % 2 == 0:
                        dve.wait_ge(xhi_ready, seen.next(xhi_ready))
                    g = gains[:, k, row:row + 1] if same is None else same
                    last = nc.vector.scalar_tensor_tensor(
                        dst[:, k, :], src[k // 2][:, (k % 2) * TOK:(k % 2 + 1) * TOK], g,
                        hi[:, k, :].bitcast(F32), ALU.mult, ALU.subtract)
                    if k % 2 or k == nk - 1:
                        last.then_inc(xlo_ready, 1)

            owed = []

            def settle():
                if owed:
                    split_lo(owed.pop() + RING)

            def row_scales():
                dve.wait_ge(ss_ready, seen.next(ss_ready, QUARTERS))
                halves = ss[:, 0:QUARTERS].rearrange("p (t h) -> p t h", h=2)
                v = nwv[:, 0:NT]
                step(nc.vector.scalar_tensor_tensor(v.rearrange("p (t o) -> p t o", o=1), halves[:, :, 0:1], EPS,
                                                    halves[:, :, 1:2], ALU.add, ALU.add))
                rsqrt(rstd[:, 0:NT], v)

            starting = [True]

            def norm(row):
                row_scales()
                if starting[0]:
                    dve.wait_ge(const_in, 16)
                for t in range(NT):
                    last = nc.vector.tensor_scalar(diag[:, t, :], ident, rstd[:, t:t + 1], None, ALU.mult)
                last.then_inc(diag_ready, 1)
                if starting[0]:
                    dve.wait_ge(setup_pe, seen.next(setup_pe))
                    nc.vector.tensor_copy(gains[:, :, 0:G_ROWS],
                                          up[3][:, 0:KD * G_ROWS].rearrange("p (k r) -> p k r", k=KD)).then_inc(setup_dve, 1)
                    dve.wait_ge(setup_dve, 1)
                    split_lo(0)
                parts_lo(KD, row)
                if starting[0]:
                    for n in range(1, RING):
                        split_lo(n)
                    starting[0] = False
                settle()

            def residual(scale):
                for t in range(NT):
                    for h in range(2):
                        cols = slice(512 * h, 512 * h + 512)
                        dve.wait_ge(acc_done, seen.next(acc_done))
                        nc.vector.scalar_tensor_tensor(x[:, t, cols], acc[2 * t + h][:], scale, x[:, t, cols],
                                                       ALU.mult, ALU.add).then_inc(x_ready, 1)
                dve.wait_ge(x_ready, seen.next(x_ready, QUARTERS))

            def product_parts(c):
                dve.wait_ge(hhi_ready, seen.next(hhi_ready))
                nc.vector.tensor_tensor(hT_lo[:, c % 2], prod[:].rearrange("p (k n) -> p k n", k=2),
                                        hT_hi[:, c % 2].bitcast(F32), ALU.subtract).then_inc(hlo_ready, 1)
                dve.wait_ge(hlo_ready, seen.next(hlo_ready))

            def ffn(s, n0, bank0):
                def chunk(n, c, down):
                    consumed(n)
                    consumed(n + 1)
                    dve.wait_ge(gate_ready, seen.next(gate_ready))
                    nc.vector.tensor_tensor(prod[:], gate[:], up[(bank0 + 2 * c + 1) % 4][:],
                                            ALU.mult).then_inc(prod_ready, 1)
                    dve.wait_ge(prod_ready, seen.next(prod_ready))
                    dve.sem_inc(bank_free, 2)
                    product_parts(c)
                    if down:
                        consumed(n + 2)

                chunk(n0, 0, False)
                chunk(n0 + 2, 1, True)
                with dve.Fori(0, 4) as i:
                    seen.enter(i, [(hi_ready, 6), (tile_used, 6), (gate_ready, 2), (prod_ready, 2), (hhi_ready, 2),
                                   (hlo_ready, 2)])
                    chunk(n0 + 5, 2, True)
                    chunk(n0 + 8, 3, True)
                    seen.leave(4)
                chunk(n0 + 29, 10, True)
                owed.append(n0 + 32)
                residual(0.5)

            def conv(s, n0, bank0):
                step(nc.vector.memset(zconv[:, :, 0:2], 0.0))
                for c in range(4):
                    n = n0 + 4 * c - (c > 0)
                    b = bank0 + 3 * c
                    consumed(n)
                    consumed(n + 1)
                    dve.wait_ge(gate_ready, seen.next(gate_ready))
                    step(nc.vector.tensor_tensor(zconv[:, :, 2:], gate[:].rearrange("p (k n) -> p k n", k=2),
                                                 up[(b + 1) % 4][:].rearrange("p (k n) -> p k n", k=2), ALU.mult))
                    dve.sem_inc(bank_free, 2)
                    for j in (2, 1, 0):
                        for m in range(2):
                            tap = gains[:, 2 * c + m, G_CONV + 3 * s[1] + j:G_CONV + 3 * s[1] + j + 1]
                            z = zconv[:, m, j:j + TOK]
                            if j == 2:
                                last = nc.vector.tensor_scalar(yconv[:, m, :], z, tap, None, ALU.mult)
                            else:
                                last = nc.vector.scalar_tensor_tensor(yconv[:, m, :], z, tap, yconv[:, m, :],
                                                                      ALU.mult, ALU.add)
                        step(last)
                    consumed(n + 2)
                    nc.vector.tensor_tensor(prod[:], yconv[:].rearrange("p k n -> p (k n)"), up[(b + 2) % 4][:],
                                            ALU.mult).then_inc(prod_ready, 1)
                    dve.wait_ge(prod_ready, seen.next(prod_ready))
                    dve.sem_inc(bank_free, 1)
                    product_parts(c)
                    if c:
                        consumed(n + 3)
                owed.append(n0 + 15)
                residual(1.0)

            def trig_arguments():
                posf, k = rsh[:, 0:NT], nwt[:, 0:32]
                dve.wait_ge(misc_in, seen.next(misc_in, 48))
                step(nc.vector.tensor_copy(posf, pos[:]))
                for t in range(NT):
                    last = nc.vector.tensor_scalar(sin[:, t, :], consts[:, C_FREQ:C_FREQ + 16], posf[:, t:t + 1], None,
                                                   ALU.mult)
                step(last)
                ang = sin[:].rearrange("p t f -> p (t f)")
                shifted = cos[:].rearrange("p t f -> p (t f)")
                big = 1.5 * 2.0 ** 23
                step(nc.vector.tensor_scalar(k, ang, 1.0 / (2 * np.pi), big, ALU.mult, ALU.add))
                step(nc.vector.tensor_scalar(k, k, big, None, ALU.subtract))
                for part in TWO_PI:
                    step(nc.vector.scalar_tensor_tensor(ang, k, -part, ang, ALU.mult, ALU.add))
                step(nc.vector.tensor_scalar(shifted, ang, np.pi / 2, None, ALU.add))
                step(nc.vector.tensor_scalar(k, shifted, np.pi, -2 * np.pi, ALU.is_gt, ALU.mult))
                step(nc.vector.tensor_tensor(shifted, shifted, k, ALU.add))
                step(nc.vector.tensor_scalar(shifted, shifted, PI_IN, -PI_IN, ALU.min, ALU.max))
                nc.vector.tensor_scalar(ang, ang, PI_IN, -PI_IN, ALU.min, ALU.max).then_inc(trig_arg, 1)

            def score_unit(u, scale, near, far, negsink=BIG):
                b = u % DEEP
                if u >= DEEP:
                    dve.wait_ge(turned, seen.next(turned))
                dve.wait_ge(scores_done, seen.next(scores_done))
                nc.vector.tensor_tensor_reduce(S[b][:, 0:256], acc[u % 2][:, 0:256], far, scale[1], negsink, ALU.add, ALU.min,
                                               nmax[b][:, 1:2])
                nc.vector.tensor_tensor_reduce(S[b][:, 256:384], acc[u % 2][:, 256:384], near, scale[0], negsink, ALU.add,
                                               ALU.min, nmax[b][:, 0:1]).then_inc(nmax_ready, 1)

            def row_sums(u, sink=False):
                b = u % DEEP
                dve.wait_ge(exp_ready, seen.next(exp_ready))
                if sink:
                    step(nc.vector.tensor_tensor(esum[b][:], esum[b][:], esink[b][:], ALU.add))
                nc.vector.reciprocal(rsum[b][:], esum[b][:]).then_inc(rsum_ready, 1)

            def rope(dst, src, w):
                def table(v):
                    if w is None:
                        return v
                    return v.rearrange("p t (o f) -> p t o f", o=1).broadcast_to([P, NT, w, 16])
                c, sn = table(cos[:]), table(sin[:])
                n = NT * (w or 1)
                tmp = [rtmp[:, i, 0:n, :] for i in range(4)]
                if w is not None:
                    tmp = [v.rearrange("p (t h) f -> p t h f", t=NT) for v in tmp]
                a1, a2 = src[..., 0:16], src[..., 16:32]
                nc.vector.tensor_tensor(tmp[0], a1, c, ALU.mult)
                nc.vector.tensor_tensor(tmp[1], a2, sn, ALU.mult)
                nc.vector.tensor_tensor(tmp[2], a2, c, ALU.mult)
                step(nc.vector.tensor_tensor(tmp[3], a1, sn, ALU.mult))
                nc.vector.tensor_tensor(dst[..., 0:16], tmp[0], tmp[1], ALU.subtract)
                step(nc.vector.tensor_tensor(dst[..., 16:32], tmp[2], tmp[3], ALU.add))

            def mla(s, n0, bank0):
                trig_arguments()
                consumed(n0)
                consumed(n0 + 1)
                for t in range(NT):
                    last = nc.vector.tensor_copy(latent[:, t, :], up[(bank0 + t) % 4][:, 0:QL + KVL + ROPE])
                step(last)
                dve.sem_inc(bank_free, NT)
                for t in range(NT):
                    nc.vector.tensor_tensor_reduce(cn[:, t, 0:QL], latent[:, t, 0:QL], latent[:, t, 0:QL], 1.0, 0.0,
                                                   ALU.mult, ALU.add, ssh[:, t:t + 1])
                    last = nc.vector.tensor_tensor_reduce(cn[:, t, QL:QL + KVL], latent[:, t, QL:QL + KVL],
                                                          latent[:, t, QL:QL + KVL], QL / KVL, 0.0,
                                                          ALU.mult, ALU.add, ssh[:, 2 + t:3 + t])
                step(last)
                rsqrt_mean(rsh[:, 0:4], ssh[:, 0:4], 1.0 / QL)
                for t in range(NT):
                    nc.vector.tensor_scalar(cn[:, t, 0:QL], latent[:, t, 0:QL], rsh[:, t:t + 1], None, ALU.mult)
                    nc.vector.tensor_scalar(cn[:, t, QL:], latent[:, t, QL:QL + KVL], rsh[:, 2 + t:3 + t], None,
                                            ALU.mult).then_inc(cn_ready, 1)
                parts_lo(3, G_MISC)
                pe_in = latent[:, :, QL + KVL:]
                nc.vector.tensor_tensor(rtmp[:, 0, 0:2, :].rearrange("p a b -> p (a b)"), pe_in[:, 0, :],
                                        pe_in[:, 0, :], ALU.mult)
                step(nc.vector.tensor_tensor(rtmp[:, 0, 2:4, :].rearrange("p a b -> p (a b)"), pe_in[:, 1, :],
                                             pe_in[:, 1, :], ALU.mult))
                step(nc.vector.tensor_reduce(ss[:, 4:6], rtmp[:, 0, 0:4, :].rearrange("p (t a) b -> p t (a b)", t=NT),
                                             AX.X, ALU.add))
                for t in range(NT):
                    last = nc.vector.tensor_tensor(kpe[:, t, :], pe_in[:, t, :], g96[:, 1, NOPE:], ALU.mult)
                step(last)
                dve.wait_ge(trig_done, seen.next(trig_done))
                rope(kpe, kpe, None)
                for i, (tile, groups) in enumerate(((n0 + 2, (0, 1)), (n0 + 3, (2,)))):
                    consumed(tile)
                    for g in groups:
                        for t in range(NT):
                            last = nc.vector.tensor_copy(arena[:, 1536 * t + 512 * g:1536 * t + 512 * g + 512],
                                                         up[(bank0 + 2 + 2 * g + t) % 4][:])
                    step(last)
                    dve.sem_inc(bank_free, NT * len(groups))
                dve.sem_inc(q_copied, 1)
                dve.wait_ge(kv_copied, seen.next(kv_copied, 2))
                dve.sem_inc(bank_free, 4)

                def flat(v):
                    return v.rearrange("p t h d -> p (t h) d")

                def over(v, n):
                    return v.rearrange("p (a o) -> p a o", o=1).broadcast_to([P, NT * MH, n])

                def gain(v, n):
                    return v.rearrange("p (o d) -> p o d", o=1).broadcast_to([P, NT * MH, n])

                step(nc.vector.tensor_tensor(g96[:, 0, 0:NOPE], g96[:, 0, 0:NOPE], g96[:, 1, 0:NOPE], ALU.mult))
                step(nc.vector.tensor_reduce(ssh[:, 0:32], flat(squares), AX.X, ALU.add))
                dve.wait_ge(kv_copied, seen.next(kv_copied, 2))
                dve.sem_inc(bank_free, 4)
                kn = KV[:, :, :, 0:NOPE]
                step(nc.vector.tensor_tensor(squares[:, :, :, 0:NOPE], kn, kn, ALU.mult))
                step(nc.vector.tensor_reduce(ssh[:, 32:64], flat(squares)[:, :, 0:NOPE], AX.X, ALU.add))
                for t in range(NT):
                    last = nc.vector.tensor_scalar(ssh[:, 32 + MH * t:48 + MH * t], ssh[:, 32 + MH * t:48 + MH * t],
                                                   ss[:, 4 + t:5 + t], None, ALU.add)
                step(last)
                rsqrt_mean(rsh[:], ssh[:], 1.0 / QKH)
                nc.vector.tensor_scalar(qscale[:], rsh[:, 0:32], -float(QKH) ** -0.5, None, ALU.mult)
                nc.vector.tensor_tensor(flat(KF)[:, :, 0:NOPE], flat(KV)[:, :, 0:NOPE], over(rsh[:, 32:64], NOPE), ALU.mult)
                for t in range(NT):
                    last = nc.vector.tensor_tensor(
                        KF[:, t, :, NOPE:], kpe[:, t, :].rearrange("p (o d) -> p o d", o=1).broadcast_to([P, MH, ROPE]),
                        rsh[:, 32 + MH * t:48 + MH * t].rearrange("p (h o) -> p h o", o=1).broadcast_to([P, MH, ROPE]),
                        ALU.mult)
                step(last)
                step(nc.vector.tensor_tensor(flat(Q), flat(Q), gain(g96[:, 0, :], QKH), ALU.mult))
                rope(Q[:, :, :, NOPE:], Q[:, :, :, NOPE:], MH)
                dve.sem_inc(qk_ready, 1)
                consumed(n0 + 4)
                far, near = consts[:, C_CAUSAL:C_CAUSAL + 256], consts[:, C_CAUSAL + 128:C_CAUSAL + 256]

                def o_lo(j):
                    dve.wait_ge(ohi_ready, seen.next(ohi_ready))
                    nc.vector.tensor_tensor(xT_lo[:, j, :], up[2 + j % 2][:, 0:TOK],
                                            xT_hi[:, j, :].bitcast(F32), ALU.subtract).then_inc(olo_ready, 1)
                    dve.wait_ge(olo_ready, seen.next(olo_ready))

                for i in range(MH + 7):
                    if i < MH:
                        dve.wait_ge(headT_done, seen.next(headT_done))
                        nc.vector.tensor_copy(headT[i % 2][0:QKH, :], up[i % 2][0:QKH, :]).then_inc(headT_ready, 1)
                    if 0 <= i - 1 < MH:
                        score_unit(i - 1, [qscale[:, MH * t + i - 1:MH * t + i] for t in range(NT)], near, far)
                    if 0 <= i - 2 < MH:
                        row_sums(i - 2)
                    if 0 <= i - 6 < MH and (i - 6) % 2:
                        o_lo((i - 6) // 2)
                dve.wait_ge(turned, seen.next(turned, DEEP))
                for j in range(3):
                    consumed(n0 + 5 + j)
                owed.append(n0 + 8)
                residual(1.0)

            def sg(s, n0, bank0):
                for h in range(2):
                    dve.wait_ge(ws_turned, seen.next(ws_turned))
                    last = nc.vector.tensor_tensor(
                        wsT[:, 4 * h:4 * h + 4, :], acc[h][:].rearrange("p (g t) -> p g t", g=4),
                        consts[:, C_LOWT:C_LOWT + P].rearrange("p (o t) -> p o t", o=1).broadcast_to([P, 4, P]),
                        ALU.mult)
                last.then_inc(ws_ready, 1)
                for g in range(2):
                    consumed(n0 + 2 * g)
                    consumed(n0 + 2 * g + 1)
                    dve.wait_ge(v_ready, seen.next(v_ready))
                    dve.sem_inc(bank_free, NT)
                    for t in range(NT):
                        last = nc.vector.tensor_tensor_reduce(prod[:], xn[:, t, 512 * g:512 * g + 512],
                                                              xn[:, t, 512 * g:512 * g + 512], 1.0, 0.0, ALU.mult,
                                                              ALU.add, ssh[:, 2 * g + t:2 * g + t + 1])
                        step(last)
                step(nc.vector.tensor_tensor(ssh[:, 0:2], ssh[:, 0:2], ssh[:, 2:4], ALU.add))
                rsqrt_mean(rsh[:, 0:2], ssh[:, 0:2], 1.0 / D)
                for t in range(NT):
                    last = nc.vector.tensor_scalar(xn[:, t, :], xn[:, t, :], rsh[:, t:t + 1], None, ALU.mult)
                last.then_inc(vn_ready, 1)
                for c in range(4):
                    n = n0 + 4 + 2 * c - (c > 0)
                    consumed(n)
                    dve.wait_ge(mix_done, seen.next(mix_done))
                    dve.wait_ge(gate_ready, seen.next(gate_ready))
                    ps = up[(bank0 + 5 + 2 * c) % 4]
                    for m in range(2):
                        g = 2 * c + m
                        for t in range(NT):
                            last = nc.vector.scalar_tensor_tensor(
                                mixed[:, m, t * P:(t + 1) * P], ps[:, m * TOK + t * P:m * TOK + (t + 1) * P],
                                gains[:, g, G_SGV:G_SGV + 1], sgb[:, g * P:(g + 1) * P], ALU.mult, ALU.add)
                    step(last)
                    dve.sem_inc(bank_free, 2)
                    nc.vector.tensor_tensor(prod[:], gate[:], mixed.rearrange("p m t -> p (m t)"),
                                            ALU.mult).then_inc(prod_ready, 1)
                    dve.wait_ge(prod_ready, seen.next(prod_ready))
                    product_parts(c)
                    if c:
                        consumed(n + 1)
                owed.append(n0 + 11)
                residual(1.0)

            def tables(part):
                settle()
                if part == 0:
                    nc.vector.memset(relb, NEG).then_inc(arena_free, 1)
                    return
                if part == 2:
                    flipped_tables()
                    return
                dve.wait_ge(tables_in, seen.next(tables_in, 16 * 8))
                for i in range(2):
                    for j in range(2):
                        last = nc.vector.tensor_tensor_reduce(nwt[:], lp[:, i, 2 * j, :], lp[:, i, 2 * j + 1, :], 1.0, 0.0,
                                                              ALU.mult, ALU.add, ssh[:, 2 * i + j:2 * i + j + 1])
                        step(last)
                    step(nc.vector.tensor_scalar(subln[:, i:i + 1], gains[:, 3 + i, G_MISC:G_MISC + 1],
                                                 1.0 - LAM_INIT[i], None, ALU.mult))
                nc.vector.tensor_scalar(negsinks[:], sinks[:], -1.0, None, ALU.mult).then_inc(tab_dve, 1)
                dve.wait_ge(tab_dve, seen.next(tab_dve))
                dve.wait_ge(tab_pe, seen.next(tab_pe))
                nc.vector.tensor_copy(rv[0:12, 0, :], acc[0][0:12, 0:384])
                nc.vector.tensor_copy(rv[0:8, 1, :], acc[1][0:8, 0:384]).then_inc(rv_ready, 1)
                nc.vector.tensor_copy(pos2[:].rearrange("p i v j -> p (i v j)"), acc[2][:, 0:64])
                step(nc.vector.tensor_scalar(TC, acc[3][:, 0:240].rearrange("p (n h) -> p h n", h=8), 1.0 / HSCALE, None,
                                             ALU.mult))
                dve.sem_inc(tab_dve, 1)
                dve.wait_ge(tab_dve, seen.next(tab_dve))
                dve.wait_ge(tab_act, seen.next(tab_act))
                for i in range(2):
                    step(nc.vector.tensor_tensor(neglam[:, i:i + 1], ssh[:, 5 + 2 * i:6 + 2 * i], ssh[:, 4 + 2 * i:5 + 2 * i],
                                                 ALU.subtract))
                    step(nc.vector.tensor_scalar(neglam[:, i:i + 1], neglam[:, i:i + 1], -LAM_INIT[i], None, ALU.add))

            def flipped_tables():
                for g in range(10):
                    dve.wait_ge(tab_pe, seen.next(tab_pe))
                    nc.vector.tensor_scalar(T[:, 2 * g:2 * g + 2, :].rearrange("p h j -> p (h j)"), acc[g % 4][:],
                                            1.0 / HSCALE, None, ALU.mult).then_inc(tab_dve, 1)
                    dve.wait_ge(tab_dve, seen.next(tab_dve))

            def mix(s, n0, bank0):
                n = n0
                bank = [bank0]

                def out(dst):
                    step(nc.vector.tensor_copy(dst, up[bank[0] % 4][:]))
                    bank[0] += 1
                    dve.sem_inc(bank_free, 1)

                def flat(v):
                    return v.rearrange("p k n -> p (k n)")

                consumed(n)
                out(flat(KC))
                dve.sem_inc(kc_ready, 1)
                for j, dst in enumerate((AQ, AQ, AK, AK)):
                    consumed(n + 1 + j)
                    out(flat(dst[:, 2 * (j % 2):2 * (j % 2) + 2, :]))
                consumed(n + 5)
                consumed(n + 6)
                for t in range(NT):
                    out(AV[:, t, :])
                dve.wait_ge(kc2_in, seen.next(kc2_in, 16 * 8))
                for v in range(2):
                    for j in range(16):
                        last = nc.vector.tensor_scalar(
                            blk[:, v, j, :].rearrange("p (g b) -> p g b", g=2),
                            KC2[:, v, :, 2 * j:2 * j + 16 * (NCMP - 1) + 1:16], pos2[:, s[1], v, j:j + 1], None, ALU.add)
                    last.then_inc(blk_ready, 1)
                    dve.wait_ge(blkhi_ready, seen.next(blkhi_ready))
                    nc.vector.tensor_tensor(blk_lo[:, v], blk[:, v], blk_hi[:, v].bitcast(F32),
                                            ALU.subtract).then_inc(blklo_ready, 1)
                places = [flat(BQ[:, 0:2, :]), flat(BQ[:, 2:4, :]), None, BS, None, BW, flat(CQ[:, 0:2, :]), None,
                          flat(CQ[:, 2:4, :]), None, CKV]
                for i, place in enumerate(places):
                    consumed(n0 + 7 + i)
                    if place is not None:
                        out(place)
                dve.wait_ge(hid_turned, seen.next(hid_turned))
                nc.vector.tensor_copy(hidT.rearrange("p v m n -> p (v m n)"), acc[1][:, 0:8 * NCMP]).then_inc(hidT_ready, 1)
                consumed(n0 + 18)
                dve.wait_ge(gates_ready, seen.next(gates_ready))
                bank[0] += 1
                dve.sem_inc(bank_free, 1)
                dve.wait_ge(cmp_done, seen.next(cmp_done))
                nc.vector.tensor_copy(kcT, up[bank[0] % 4][:, 0:2 * NCMP])
                step(nc.vector.tensor_copy(vc, up[(bank[0] + 1) % 4][0:NCMP, 0:128]))
                dve.sem_inc(bank_free, 2)
                dve.sem_inc(proj_ready, 1)

                late, late_since = [], [0]

                def merge(br, c, piece):
                    if piece % 2 == 0:
                        return
                    n = n0 + MIX_PROJ + 6 * br + 3 * c + piece // 2
                    dve.wait_ge(tile_used, seen.next(tile_used))
                    late.append(n)
                    if piece < 5:
                        return
                    dve.wait_ge(merge_gate, seen.next(merge_gate, 2))
                    for j, g in enumerate((gate, prod)):
                        dst = flat(merged[:, 4 * c + 2 * j:4 * c + 2 * j + 2, :])
                        ps = up[j + (2 if br == 2 else 0)][:]
                        if br == 0:
                            step(nc.vector.tensor_tensor(dst, g[:], ps, ALU.mult))
                        else:
                            step(nc.vector.tensor_tensor(g[:], g[:], ps, ALU.mult))
                            step(nc.vector.tensor_tensor(dst, dst, g[:], ALU.add))
                    dve.sem_inc(merge_step, 1)
                    if br == 2 and c == 0:
                        parts_of_merged(0)

                def parts_of_merged(c):
                    for j in range(2 * c, 2 * c + 2):
                        if j >= 2:
                            consumed(n0 + MIX_PROJ + 18 + j - 2)
                        dve.wait_ge(mhi_ready, seen.next(mhi_ready))
                        nc.vector.tensor_tensor(hT_lo[:, j % 2], merged[:, 2 * j:2 * j + 2, :],
                                                hT_hi[:, j % 2].bitcast(F32), ALU.subtract).then_inc(mlo_ready, 1)

                for i in range(STEPS):
                    if i < NU:
                        br, kind, h, _ = UNITS[i]
                        if kind == "cmp":
                            score_cmp(i, HSCALE, TC[:, h, :])
                        else:
                            tab = T[:, (0, 4, 12)[br] + h, :]
                            at = 8 * s[1] + h
                            score_unit(i, (-HSCALE, -HSCALE), tab[:, 128:256], tab, negsinks[:, at:at + 1] if br == 2 else BIG)
                    if 0 <= i - 1 < NU:
                        row_sums(i - 1, sink=UNITS[i - 1][0] == 2)
                    if 0 <= i - 5 < NU and UNITS[i - 5][3]:
                        br, _, h, _ = UNITS[i - 5]
                        if br == 0:
                            dve.wait_ge(oa_done, seen.next(oa_done))
                            for t in range(NT):
                                last = nc.vector.tensor_copy(YA[:, t, P * h:P * h + P],
                                                             up[2 * ((h + 1) % 2) + t][:, 0:P])
                            last.then_inc(ya_copied, 1)
                        else:
                            j = h // 2
                            hi, lo = (yB_hi, yB_lo) if br == 1 else (yT_hi, yT_lo)
                            dve.wait_ge(ohi_ready, seen.next(ohi_ready))
                            nc.vector.tensor_tensor(lo[:, j, :], up[2 + j % 2][:, 0:TOK], hi[:, j, :].bitcast(F32),
                                                    ALU.subtract).then_inc(olo_ready, 1)
                    if i == 13:
                        dve.wait_ge(ya_squares, seen.next(ya_squares, 4))
                        rsqrt_mean(rsh[:, 0:8], ssh[:, 0:8], 1.0 / P)
                        dve.sem_inc(ya_scale, 1)
                    if i == YA_STEP:
                        parts_lo(4, 0, yT_lo, yT_hi, subln[:, s[1]:s[1] + 1], up)
                    if late and i - late_since[0] >= 2:
                        split_lo(late.pop(0) + RING)
                    if i in PIECES:
                        merge(*PIECES[i])
                        if PIECES[i][2] % 2:
                            late_since[0] = i
                    if i >= NU:
                        while late:
                            split_lo(late.pop(0) + RING)
                dve.wait_ge(turned, seen.next(turned, DEEP))
                for c in range(2):
                    for piece in range(6):
                        merge(2, c, piece)
                        while late:
                            split_lo(late.pop(0) + RING)
                parts_of_merged(1)
                consumed(n0 + MIX_PROJ + 20)
                owed.append(n0 + MIX_PROJ + 21)
                residual(1.0)

            def score_cmp(u, scale, tab):
                b = u % DEEP
                if u >= DEEP:
                    dve.wait_ge(turned, seen.next(turned))
                dve.wait_ge(scores_done, seen.next(scores_done))
                for t in range(NT):
                    cols = slice(NCMP * t, NCMP * t + NCMP)
                    last = nc.vector.tensor_tensor_reduce(S[b][:, cols], acc[u % 2][:, cols], tab[:, cols], -scale, BIG,
                                                          ALU.add, ALU.min, nmax[b][:, t:t + 1])
                last.then_inc(nmax_ready, 1)

            def ple(s, n0, bank0):
                dve.wait_ge(xhi_ready, seen.next(xhi_ready))
                nc.vector.tensor_tensor(hT_lo[:, 0], acc[0][:].rearrange("p (k n) -> p k n", k=2),
                                        hT_hi[:, 0].bitcast(F32), ALU.subtract).then_inc(xlo_ready, 1)
                for c in range(2):
                    consumed(n0 + 3 * c)
                    consumed(n0 + 3 * c + 1)
                    dve.wait_ge(gate_ready, seen.next(gate_ready))
                    dve.sem_inc(bank_free, 2)
                    if c == 0:
                        consumed(n0 + 2)
                    for t, g in enumerate((gate, prod)):
                        if c:
                            dve.wait_ge(acc_done, seen.next(acc_done, QUARTERS // NT))
                        step(nc.vector.tensor_tensor(g[:], g[:], up[(bank0 + 4 * c + 2 + t) % 4][:], ALU.mult))
                        dve.sem_inc(bank_free, 1)
                        cols = slice(512 * c, 512 * c + 512)
                        nc.vector.tensor_tensor(x[:, t, cols], x[:, t, cols], g[:], ALU.add).then_inc(ple_added, 1)
                        dve.wait_ge(ple_added, seen.next(ple_added))
                        if c:
                            dve.sem_inc(x_ready, QUARTERS // NT)
                    if c == 0:
                        dve.sem_inc(ple_step, 1)
                owed.append(n0 + 5)
                dve.wait_ge(x_ready, seen.next(x_ready, QUARTERS))

            def final():
                row_scales()
                dve.wait_ge(fin_in, seen.next(fin_in, 16))
                for t in range(NT):
                    last = nc.vector.scalar_tensor_tensor(xn[:, t, :], x[:, t, :], rstd[:, t:t + 1], gfin, ALU.mult,
                                                          ALU.mult)
                last.then_inc(fin_ready, 1)

            nc.vector.memset(g_rows, 0.0).then_inc(rows_clear, 1)
            dve.wait_ge(x_in, 16)
            dve.sem_inc(x_ready, QUARTERS)
            dve.wait_ge(x_ready, seen.next(x_ready, QUARTERS))
            bank = 0
            for s, n0 in zip(plan, first):
                if s[0] == "norm":
                    norm(s[1])
                elif s[0] == "ffn":
                    ffn(s, n0, bank)
                    bank = (bank + 2 * NCH) % 4
                elif s[0] == "conv":
                    conv(s, n0, bank)
                    bank = (bank + 12) % 4
                elif s[0] == "mla":
                    mla(s, n0, bank)
                    bank = (bank + 16) % 4
                elif s[0] == "sg":
                    sg(s, n0, bank)
                    bank = (bank + 12) % 4
                elif s[0] == "tables":
                    tables(s[1])
                elif s[0] == "mix":
                    mix(s, n0, bank)
                    bank = (bank + MIX_BANKS) % 4
                elif s[0] == "ple":
                    ple(s, n0, bank)
                    bank = (bank + 8) % 4
                elif s[0] == "final":
                    final()

        @block.tensor
        def _(pe):
            seen = Seen()
            banks, credit, pairs_to_come = [0], [4], [0]
            residuals = [0]

            def matmul3(ps, lh, ll, rh, rl, start, stop):
                pe.matmul(ps, lh, rh, start=start, stop=False)
                pe.matmul(ps, lh, rl, start=False, stop=False)
                return pe.matmul(ps, ll, rh, start=False, stop=stop)

            def take_bank():
                if credit[0]:
                    credit[0] -= 1
                else:
                    pe.wait_ge(bank_free, seen.next(bank_free))
                banks[0] += 1
                return (banks[0] - 1) % 4

            def drain_banks():
                pe.wait_ge(bank_free, seen.next(bank_free, 4 - credit[0]))
                credit[0] = 4

            def up_matmuls(n, b):
                wh, wl = tview(w_hi[n % RING], KD, CW), tview(w_lo[n % RING], KD, CW)
                for m in range(2):
                    for k in range(KD):
                        if k % 2 == 0:
                            next_pair()
                        last = matmul3(up[b][:, m * TOK:(m + 1) * TOK], wh[:, k, m * P:(m + 1) * P],
                                       wl[:, k, m * P:(m + 1) * P], xT_hi[:, k, :], xT_lo[:, k, :],
                                       k == 0, k == KD - 1)
                last.then_inc(tile_used, 1)

            def down_matmuls(n, lh, ll, start, stop):
                wh, wl = tview(w_hi[n % RING], 2, D), tview(w_lo[n % RING], 2, D)
                for t in range(NT):
                    for h in range(2):
                        for k in range(2):
                            cols = slice(512 * h, 512 * h + 512)
                            last = matmul3(acc[2 * t + h][:], lh[:, k, t * P:(t + 1) * P], ll[:, k, t * P:(t + 1) * P],
                                           wh[:, k, cols], wl[:, k, cols], start and k == 0, stop and k == 1)
                        if stop:
                            last.then_inc(acc_done, 1)
                if not stop:
                    last.then_inc(tile_used, 1)

            def turn(src, nk, ready):
                for t in range(NT):
                    pe.wait_ge(ready, seen.next(ready))
                    for k in range(nk):
                        last = pe.transpose(acc[k // 2][:, (k % 2) * TOK + t * P:(k % 2) * TOK + (t + 1) * P],
                                            src[:, t, k * P:(k + 1) * P], ident)
                        if t == NT - 1 and (k % 2 or k == nk - 1):
                            last.then_inc(xT_ready, 1)

            def keep_clock(n):
                drain_banks()
                for _ in range(n):
                    pe.matmul(up[banks[0] % 4][:, 0:P], ident, ident, start=True, stop=True)

            def turn_norm():
                keep_clock(NORM_FILL)
                pe.wait_ge(diag_ready, seen.next(diag_ready))
                for k in range(KD):
                    for t in range(NT):
                        last = pe.matmul(acc[k // 2][:, (k % 2) * TOK + t * P:(k % 2) * TOK + (t + 1) * P],
                                         x[:, t, k * P:(k + 1) * P], diag[:, t, :], start=True, stop=True)
                    if k % 2:
                        last.then_inc(xT_ready, 1)
                pairs_to_come[0] = KD // 2

            def next_pair():
                if pairs_to_come[0]:
                    pe.wait_ge(xlo_ready, seen.next(xlo_ready))
                    pairs_to_come[0] -= 1

            def token_matmuls(n, nk, ncol, col, width, k0, ps, start, stop):
                wh, wl = tview(w_hi[n % RING], nk, ncol), tview(w_lo[n % RING], nk, ncol)
                for t in range(NT):
                    for k in range(nk):
                        if k % 2 == 0:
                            next_pair()
                        last = matmul3(ps[t], xT_hi[:, k0 + k, t * P:(t + 1) * P], xT_lo[:, k0 + k, t * P:(t + 1) * P],
                                       wh[:, k, col:col + width], wl[:, k, col:col + width],
                                       start and k == 0, stop and k == nk - 1)
                return last

            def ups(n):
                pe.wait_ge(lo_ready, seen.next(lo_ready))
                up_matmuls(n, take_bank())

            def down(n, c, start, stop):
                pe.wait_ge(lo_ready, seen.next(lo_ready))
                pe.wait_ge(hlo_ready, seen.next(hlo_ready))
                down_matmuls(n, hT_hi[:, c % 2], hT_lo[:, c % 2], start, stop)

            def conv(s, n0):
                n = n0
                for c in range(4):
                    for _ in range(3):
                        ups(n)
                        n += 1
                    if c:
                        down(n, c - 1, c == 1, False)
                        n += 1
                down(n, 3, False, True)

            def scores(u, q, k):
                if u >= 2:
                    pe.wait_ge(nmax_ready, seen.next(nmax_ready))
                ps = acc[u % 2]
                pe.matmul(ps[:, 0:256], q[:, P:TOK], k, start=True, stop=True)
                pe.matmul(ps[:, 256:384], q[:, 0:P], k[:, 0:P], start=True, stop=True).then_inc(scores_done, 1)

            def turn_unit(u):
                pe.wait_ge(p_ready, seen.next(p_ready))
                b, ps = u % DEEP, acc[2 + u % 2]
                pe.transpose(ps[:, 0:P], S[b][:, 256:384], ident)
                pe.transpose(ps[:, P:2 * P], S[b][:, 0:P], ident)
                pe.transpose(ps[:, 2 * P:3 * P], S[b][:, P:2 * P], ident).then_inc(turned, 1)

            def mla(s, n0):
                ps = [up[take_bank()][:, 0:QL + KVL + ROPE] for _ in range(NT)]
                for h in range(2):
                    pe.wait_ge(lo_ready, seen.next(lo_ready))
                    token_matmuls(n0 + h, 4, QL + KVL + ROPE, 0, QL + KVL + ROPE, 4 * h, ps, h == 0, h == 1
                                  ).then_inc(tile_used, 1)
                turn(cn, 3, cn_ready)
                pe.wait_ge(xlo_ready, seen.next(xlo_ready, 2))
                for tile, groups in ((n0 + 2, 2), (n0 + 3, 1)):
                    pe.wait_ge(lo_ready, seen.next(lo_ready))
                    for g in range(groups):
                        ps = [up[take_bank()][:] for _ in range(NT)]
                        last = token_matmuls(tile, 2, 512 * groups, 512 * g, 512, 0, ps, True, True)
                    last.then_inc(tile_used, 1)
                pe.wait_ge(lo_ready, seen.next(lo_ready))
                for g in range(4):
                    ps = [up[take_bank()][:] for _ in range(NT)]
                    last = token_matmuls(n0 + 4, 1, 2048, 512 * g, 512, 2, ps, True, True)
                    last.then_inc(group_done if g < 3 else tile_used, 1)
                pe.wait_ge(qk_ready, seen.next(qk_ready))
                drain_banks()
                def turn_head(h):
                    b = h % 2
                    for i, v in enumerate((Q, KF)):
                        for t in range(NT):
                            last = pe.transpose(up[b][0:QKH, i * TOK + t * P:i * TOK + (t + 1) * P], v[:, t, h, :], ident)
                    last.then_inc(headT_done, 1)

                def values(h):
                    if h % 2 == 0 and h >= 4:
                        pe.wait_ge(olo_ready, seen.next(olo_ready))
                    ps = up[2 + h // 2 % 2][64 * (h % 2):64 * (h % 2) + VH, 0:TOK]
                    pe.wait_ge(pt_ready, seen.next(pt_ready))
                    pe.matmul(ps, KV[:, 0, h, NOPE:], PT[h % 2][:, 0:256], start=True, stop=False)
                    last = pe.matmul(ps[:, P:TOK], KV[:, 1, h, NOPE:], PT[h % 2][:, 256:384], start=False, stop=True)
                    if h % 2:
                        last.then_inc(o_done, 1)

                for i in range(MH + 5):
                    if i < MH:
                        turn_head(i)
                    if 0 <= i - 1 < MH:
                        pe.wait_ge(headT_ready, seen.next(headT_ready))
                        scores(i - 1, headT[(i - 1) % 2][0:QKH, 0:TOK], headT[(i - 1) % 2][0:QKH, TOK:2 * TOK])
                    if 0 <= i - 4 < MH:
                        turn_unit(i - 4)
                    if 0 <= i - 5 < MH:
                        values(i - 5)
                pe.wait_ge(nmax_ready, seen.next(nmax_ready, 2))
                pe.wait_ge(olo_ready, seen.next(olo_ready, 2))
                for j in range(4):
                    pe.wait_ge(lo_ready, seen.next(lo_ready))
                    down_matmuls(n0 + 5 + j, xT_hi[:, 2 * j:2 * j + 2], xT_lo[:, 2 * j:2 * j + 2], j == 0, j == 3)

            def sg(s, n0):
                pe.wait_ge(ws_in, seen.next(ws_in, 32))
                for _ in range(KD // 2):
                    next_pair()
                for g in range(8):
                    last = pe.transpose(acc[g // 4][:, (g % 4) * P:(g % 4 + 1) * P], wsr[:, g, :], ident)
                    if g % 4 == 3:
                        last.then_inc(ws_turned, 1)
                for g in range(2):
                    ps = [up[take_bank()][:] for _ in range(NT)]
                    for h in range(2):
                        pe.wait_ge(lo_ready, seen.next(lo_ready))
                        token_matmuls(n0 + 2 * g + h, 4, 512, 0, 512, 4 * h, ps, h == 0, h == 1).then_inc(tile_used, 1)
                pe.wait_ge(ws_ready, seen.next(ws_ready))
                n = n0 + 4
                for c in range(4):
                    ups(n)
                    n += 1
                    if c == 0:
                        pe.wait_ge(vn_ready, seen.next(vn_ready))
                    b = take_bank()
                    for m in range(2):
                        g = 2 * c + m
                        for t in range(NT):
                            last = pe.matmul(up[b][:, m * TOK + t * P:m * TOK + (t + 1) * P],
                                             xn[:, t, g * P:(g + 1) * P], wsT[:, g, :], start=True, stop=True)
                    last.then_inc(mix_done, 1)
                    if c:
                        down(n, c - 1, c == 1, False)
                        n += 1
                down(n, 3, False, True)

            def ffn(s, n0):
                def gate_up(n, c, b, loop=False):
                    for j in range(2):
                        pe.wait_ge(lo_ready, seen.next(lo_ready))
                        if loop:
                            pe.wait_ge(bank_free, seen.next(bank_free))
                        else:
                            assert take_bank() == (b + j) % 4
                        up_matmuls(n + j, (b + j) % 4)

                b = banks[0] % 4
                gate_up(n0, 0, b)
                gate_up(n0 + 2, 1, b + 2)
                down(n0 + 4, 0, True, False)
                with pe.Fori(0, 4) as i:
                    seen.enter(i, [(lo_ready, 6), (bank_free, 4), (hlo_ready, 2)])
                    gate_up(n0 + 5, 2, b, True)
                    down(n0 + 7, 1, False, False)
                    gate_up(n0 + 8, 3, b + 2, True)
                    down(n0 + 10, 2, False, False)
                    seen.leave(4)
                banks[0] += 16
                gate_up(n0 + 29, 10, b)
                down(n0 + 31, 9, False, False)
                down(n0 + 32, 10, False, True)

            def tables(part):
                if part == 0:
                    return
                if part == 2:
                    flipped_tables()
                    return
                pe.wait_ge(tables_in, seen.next(tables_in, 16 * 8))
                pe.wait_ge(tab_dve, seen.next(tab_dve))
                pe.matmul(acc[0][0:12, 0:384], relb[:, 0:12], one_hots[:, 0:384], start=True, stop=True)
                pe.matmul(acc[1][0:8, 0:384], relb[:, 12:20], one_hots[:, 384:768], start=True,
                          stop=True)
                pe.transpose(acc[2][:, 0:64], prows, ident[0:64, 0:64])
                for t in range(NT):
                    for b in range(NCMP):
                        at = C_OHF - C_KEPT + 256 + P * t - 16 * b - 31
                        i = NCMP * t + b
                        last = pe.matmul(acc[3][:, 8 * i:8 * i + 8], one_hots[:, at:at + P], relb[:, 4:12], start=True,
                                         stop=True)
                last.then_inc(tab_pe, 1)
                pe.wait_ge(tab_dve, seen.next(tab_dve))

            def flipped_tables():
                pe.wait_ge(u_in, seen.next(u_in, 16))
                pe.wait_ge(x_ready, QUARTERS * (1 + residuals[0]))
                for g in range(10):
                    if g >= 4:
                        pe.wait_ge(tab_dve, seen.next(tab_dve))
                    pe.matmul(acc[g % 4][:], consts[:, C_FLIP:C_FLIP + P],
                              U[:, 2 * g:2 * g + 2, :].rearrange("p h j -> p (h j)"), start=True,
                              stop=True).then_inc(tab_pe, 1)
                pe.wait_ge(tab_dve, seen.next(tab_dve, 4))

            def mix(s, n0):
                n = n0
                for _ in range(5):
                    ups(n)
                    n += 1
                ps = [up[take_bank()][:] for _ in range(NT)]
                for h in range(2):
                    pe.wait_ge(lo_ready, seen.next(lo_ready))
                    token_matmuls(n, 4, 512, 0, 512, 4 * h, ps, h == 0, h == 1).then_inc(tile_used, 1)
                    n += 1

                def key_value(n):
                    pe.wait_ge(lo_ready, seen.next(lo_ready))
                    ps = up[take_bank()]
                    wh, wl = tview(w_hi[n % RING], KD, CW), tview(w_lo[n % RING], KD, CW)
                    for k in range(KD):
                        matmul3(ps[:, 0:TOK], wh[:, k, 0:P], wl[:, k, 0:P], xT_hi[:, k, :], xT_lo[:, k, :],
                                k == 0, k == KD - 1)
                    token_matmuls(n, KD, CW, P, P, 0, [ps[:, TOK:TOK + P], ps[:, TOK + P:2 * TOK]], True, True
                                  ).then_inc(tile_used, 1)

                def hidden(n, v, h):
                    if h == 0:
                        pe.wait_ge(blklo_ready, seen.next(blklo_ready))
                    pe.wait_ge(lo_ready, seen.next(lo_ready))
                    wh, wl = tview(w_hi[n % RING], KD, CW), tview(w_lo[n % RING], KD, CW)
                    for k in range(KD):
                        last = matmul3(acc[2 * v][0:2 * NCMP, 0:CW], blk_hi[:, v, 8 * h + k, :],
                                       blk_lo[:, v, 8 * h + k, :], wh[:, k, :], wl[:, k, :], h == 0 and k == 0,
                                       h == 1 and k == KD - 1)
                    last.then_inc(tile_used, 1)

                ups(n)
                ups(n + 1)
                hidden(n + 2, 0, 0)
                key_value(n + 3)
                hidden(n + 4, 0, 1)
                key_value(n + 5)
                ups(n + 6)
                hidden(n + 7, 1, 0)
                ups(n + 8)
                hidden(n + 9, 1, 1)
                key_value(n + 10)
                pe.wait_ge(hid_ready, seen.next(hid_ready, 2))
                for v in range(2):
                    for m in range(2):
                        at = (2 * v + m) * 2 * NCMP
                        last = pe.transpose(acc[1][:, at:at + 2 * NCMP], hid[:, v, P * m:P * m + P],
                                            ident[0:2 * NCMP, 0:2 * NCMP])
                last.then_inc(hid_turned, 1)
                pe.wait_ge(lo_ready, seen.next(lo_ready))
                ps = up[take_bank()]
                token_matmuls(n + 11, KD, 24, 0, 24, 0, [ps[:, 0:24], ps[:, 24:48]], True, True).then_inc(tile_used, 1)
                pe.wait_ge(hidT_ready, seen.next(hidT_ready))
                if s[1] == 0:
                    pe.wait_ge(w2_in, seen.next(w2_in, 64))
                kb, vb = up[take_bank()], up[take_bank()]
                for base in (0, 64):
                    for m in range(2):
                        pe.matmul(kb[base:base + 64, 0:2 * NCMP], w2[:, s[1], 0, m, :], hidT[:, 0, m, :], start=m == 0,
                                  stop=m == 1)
                for g in range(2):
                    for m in range(2):
                        last = pe.matmul(vb[0:NCMP, 64 * g:64 * g + 64], hidT[:, 1, m, NCMP * g:NCMP * g + NCMP],
                                         w2[:, s[1], 1, m, :], start=m == 0, stop=m == 1)
                last.then_inc(cmp_done, 1)
                pe.wait_ge(proj_ready, seen.next(proj_ready))

                def operands(br, kind, h):
                    g, r = h // 4, h % 4
                    rows = slice(64 * g, 64 * g + 64)
                    if br == 0:
                        rows = slice(64 * kind, 64 * kind + 64)
                        return AQ[rows, h, :], AK[rows, h, :]
                    if br == 2:
                        return CQ[rows, r, :], CKV[rows, 0:TOK]
                    q = BQ[rows, r, :]
                    if kind == "cmp":
                        return q, kcT[rows, NCMP * g:NCMP * g + NCMP]
                    return q, (BS if kind == "sel" else BW)[rows, 0:TOK]

                def values_a(u, c, h):
                    pe.wait_ge(pt_ready, seen.next(pt_ready))
                    if c == 0 and h >= 2:
                        pe.wait_ge(ya_copied, seen.next(ya_copied))
                    o = [up[2 * ((h + 1) % 2) + t][:, 0:P] for t in range(NT)]
                    cols = slice(P * h, P * h + P)
                    pe.matmul(o[0], PT[u % 2][:, 0:P], AV[:, 0, cols], start=c == 0, stop=c == 1)
                    pe.matmul(o[1], PT[u % 2][:, P:2 * P], AV[:, 0, cols], start=c == 0, stop=False)
                    last = pe.matmul(o[1], PT[u % 2][:, 2 * P:3 * P], AV[:, 1, cols], start=False, stop=c == 1)
                    if c == 1:
                        last.then_inc(oa_done, 1)

                def values_bc(u, br, kind, h, ends):
                    pe.wait_ge(pt_ready, seen.next(pt_ready))
                    if br == 1 and h == 0 and kind == "sel":
                        pe.wait_ge(ya_copied, seen.next(ya_copied))
                    starts = kind == "sel" or br == 2
                    stops = kind == "cmp" or br == 2
                    if starts and h % 2 == 0 and 4 * (br - 1) + h // 2 >= 2:
                        pe.wait_ge(olo_ready, seen.next(olo_ready))
                    g = h // 4
                    o = up[2 + h // 2 % 2][64 * (h % 2):64 * (h % 2) + 64, 0:TOK]
                    cols = slice(TOK + 64 * g, TOK + 64 * g + 64)
                    cols1 = slice(TOK + P + 64 * g, TOK + P + 64 * g + 64)
                    if kind == "cmp":
                        last = pe.matmul(o, vc[:, 64 * g:64 * g + 64], PT[u % 2][0:NCMP, 0:TOK], start=False, stop=True)
                    else:
                        kv = CKV if br == 2 else BS if kind == "sel" else BW
                        pe.matmul(o, kv[:, cols], PT[u % 2][:, 0:TOK], start=starts, stop=False)
                        last = pe.matmul(o[:, P:TOK], kv[:, cols1], PT[u % 2][:, TOK:384], start=False, stop=stops)
                    if ends:
                        last.then_inc(o_done, 1)

                olo_before = seen.n.get(olo_ready.name, 0)

                def merge(br, c, piece):
                    g, m = piece // 2, piece % 2
                    n = n0 + MIX_PROJ + 6 * br + 3 * c + g
                    if m == 0:
                        pe.wait_ge(lo_ready, seen.next(lo_ready))
                    if g < 2:
                        if piece == 0 and br == 2 and c == 1:
                            pe.wait_ge(merge_gate, seen.next(merge_gate, 2))
                        elif piece == 0 and (br or c):
                            pe.wait_ge(merge_step, seen.next(merge_step))
                        elif piece == 0:
                            pe.wait_ge(xlo_ready, seen.next(xlo_ready, 2))
                        wh, wl = tview(w_hi[n % RING], KD, CW), tview(w_lo[n % RING], KD, CW)
                        for k in range(KD):
                            last = matmul3(up[g][:, m * TOK:(m + 1) * TOK], wh[:, k, m * P:(m + 1) * P],
                                           wl[:, k, m * P:(m + 1) * P], xT_hi[:, k, :], xT_lo[:, k, :], k == 0,
                                           k == KD - 1)
                    else:
                        b = m + (2 if br == 2 else 0)
                        if br < 2:
                            pe.wait_ge(merge_gate, seen.next(merge_gate))
                        elif m == 0 and c == 1:
                            pe.wait_ge(merge_step, seen.next(merge_step))
                        if br and m == 0 and c == 0:
                            pe.wait_ge(olo_ready, olo_before + 4 * br)
                        wh, wl = tview(w_hi[n % RING], 4, 512), tview(w_lo[n % RING], 4, 512)
                        yh, yl = (yB_hi, yB_lo) if br == 1 else (yT_hi, yT_lo)
                        for f in range(2):
                            cols = slice(CW * m + P * f, CW * m + P * f + P)
                            for k in range(4):
                                last = matmul3(up[b][:, f * TOK:(f + 1) * TOK], wh[:, k, cols], wl[:, k, cols],
                                               yh[:, k, :], yl[:, k, :], k == 0, k == 3)
                    if m:
                        last.then_inc(tile_used, 1)

                drain_banks()
                for i in range(STEPS):
                    if i < NU:
                        br, kind, h, _ = UNITS[i]
                        q, k = operands(br, kind, h)
                        if kind == "cmp":
                            scores_cmp(i, q, k)
                        else:
                            scores(i, q, k)
                    if 0 <= i - 3 < NU:
                        if UNITS[i - 3][1] == "cmp":
                            turn_cmp(i - 3)
                        else:
                            turn_unit(i - 3)
                    if 0 <= i - 4 < NU:
                        br, kind, h, ends = UNITS[i - 4]
                        if br == 0:
                            values_a(i - 4, kind, h)
                        else:
                            values_bc(i - 4, br, kind, h, ends)
                    if i == YA_STEP:
                        pe.wait_ge(ya_copied, seen.next(ya_copied))
                        pe.wait_ge(ya_ready, seen.next(ya_ready))
                        for k in range(4):
                            for t in range(NT):
                                last = pe.transpose(up[k // 2][:, (k % 2) * TOK + t * P:(k % 2) * TOK + (t + 1) * P],
                                                    YA[:, t, k * P:(k + 1) * P], ident)
                            if k % 2:
                                last.then_inc(xT_ready, 1)
                    if i in PIECES:
                        merge(*PIECES[i])
                pe.wait_ge(nmax_ready, seen.next(nmax_ready, 2))
                for c in range(2):
                    for piece in range(6):
                        merge(2, c, piece)
                pe.wait_ge(olo_ready, seen.next(olo_ready, 2))
                for j in range(4):
                    pe.wait_ge(lo_ready, seen.next(lo_ready))
                    pe.wait_ge(mlo_ready, seen.next(mlo_ready))
                    down_matmuls(n0 + MIX_PROJ + 18 + j, hT_hi[:, j % 2], hT_lo[:, j % 2], j == 0, j == 3)
                pe.wait_ge(merge_gate, seen.next(merge_gate, 2))
                pe.wait_ge(merge_step, seen.next(merge_step))

            def scores_cmp(u, q, k):
                if u >= 2:
                    pe.wait_ge(nmax_ready, seen.next(nmax_ready))
                for t in range(NT):
                    last = pe.matmul(acc[u % 2][:, NCMP * t:NCMP * t + NCMP], q[:, P * t:P * t + P], k, start=True,
                                     stop=True)
                last.then_inc(scores_done, 1)

            def turn_cmp(u):
                pe.wait_ge(p_ready, seen.next(p_ready))
                for t in range(NT):
                    last = pe.transpose(acc[2 + u % 2][0:NCMP, P * t:P * t + P], S[u % DEEP][:, NCMP * t:NCMP * t + NCMP],
                                        ident)
                last.then_inc(turned, 1)

            def ple(s, n0):
                for _ in range(KD // 2):
                    next_pair()
                pe.wait_ge(ple_arrived, seen.next(ple_arrived, 16))
                for t in range(NT):
                    for k in range(2):
                        last = pe.transpose(acc[0][:, k * TOK + t * P:k * TOK + (t + 1) * P],
                                            ple_in[:, t, k * P:(k + 1) * P], ident)
                last.then_inc(xT_ready, 1)
                n = n0
                for c in range(2):
                    ps = [up[take_bank()][:] for _ in range(NT)]
                    for h in range(2):
                        pe.wait_ge(lo_ready, seen.next(lo_ready))
                        token_matmuls(n, 4, 512, 0, 512, 4 * h, ps, h == 0, h == 1).then_inc(tile_used, 1)
                        n += 1
                    ps = [up[take_bank()][:] for _ in range(NT)]
                    pe.wait_ge(lo_ready, seen.next(lo_ready))
                    if c == 0:
                        pe.wait_ge(xlo_ready, seen.next(xlo_ready))
                    wh, wl = tview(w_hi[n % RING], 2, 512), tview(w_lo[n % RING], 2, 512)
                    for t in range(NT):
                        for k in range(2):
                            tok = slice(t * P, (t + 1) * P)
                            last = matmul3(ps[t], hT_hi[:, 0, k, tok], hT_lo[:, 0, k, tok], wh[:, k, :], wl[:, k, :],
                                           k == 0, k == 1)
                        if c:
                            last.then_inc(acc_done, QUARTERS // NT)
                    if c == 0:
                        last.then_inc(tile_used, 1)
                    n += 1

            pe.wait_ge(const_in, seen.next(const_in, 16))
            pe.wait_ge(gain_in, seen.next(gain_in, 112))
            for k in range(KD):
                last = pe.transpose(up[3][:, k * G_ROWS:(k + 1) * G_ROWS], g_rows[:, k * P:(k + 1) * P],
                                    ident[0:G_ROWS, 0:G_ROWS])
            last.then_inc(setup_pe, 1)
            for s, n0 in zip(plan, first):
                if s[0] == "norm":
                    turn_norm()
                elif s[0] == "ffn":
                    ffn(s, n0)
                elif s[0] == "conv":
                    conv(s, n0)
                elif s[0] == "mla":
                    mla(s, n0)
                elif s[0] == "sg":
                    sg(s, n0)
                elif s[0] == "tables":
                    tables(s[1])
                elif s[0] == "mix":
                    mix(s, n0)
                elif s[0] == "ple":
                    ple(s, n0)
                residuals[0] += s[0] not in ("norm", "tables", "final")

        @block.gpsimd
        def _(pool):
            pool.dma_start(pos[:], A["positions"][0].rearrange("(t p) -> p t", p=P), allow_slow_non_contiguous=True).then_inc(misc_in, 16)
            pool.dma_start(g96[:, 0, :], A["mla_q_gain"].partition_broadcast(P)).then_inc(misc_in, 16)
            pool.dma_start(g96[:, 1, :], A["mla_k_gain"].partition_broadcast(P)).then_inc(misc_in, 16)
            seen = Seen()

            def probabilities(u, factors=(None, None)):
                b = u % DEEP
                pool.wait_ge(rsum_ready, seen.next(rsum_ready))
                for t, lo, hi in ((1, 0, 256), (0, 256, 384)):
                    last = pool.tensor_scalar(S[b][:, lo:hi], S[b][:, lo:hi], rsum[b][:, t:t + 1], factors[t], ALU.mult,
                                              ALU.mult if factors[t] is not None else ALU.bypass)
                last.then_inc(p_ready, 1)

            def probabilities_cmp(u, factors):
                b = u % DEEP
                pool.wait_ge(rsum_ready, seen.next(rsum_ready))
                for t in range(NT):
                    cols = slice(NCMP * t, NCMP * t + NCMP)
                    last = pool.tensor_scalar(S[b][:, cols], S[b][:, cols], rsum[b][:, t:t + 1], factors[t], ALU.mult,
                                              ALU.mult)
                last.then_inc(pool_step, 1)
                pool.wait_ge(pool_step, seen.next(pool_step))
                pool.tensor_tensor(S[b][:, 0:2 * NCMP], S[b][:, 0:2 * NCMP], consts[:, C_CMPOK:C_CMPOK + 2 * NCMP],
                                   ALU.mult).then_inc(p_ready, 1)

            def sg():
                if any(s[0] == "mla" for s in plan):
                    pool.wait_ge(x_ready, QUARTERS * (2 + [s[0] for s in plan if s[0] not in ("norm",)].index("mla")))
                pool.dma_start(sgb, A["sg_b"][0].rearrange("g t -> (g t)").partition_broadcast(P)).then_inc(ws_in, 16)
                pool.dma_start(wsr, A["sg_w_s"][0].rearrange("g t s -> t g s")).then_inc(ws_in, 16)

            def tables():
                for i in range(2):
                    for v in range(2):
                        pool.dma_start(w2[:, i, v], A["nsa_cmp_w2_2"][i, v].rearrange("(m p) d -> p m d", p=P)
                                       ).then_inc(w2_in, 16)
                pool.wait_ge(arena_free, 1)
                pool.dma_start(relb[0:32, :], A["rel_bias_2"]).then_inc(tables_in, 16)
                pool.dma_start(one_hots, A["consts"][0:33, C_KEPT:]).then_inc(tables_in, 16)
                pool.dma_start(lp.rearrange("p i a d -> p (i a d)"),
                               A["diff_lambda_2"].rearrange("i a d -> (i a d)").partition_broadcast(P)
                               ).then_inc(tables_in, 16)
                pool.dma_start(sinks[:], A["swa_sinks_2"].rearrange("i h -> (i h)").partition_broadcast(P)
                               ).then_inc(tables_in, 16)
                for i in range(2):
                    for v in range(2):
                        at = 32 * i + 16 * v
                        pool.dma_start(prows[at:at + 16, :],
                                       A["nsa_cmp_pos_2"][i, v].rearrange("(j q) d -> j (q d)", q=2)
                                       ).then_inc(tables_in, 16)
                pool.wait_ge(rv_ready, 1)
                pool.dma_start(scratch[0:12, :], rv[0:12, 0, :]).then_inc(rv_stored, 16)
                pool.dma_start(scratch[12:20, :], rv[0:8, 1, :]).then_inc(rv_stored, 16)
                pool.wait_ge(rv_stored, 32)
                askew = bass.AP(scratch.tensor, 0, [[1, P], [384, 20], [1, 256]])
                pool.dma_start(U, askew).then_inc(u_in, 16)

            def mix(s):
                pool.wait_ge(kc_ready, seen.next(kc_ready))
                for v in range(2):
                    for g in range(2):
                        src = KC[64 * g:64 * g + 64, v, :]
                        pool.dma_start(KC2[0:64, v, g, :], src).then_inc(kc2_in, 16)
                        pool.dma_start(KC2[64:128, v, g, 0:TOK - 1], src[:, 1:TOK]).then_inc(kc2_in, 16)
                pool.wait_ge(gates_ready, seen.next(gates_ready))
                for i, (br, kind, h, _) in enumerate(UNITS):
                    if br == 0:
                        probabilities(i, (neglam[:, s[1]:s[1] + 1],) * 2 if kind == 1 else (None, None))
                    elif br == 2:
                        probabilities(i)
                    else:
                        col = 3 * h + ("cmp", "sel", "win").index(kind)
                        factors = [gB[:, t, col:col + 1] for t in range(NT)]
                        if kind == "cmp":
                            probabilities_cmp(i, factors)
                        else:
                            probabilities(i, factors)
                    if i == 13:
                        pool.wait_ge(ya_scale, seen.next(ya_scale))
                        ya = YA.rearrange("p t (h e) -> p (t h) e", h=4)
                        pool.tensor_tensor(ya, ya, rsh[:, 0:8].rearrange("p (a o) -> p a o", o=1)
                                           .broadcast_to([P, 8, P]), ALU.mult).then_inc(ya_ready, 1)

            residuals = 0
            for s in plan:
                if s[0] == "mla":
                    for h in range(MH):
                        probabilities(h)
                elif s[0] == "sg":
                    sg()
                elif s[0] == "tables":
                    if s[1] == 0:
                        tables()
                elif s[0] == "mix":
                    mix(s)
                elif s[0] == "ple":
                    pool.wait_ge(x_ready, QUARTERS * residuals)
                    pool.dma_start(ple_in, A["p_2"][s[1], 0].rearrange("(t p) d -> p t d", p=P)
                                   ).then_inc(ple_arrived, 16)
                residuals += s[0] not in ("norm", "tables", "final")
            if plan[-1][0] == "final":
                pool.wait_ge(x_ready, QUARTERS * (residuals - 1))
                pool.dma_start(gfin, A["final_norm_2"].partition_broadcast(P)).then_inc(fin_in, 16)


_INS = ["x", "positions", "norm_g", "ffn_gate", "ffn_up", "ffn_down", "conv_w_in", "conv_k", "conv_w_out", "mla_w_a",
        "mla_q_norm", "mla_w_uq", "mla_kv_norm", "mla_w_ukv", "mla_q_gain", "mla_k_gain", "mla_w_o", "sg_w_in",
        "sg_v_norm", "sg_w_s", "sg_b", "sg_w_out", "p_2", "norm_g_2", "ffn1_wi_2", "ffn1_wo_2", "w_in_2",
        "diff_lambda_2", "diff_subln_2", "nsa_cmp_pos_2", "nsa_cmp_w1_2", "nsa_cmp_w2_2", "swa_sinks_2",
        "w_branch_2", "w_out_2", "ffn2_wi_2", "ffn2_wo_2", "w_ple_2", "w_ple_gate_2", "rel_bias_2", "final_norm_2"]


def shape_constants():
    c = np.zeros((P, C_END), np.float32)
    q = np.arange(P)[:, None]
    c[:, C_ID:C_ID + P] = np.eye(P)
    c[:, C_FLIP:C_FLIP + P] = np.eye(P)[::-1]
    c[:, C_CAUSAL:C_CAUSAL + 2 * P] = np.where(P + q - np.arange(2 * P)[None] >= 0, 0.0, NEG)
    c[:, C_LOWT:C_LOWT + P] = (q <= np.arange(P)[None])
    for t in range(2):
        c[:, C_CMPOK + 15 * t:C_CMPOK + 15 * t + 15] = (P * t + q - 16 * np.arange(15)[None] - 31 >= 0)
    f = np.arange(0, ROPE, 2, dtype=np.float32) / np.float32(ROPE)
    c[:, C_FREQ:C_FREQ + 16] = np.float32(1.0) / np.float32(10000.0) ** f

    def one_hot(dist, masked):
        n = np.maximum(dist, 0)
        nf = np.maximum(n, 1).astype(np.float32)
        large = 16 + (np.log(nf / np.float32(16)) / np.float32(np.log(8.0)) * np.float32(16)).astype(np.int32)
        b = np.where(n < 16, n, np.minimum(large, 31))
        o = np.zeros((33, dist.size), np.float32)
        o[np.where(masked, 32, b), np.arange(dist.size)] = 1.0
        return o

    d = 255 - np.arange(384)
    c[0:33, C_OHREV:C_OHREV + 384] = one_hot(d, d < 0)
    c[0:33, C_OHREV + 384:C_OHREV + 768] = one_hot(d, (d < 0) | (d >= 128))
    d = np.arange(512) - 256
    c[0:33, C_OHF:C_OHF + 512] = one_hot(d, d < 0)
    return c


def kernel(**inputs):
    import concourse.bacc as bacc
    from concourse.bass_utils import run_bass_kernel_spmd

    nc = bacc.Bacc("TRN2", target_bir_lowering=False, num_devices=1)
    arrays, A = {}, {}
    for name in _INS + ["consts"]:
        a = shape_constants() if name == "consts" else np.ascontiguousarray(inputs[name])
        arrays[f"in_{name}"] = a
        A[name] = nc.dram_tensor(f"in_{name}", a.shape, mybir.dt.from_np(a.dtype), kind="ExternalInput").ap()
    out = nc.dram_tensor("out_0", (1, TOK, D), F32, kind="ExternalOutput").ap()
    build(nc, A, out)
    r = run_bass_kernel_spmd(nc, [arrays], core_ids=[0])
    return r.results[0]["out_0"]
```
